# Optimizing a Trainium2 kernel written in Bass

```python
import jax, jax.numpy as jnp
from jax import lax
import numpy as np

D_MODEL = 1024
BATCH = 1
SEQ = 1024
DEPTH = 2

MIX_WIDTH = D_MODEL
A_WIDTH = MIX_WIDTH // 2
B_WIDTH = MIX_WIDTH - A_WIDTH
A_HEADS = 8
A_HEAD_DIM = A_WIDTH // A_HEADS
B_HEADS = 8
CHUNK = 128
CONV_WIDTH = 3
IN_COLS = 2 * A_WIDTH + 3 * B_WIDTH
POOL_WINDOWS = (2, 4, 8, 16)
POOL_GROUPS = len(POOL_WINDOWS)
POOL_GROUP_DIM = D_MODEL // POOL_GROUPS
N_GROUPS = 4
EXPERTS_PER_GROUP = 8
N_EXPERTS = N_GROUPS * EXPERTS_PER_GROUP
TOP_K = 2
D_EXPERT = D_MODEL // 2
DISPATCH_BLOCK = 128
EPS = 1e-6
N_EVEN = (DEPTH + 1) // 2
N_ODD = DEPTH // 2

kernel_name = "hybrid_sgu_conv_pool_hmoe_adaln"

def rmsnorm(x, g):
    xf = x.astype(jnp.float32)
    y = xf * lax.rsqrt(jnp.mean(xf * xf, axis=-1, keepdims=True) + EPS)
    return (y * g.astype(jnp.float32)).astype(x.dtype)

def chunk_sgu(u, v, g_v, w_s, b_s):
    bsz, s, _ = v.shape
    n_chunks = s // CHUNK
    vh = v.reshape(bsz, n_chunks, CHUNK, A_HEADS, A_HEAD_DIM)
    vh = rmsnorm(vh, g_v.reshape(A_HEADS, A_HEAD_DIM))
    causal = jnp.tril(jnp.ones((CHUNK, CHUNK), dtype=bool))
    w = jnp.where(causal[None], w_s, 0).astype(v.dtype)
    sv = jnp.einsum('hts,bnshd->bnthd', w, vh)
    sv = sv + b_s.T[None, None, :, :, None].astype(v.dtype)
    return u * sv.reshape(bsz, s, A_WIDTH)

def short_gated_conv(b_gate, c_gate, x_in, conv_w):
    z = c_gate * x_in
    s = z.shape[1]
    zp = jnp.pad(z, ((0, 0), (CONV_WIDTH - 1, 0), (0, 0)))
    conv = sum(conv_w[k] * zp[:, k:k + s] for k in range(CONV_WIDTH))
    return b_gate * conv

def pool_mixer(h, w_pool, pool_scale):
    s = h.shape[1]
    hf = h.astype(jnp.float32)
    csum = jnp.cumsum(hf, axis=1)
    t = jnp.arange(s)
    outs = []
    for g, win in enumerate(POOL_WINDOWS):
        sl = slice(g * POOL_GROUP_DIM, (g + 1) * POOL_GROUP_DIM)
        cg = csum[..., sl]
        lagged = jnp.pad(cg, ((0, 0), (win, 0), (0, 0)))[:, :s]
        count = jnp.minimum(t + 1, win).astype(jnp.float32)[None, :, None]
        pooled = (cg - lagged) / count - hf[..., sl]
        outs.append(pooled.astype(h.dtype) @ w_pool[g])
    return jnp.concatenate(outs, axis=-1) * pool_scale

def routed_experts(hf, expert_id, gate, w_gate, w_up, w_down):
    t_tok, d = hf.shape
    n_assign = t_tok * TOP_K
    flat_e = expert_id.reshape(n_assign)
    flat_g = gate.reshape(n_assign)
    flat_tok = jnp.repeat(jnp.arange(t_tok, dtype=jnp.int32), TOP_K)
    order = jnp.argsort(flat_e)
    sorted_e = flat_e[order]
    counts = jnp.bincount(flat_e, length=N_EXPERTS)
    starts = jnp.cumsum(counts) - counts
    padded = (counts + DISPATCH_BLOCK - 1) // DISPATCH_BLOCK * DISPATCH_BLOCK
    pad_ends = jnp.cumsum(padded)
    pad_starts = pad_ends - padded
    dest = pad_starts[sorted_e] + jnp.arange(n_assign) - starts[sorted_e]
    n_blocks = (n_assign + DISPATCH_BLOCK - 1) // DISPATCH_BLOCK + N_EXPERTS
    n_rows = n_blocks * DISPATCH_BLOCK
    buf_tok = jnp.full((n_rows,), t_tok, jnp.int32).at[dest].set(flat_tok[order])
    buf_gate = jnp.zeros((n_rows,), hf.dtype).at[dest].set(flat_g[order].astype(hf.dtype))
    blk_expert = jnp.minimum(
        jnp.searchsorted(pad_ends, jnp.arange(n_blocks) * DISPATCH_BLOCK, side='right'),
        N_EXPERTS - 1)
    x_pad = jnp.concatenate([hf, jnp.zeros((1, d), hf.dtype)], axis=0)
    xb = x_pad[buf_tok].reshape(n_blocks, DISPATCH_BLOCK, d)

    def run_block(args):
        xblk, e = args
        a = xblk @ w_gate[e]
        b = xblk @ w_up[e]
        return (jax.nn.silu(a) * b) @ w_down[e]

    yb = lax.map(run_block, (xb, blk_expert)).reshape(n_rows, d)
    out = jax.ops.segment_sum(yb * buf_gate[:, None], buf_tok, num_segments=t_tok + 1)
    return out[:t_tok]

def hier_moe(h, w_gr, b_gr, w_er, b_er, w_gate, w_up, w_down):
    bsz, s, d = h.shape
    t_tok = bsz * s
    hf = h.reshape(t_tok, d)
    rows = jnp.arange(t_tok)
    g_logits = (hf @ w_gr + b_gr).astype(jnp.float32)
    g_prob = jax.nn.softmax(g_logits, axis=-1)
    g_sel = jnp.argmax(g_logits, axis=-1).astype(jnp.int32)
    g_w = g_prob[rows, g_sel][:, None]
    e_logits = (hf @ w_er + b_er).astype(jnp.float32).reshape(t_tok, N_GROUPS, EXPERTS_PER_GROUP)
    e_logits = e_logits[rows, g_sel]
    top_v, top_i = lax.top_k(e_logits, TOP_K)
    gate = g_w * jax.nn.softmax(top_v, axis=-1)
    expert_id = g_sel[:, None] * EXPERTS_PER_GROUP + top_i.astype(jnp.int32)
    y = routed_experts(hf, expert_id, gate, w_gate, w_up, w_down)
    return y.reshape(bsz, s, d)

def setup_inputs(seed: int = 0) -> dict:
    key = jax.random.key(seed)
    ks = jax.random.split(key, 24)
    D = D_MODEL

    def nrm(k, shape, scale):
        return jax.random.normal(k, shape, jnp.float32) * scale

    gate_offset = jnp.concatenate([jnp.zeros((2 * D,), jnp.float32), jnp.ones((D,), jnp.float32),
                                   jnp.zeros((2 * D,), jnp.float32), jnp.ones((D,), jnp.float32)])
    return {
        "x": nrm(ks[0], (BATCH, SEQ, D), 1.0),
        "c": nrm(ks[1], (BATCH, D), 1.0),
        "w_ada": nrm(ks[2], (DEPTH, D, 6 * D), 0.25 * D ** -0.5),
        "b_ada": nrm(ks[3], (DEPTH, 6 * D), 0.02) + gate_offset,
        "norm_mix_g": 1.0 + nrm(ks[4], (DEPTH, D), 0.02),
        "norm_ffn_g": 1.0 + nrm(ks[5], (DEPTH, D), 0.02),
        "w_in_even": nrm(ks[6], (N_EVEN, D, IN_COLS), D ** -0.5),
        "sgu_norm_g": 1.0 + nrm(ks[7], (N_EVEN, A_WIDTH), 0.02),
        "w_spatial": nrm(ks[8], (N_EVEN, A_HEADS, CHUNK, CHUNK), CHUNK ** -0.5),
        "b_spatial": 1.0 + nrm(ks[9], (N_EVEN, A_HEADS, CHUNK), 0.02),
        "conv_w": nrm(ks[10], (N_EVEN, CONV_WIDTH, B_WIDTH), CONV_WIDTH ** -0.5),
        "w_out_even": nrm(ks[11], (N_EVEN, MIX_WIDTH, D), MIX_WIDTH ** -0.5),
        "w_pool": nrm(ks[12], (N_ODD, POOL_GROUPS, POOL_GROUP_DIM, POOL_GROUP_DIM), POOL_GROUP_DIM ** -0.5),
        "pool_scale": 1.0 + nrm(ks[13], (N_ODD, D), 0.02),
        "w_group_router": nrm(ks[14], (DEPTH, D, N_GROUPS), D ** -0.5),
        "b_group_router": nrm(ks[15], (DEPTH, N_GROUPS), 0.01),
        "w_expert_router": nrm(ks[16], (DEPTH, D, N_EXPERTS), D ** -0.5),
        "b_expert_router": nrm(ks[17], (DEPTH, N_EXPERTS), 0.01),
        "moe_w_gate": nrm(ks[18], (DEPTH, N_EXPERTS, D, D_EXPERT), D ** -0.5),
        "moe_w_up": nrm(ks[19], (DEPTH, N_EXPERTS, D, D_EXPERT), D ** -0.5),
        "moe_w_down": nrm(ks[20], (DEPTH, N_EXPERTS, D_EXPERT, D), D_EXPERT ** -0.5),
        "final_norm_g": 1.0 + nrm(ks[21], (D,), 0.02),
    }

def reference(x, c, w_ada, b_ada, norm_mix_g, norm_ffn_g, w_in_even, sgu_norm_g,
              w_spatial, b_spatial, conv_w, w_out_even, w_pool, pool_scale,
              w_group_router, b_group_router, w_expert_router, b_expert_router,
              moe_w_gate, moe_w_up, moe_w_down, final_norm_g):
    c_act = jax.nn.silu(c)
    split_pts = [A_WIDTH, 2 * A_WIDTH, 2 * A_WIDTH + B_WIDTH, 2 * A_WIDTH + 2 * B_WIDTH]
    for l in range(DEPTH):
        mod = c_act @ w_ada[l] + b_ada[l]
        sh_m, sc_m, g_m, sh_f, sc_f, g_f = [m[:, None, :] for m in jnp.split(mod, 6, axis=-1)]
        h = rmsnorm(x, norm_mix_g[l]) * (1 + sc_m) + sh_m
        i = l // 2
        if l % 2 == 0:
            z = h @ w_in_even[i]
            u, v, b_gate, c_gate, x_in = jnp.split(z, split_pts, axis=-1)
            y_a = chunk_sgu(u, v, sgu_norm_g[i], w_spatial[i], b_spatial[i])
            y_b = short_gated_conv(b_gate, c_gate, x_in, conv_w[i])
            y = jnp.concatenate([y_a, y_b], axis=-1) @ w_out_even[i]
        else:
            y = pool_mixer(h, w_pool[i], pool_scale[i])
        x = x + g_m * y
        h = rmsnorm(x, norm_ffn_g[l]) * (1 + sc_f) + sh_f
        y = hier_moe(h, w_group_router[l], b_group_router[l], w_expert_router[l],
                     b_expert_router[l], moe_w_gate[l], moe_w_up[l], moe_w_down[l])
        x = x + g_f * y
    return rmsnorm(x, final_norm_g)


_drawn_inputs = setup_inputs


def setup_inputs(seed=0):
    import zlib

    import numpy as np

    out = dict(_drawn_inputs(seed))
    spreads = {}
    factors = {'sgu_norm_g': 8.575,
     'pool_scale': 10.155,
     'b_group_router': 26.301,
     'b_expert_router': 11.318,
     'final_norm_g': 7.581,
     'norm_ffn_g': 3.132,
     'b_spatial': 4.304}
    for name, (base, spread) in spreads.items():
        noise = np.random.default_rng([zlib.crc32(name.encode()), seed]).standard_normal(out[name].shape)
        drawn = base * np.exp(spread * noise) if base else spread * noise
        out[name] = __import__('jax').numpy.asarray(drawn.astype(out[name].dtype))
    for name, factor in factors.items():
        out[name] = (out[name] * factor).astype(out[name].dtype)
    return out
```

```python
import concourse.bass as bass
from concourse import mybir
from contextlib import ExitStack


class Chain:

    def __init__(self, engine, sem):
        self.engine, self.sem, self.count, self.index = engine, sem, 0, None

    def value(self):
        return self.count if self.index is None else self.index * self.per + self.count

    def link(self, ins):
        self.count += 1
        ins.then_inc(self.sem, 1)
        self.engine.wait_ge(self.sem, self.value())

    def enter(self, index, per):
        self.index, self.per, self.start = index, per, self.count

    def leave(self, trips):
        assert self.count - self.start == self.per, (self.count - self.start, self.per)
        self.count, self.index = self.start + trips * self.per, None


def hybrid_trunk(nc, x, c, w_ada, b_ada, norm_mix_g, norm_ffn_g, w_in_even, sgu_norm_g, w_spatial,
                 b_spatial, conv_w, w_out_even, w_pool, pool_scale, w_group_router, b_group_router,
                 w_expert_router, b_expert_router, moe_w_gate, moe_w_up, moe_w_down, final_norm_g, out):
    F32, I32, U32 = mybir.dt.float32, mybir.dt.int32, mybir.dt.uint32
    ALU, ACT, AX = mybir.AluOpType, mybir.ActivationFunctionType, mybir.AxisListType
    ds = bass.ds

    P = 128
    S, D = x.shape[1], x.shape[2]
    NT, KD = S // P, D // P
    LAYERS = w_ada.shape[0]
    A = D // 2
    KA = A // P
    HEADS = w_spatial.shape[1]
    HD = A // HEADS
    NG, NE = w_group_router.shape[2], w_expert_router.shape[2]
    EG = NE // NG
    FE = moe_w_gate.shape[3]
    KF = FE // P
    NR = NG + NE
    PG = w_pool.shape[1]
    PD = D // PG
    WINDOWS = (2, 4, 8, 16)
    REACH = max(WINDOWS)
    EPS = 1e-6
    ASSIGN = 2 * S
    XB = ASSIGN // P - 1
    NBLK = NE + XB + 1
    PAD = 4096
    TOKEN_MASK = PAD | (S - 1)
    CH = 512
    HALF = D // 2
    assert NT == KD == 8 and LAYERS == 2 and P == w_spatial.shape[2] and CH == FE == A
    NMOD = 6
    SH_M, SC_M, G_M, SH_F, SC_F, G_F = range(NMOD)
    HEAD, TAIL = 3, 3
    PAIRS = (NE - HEAD - TAIL) // 2
    PAIR = (HEAD, HEAD + 1)

    xv = x[0].rearrange("(t p) d -> p t d", p=P)
    outv = out[0].rearrange("(t p) d -> p t d", p=P)

    tables = [nc.dram_tensor(f"slot_table{l}", [P * NBLK, 2], U32, kind="Internal").ap() for l in range(LAYERS)]
    xn_dram = [nc.dram_tensor(f"normed_rows{l}", [S, D], F32, kind="Internal").ap() for l in range(LAYERS)]
    y_dram = [nc.dram_tensor(f"expert_rows{l}", [ASSIGN, D], F32, kind="Internal").ap() for l in range(LAYERS)]
    mod1_dram = nc.dram_tensor("mod_rows1", [NMOD, D], F32, kind="Internal").ap()

    ctx = ExitStack()
    with ctx:
        KB = 1024
        base = (nc.sbuf_base + 31) // 32 * 32
        X0 = base
        W0 = X0 + 32 * KB
        Z0 = W0 + 96 * KB
        H0 = Z0 + 16 * KB
        G0 = H0 + 32 * KB
        T0 = G0 + 8 * KB
        C0 = T0 + 16 * KB + 256
        END = nc.sbuf_top
        cursor = [C0]

        def at(name, shape, off, dt=F32):
            return nc.alloc_sbuf_tensor_at(name, shape, dt, offset=off)

        def small(name, shape, dt=F32):
            n = 4
            for s in shape[1:]:
                n *= s
            off = cursor[0]
            cursor[0] = (off + n + 31) // 32 * 32
            assert cursor[0] <= END, (name, cursor[0], END)
            return at(name, shape, off, dt)

        xr = at("x_rows", [P, NT, D], X0)
        SLOT = 16 * KB
        SA, SB_, SC, SD, SE, SF = [W0 + i * SLOT for i in range(6)]
        gate_w = [at(f"gate_w{s}", [P, KD, FE], o) for s, o in enumerate((SD, SA))]
        up_w = [at(f"up_w{s}", [P, KD, FE], o) for s, o in enumerate((SE, SB_))]
        down_w = [at(f"down_w{s}", [P, KF, D], o) for s, o in enumerate((SF, SC))]
        acc0 = at("cond_acc0", [P, NMOD * D], SF)
        cond0 = [at(f"cond0_w{q}", [P, 2, D], SD + q * 8 * KB) for q in range(4)]
        acc1 = at("cond_acc1", [P, NMOD * D], X0)
        cond1 = [at(f"cond1_w{q}", [P, D], X0 + (24 + 4 * q) * KB) for q in range(2)]
        hT = at("h_columns", [P, KD, S], H0)
        in_w = {n: at(f"in_w_{n}", [P, KD, A], o) for n, o in zip("cbuxv", (SA, SB_, SC, SD, SE))}
        zT = at("conv_in", [P, KA, S], Z0)
        ybT = at("mix_b", [P, KA, S], SF)
        yaT = at("mix_a", [P, KA, S], SA)
        out_w = at("out_w", [P, KD, D], SB_)
        ws_raw = at("spatial_w", [P, HEADS, P], SD)
        wsT = at("spatial_wT", [P, HEADS, P], SD + 4 * KB)
        bsp = at("spatial_bias", [P, KA, P], SD + 8 * KB)
        gv = at("sgu_gain", [P, A], SD + 10 * KB)
        conv_t = at("conv_out", [P, S], T0)
        v_sq = at("v_squares", [P, A], T0 + 4 * KB)
        v_n = [at(f"v_normed{s}", [P, A], T0 + (6 + 2 * s) * KB) for s in range(2)]
        gated = at("gate_tmp", [P, KA * P], T0 + 10 * KB)
        res_t = at("residual_tmp", [P, D], T0 + 12 * KB)
        a1b = at("scale_row1", [P, D], H0)
        b1b = at("shift_row1", [P, D], H0 + 4 * KB)
        YB = 4
        y_in = [at(f"y_in{s}", [P, 2, D], o) for s, o in enumerate((H0 + 8 * KB, H0 + 16 * KB, SC, SC + 8 * KB))]
        h_r = [at(f"h_rows{s}", [P, D], H0 + (24 + 4 * s) * KB) for s in range(2)]
        pool_w = at("pool_w", [P, PG, 2, PD], T0)
        pooledT = at("pooled_columns", [P, KD, P], T0 + 8 * KB)
        band = at("band", [P, PG, P], T0 + 12 * KB)
        band0 = at("band_first", [P, PG, P], T0 + 14 * KB)
        band_prev = at("band_previous", [P, PG, REACH], T0 + 16 * KB)
        xn = [at(f"xn{s}", [P, D], Z0 + 4 * KB * s) for s in range(2)]
        hTt = [at(f"h_tile_columns{s}", [P, KD, P], Z0 + (8 + 4 * s) * KB) for s in range(2)]
        xg = [at(f"gathered{s}", [P, D], H0 + 4 * KB * s) for s in range(2)]
        xT = [at(f"block_columns{s}", [P, KD, P], H0 + (8 + 4 * s) * KB) for s in range(2)]
        y_o = [at(f"y_out{s}", [P, D], H0 + (16 + 4 * s) * KB) for s in range(2)]
        aT = [at(f"act_columns{s}", [P, KF, P], H0 + (24 + 2 * s) * KB) for s in range(2)]
        act_r = at("act_rows", [P, FE], H0 + 28 * KB)
        sig = at("sigmoid_tmp", [P, FE], H0 + 30 * KB)
        grow = [at(f"gain_row{s}", [P, D], G0 + 4 * KB * s) for s in range(2)]

        rcur = [Z0]

        def routing(name, shape, dt=F32):
            n = 4
            for s in shape[1:]:
                n *= s
            off = rcur[0]
            rcur[0] = (off + n + 31) // 32 * 32
            assert rcur[0] <= H0, name
            return at(name, shape, off, dt)

        g_diff = routing("g_diff", [P, NT, NG])
        g_exp = routing("g_exp", [P, NT, NG])
        g_key = routing("g_key", [P, NT, NG])
        g_hot = routing("g_hot", [P, NT, NG])
        g_w = routing("g_weight", [P, NT])
        e_prod = routing("e_prod", [P, NT, NG, EG])
        e_sel = routing("e_sel", [P, NT, EG])
        e_diff = routing("e_diff", [P, NT, EG])
        e_key = routing("e_key", [P, NT, EG])
        e_hot = [routing(f"e_hot{i}", [P, NT, EG]) for i in range(2)]
        r_m = [routing(f"r_max{i}", [P, NT]) for i in range(4)]
        r_e = routing("r_exp", [P, NT])
        r_r = routing("r_recip", [P, NT])
        hot = [routing(f"hot{i}", [P, NT, NE]) for i in range(2)]
        hots = routing("hots", [P, NT, NE])
        before = routing("tiles_before", [P, NT + 1, NE])
        pos_i = routing("pos_int", [P, NT, NE], I32)
        quo_i = routing("quo_int", [P, NT, NE], I32)
        quo = routing("quo", [P, NT, NE])
        slot = routing("slot", [P, NT, NE])
        s_tmp = routing("slot_tmp", [P, NT, NE])
        cnt_i = routing("cnt_int", [P, NE], I32)
        nblk = routing("more_blocks", [P, NE])
        bend = routing("blocks_end", [P, NE])
        b_off = routing("block_offset", [P, NE])
        slot_f = routing("slot_float", [P, NT, 2])

        ident = small("ident", [P, P])
        ones = small("ones", [P, P])
        lower = small("strictly_before", [P, P])
        vec_rows = at("vector_rows", [P, P], T0)
        vec = small("vector_columns", [P, 64])
        c_e = small("c_exp", [P, KD])
        c_act = small("c_act", [P, KD])
        mod = [small(f"mod_columns{l}", [P, NMOD, KD]) for l in range(LAYERS)]
        a_m = small("a_mix", [P, KD])
        a_f = [small(f"a_ffn{l}", [P, KD]) for l in range(LAYERS)]
        r_w = [small(f"router_w{l}", [P, KD, NR]) for l in range(LAYERS)]
        r_b = [small(f"router_b{l}", [P, NR]) for l in range(LAYERS)]
        logits = routing("logits", [P, NT, NR])
        rank_g = small("rank_g", [P, NG])
        rank_e = small("rank_e", [P, EG])
        e_id = small("expert_ids", [P, NE])
        j_id = small("block_ids", [P, XB + 1])
        eps = small("eps", [P, 1])
        X_IN, N_FFN0, N_MIX1, N_FFN1, N_FINAL = range(5)
        ss = small("sum_squares", [P, 5, NT])
        sd = small("root_mean_square", [P, 5, NT])
        rstd = small("rstd", [P, 5, NT])
        vss = small("v_sum_squares", [P, HEADS])
        vsd = small("v_root_mean_square", [P, HEADS])
        vrs = small("v_rstd", [P, HEADS])
        slot_u = small("slot_index", [P, NT, 2], U32)
        entry = small("table_entry", [P, NT, 2, 2], U32)
        table = small("table", [P, NBLK, 2], U32)
        tok = small("token", [P, NBLK], U32)
        idx_g = [small(f"gather_index{s}", [P, 1], U32) for s in range(2)]
        idx_s = [small(f"scatter_index{s}", [P, 1], U32) for s in range(2)]
        gate_c = [small(f"block_gate{s}", [P, 1]) for s in range(2)]
        cmp_t = routing("block_compare", [1, XB + 1, NE])
        eid_f = routing("extra_expert_f", [1, XB + 2])
        extra = [small(f"extra_experts{l}", [1, XB + 2], I32) for l in range(LAYERS)]
        inv_count = small("inverse_counts", [P, REACH])
        vg_mix = [vec[:, l * KD:(l + 1) * KD] for l in range(LAYERS)]
        vg_ffn = [vec[:, (2 + l) * KD:(3 + l) * KD] for l in range(LAYERS)]
        vc = vec[:, 4 * KD:5 * KD]
        NVEC = 5 * KD + 3 * KA

        def conv_col(k, m):
            return vec[:, 5 * KD + k * KA + m:5 * KD + k * KA + m + 1]

        ps = ctx.enter_context(nc.psum_tensor("ps", [P, 8 * CH], F32))
        BANK = [ps[:, i * CH:(i + 1) * CH] for i in range(8)]
        PA = [ps[:, 0:D], ps[:, D:2 * D]]
        PT = ps[:, 4 * CH:6 * CH]
        PM = BANK[6]
        PL = BANK[7]

        def sem(name):
            return ctx.enter_context(nc.semaphore(name))

        vec_loaded, const_loaded = sem("vec_loaded"), sem("const_loaded")
        x_loaded = [sem(f"x_loaded{i}") for i in range(4)]
        bada_loaded = [sem(f"bada_loaded{l}") for l in range(LAYERS)]
        cond0_loaded = [sem(f"cond0_loaded{q}") for q in range(4)]
        cond1_loaded = [sem(f"cond1_loaded{q}") for q in range(2)]
        in_loaded = {n: sem(f"in_loaded_{n}") for n in "cbuxv"}
        sgu_loaded, out_w_loaded, x_reloaded = sem("sgu_loaded"), sem("out_w_loaded"), sem("x_reloaded")
        pool_loaded, rows1_loaded = sem("pool_loaded"), sem("rows1_loaded")
        final_loaded = sem("final_loaded")
        gate_loaded = [sem(f"gate_loaded{s}") for s in range(2)]
        up_loaded = [sem(f"up_loaded{s}") for s in range(2)]
        down_loaded = [sem(f"down_loaded{s}") for s in range(2)]
        consts = sem("consts")
        table_init = sem("table_init")
        bands_ready = sem("bands_ready")
        dve_chain, act_chain, pool_chain = sem("dve_chain"), sem("act_chain"), sem("pool_chain")
        vec_T, vec_ready, c_exp_ready = sem("vec_T"), sem("vec_ready"), sem("c_exp_ready")
        acc_init = sem("acc_init")
        cond0_used, cond1_used = sem("cond0_used"), sem("cond1_used")
        acc_ready = [sem(f"acc_ready{l}") for l in range(LAYERS)]
        mod_cols = [sem(f"mod_cols{l}") for l in range(LAYERS)]
        mod_ready = [sem(f"mod_ready{l}") for l in range(LAYERS)]
        gain_sum0, gain_ready0 = sem("gain_sum0"), sem("gain_ready0")
        row_sum1, row_kept1, row_stored1 = sem("row_sum1"), sem("row_kept1"), sem("row_stored1")
        x_ss, x_rstd, x_normed = sem("x_ss"), sem("x_rstd"), sem("x_normed")
        x_T, x_T_kept, h_act, h_dve = sem("x_T"), sem("x_T_kept"), sem("h_act"), sem("h_dve")
        proj_done, proj_kept, z_kept = sem("proj_done"), sem("proj_kept"), sem("z_kept")
        conv_done = sem("conv_done")
        ws_T, ws_kept, ws_masked = sem("ws_T"), sem("ws_kept"), sem("ws_masked")
        v_done, v_sq_done, v_rs_half, v_ready = sem("v_done"), sem("v_sq_done"), sem("v_rs_half"), sem("v_ready")
        v_ms_ready = sem("v_ms_ready")
        sgu_done, ya_ready = sem("sgu_done"), sem("ya_ready")
        mixed_done, x_mixed = sem("mixed_done"), sem("x_mixed")
        n_ss, n_rstd, xn_ready = sem("n_ss"), sem("n_rstd"), sem("xn_ready")
        xn_stored = [sem(f"xn_stored{s}") for s in range(2)]
        n_T, n_T_kept, logit_done = sem("n_T"), sem("n_T_kept"), sem("logit_done")
        g_diff_ready, g_exp_ready = sem("g_diff_ready"), sem("g_exp_ready")
        e_gap_ready, e_exp_ready = sem("e_gap_ready"), sem("e_exp_ready")
        hots_ready, rank_done, entries_ready = sem("hots_ready"), sem("rank_done"), sem("entries_ready")
        scattered, table_loaded, extra_ready = sem("scattered"), sem("table_loaded"), sem("extra_ready")
        idx_g_ready, idx_s_ready = sem("idx_g_ready"), sem("idx_s_ready")
        xg_loaded = [sem(f"xg_loaded{s}") for s in range(2)]
        y_stored = [sem(f"y_stored{s}") for s in range(2)]
        b_T, xT_ready = sem("b_T"), sem("xT_ready")
        g_done, u_done, sig_ready, act_ready = sem("g_done"), sem("u_done"), sem("sig_ready"), sem("act_ready")
        act_T, aT_ready, y_done, y_ready = sem("act_T"), sem("aT_ready"), sem("y_done"), sem("y_ready")
        names = ("w", "idx", "xg", "T", "xT", "gu", "sig", "act", "aT_ps", "aT", "y", "yr", "stored", "free", "dve")
        more = [{n: sem(f"more{l}_{n}") for n in names} for l in range(LAYERS)]
        transfers = sem("transfers")
        moe_done, more_done = sem("moe_done"), sem("more_done")
        y_in_loaded = [sem(f"y_in_loaded{s}") for s in range(4)]
        combined, c_ss = sem("combined"), sem("c_ss")
        h_ready, pool_T, pool_kept = sem("h_ready"), sem("pool_T"), sem("pool_kept")
        mixed1_done, x_mixed1 = sem("mixed1_done"), sem("x_mixed1")
        out_ready, out_stored = sem("out_ready"), sem("out_stored")

        block = ctx.enter_context(nc.Block())

        def bc(ap, shape):
            return ap.to_broadcast(shape)

        @block.sync
        def _(sp):
            for l in range(LAYERS):
                sp.dma_start(vec_rows[l * KD:(l + 1) * KD, :],
                             norm_mix_g[l].rearrange("(m p) -> m p", p=P)).then_inc(vec_loaded, 16)
                sp.dma_start(vec_rows[(2 + l) * KD:(3 + l) * KD, :],
                             norm_ffn_g[l].rearrange("(m p) -> m p", p=P)).then_inc(vec_loaded, 16)
            sp.dma_start(vec_rows[4 * KD:5 * KD, :], c[0].rearrange("(m p) -> m p", p=P)).then_inc(vec_loaded, 16)
            sp.dma_start(vec_rows[5 * KD:NVEC, :],
                         conv_w[0].rearrange("k (m p) -> (k m) p", p=P)).then_inc(vec_loaded, 16)
            for i in range(4):
                sp.dma_start(xr[:, 2 * i:2 * i + 2, :], xv[:, 2 * i:2 * i + 2, :]).then_inc(x_loaded[i], 16)
            ada0 = w_ada[0].rearrange("(k p) n -> p k n", p=P)
            for q in range(4):
                sp.dma_start(cond0[q][:, :, :], ada0[:, 2 * q:2 * q + 2, 0:D]).then_inc(cond0_loaded[q], 16)
            sp.wait_ge(acc_init, 1)
            sp.dma_start(acc0[0:1, :], b_ada[0:1, :]).then_inc(bada_loaded[0], 16)
            for l in range(LAYERS):
                sp.dma_start(r_w[l][:, :, 0:NG],
                             w_group_router[l].rearrange("(k p) n -> p k n", p=P)).then_inc(const_loaded, 16)
                sp.dma_start(r_w[l][:, :, NG:NR],
                             w_expert_router[l].rearrange("(k p) n -> p k n", p=P)).then_inc(const_loaded, 16)
                sp.dma_start(r_b[l][:, 0:NG], b_group_router[l].partition_broadcast(P)).then_inc(const_loaded, 16)
                sp.dma_start(r_b[l][:, NG:NR], b_expert_router[l].partition_broadcast(P)).then_inc(const_loaded, 16)
            with sp.Fori(1, NMOD) as j:
                for q in range(4):
                    sp.wait_ge(cond0_used, 4 * j + (q - 3))
                    sp.dma_start(cond0[q][:, :, :], ada0[:, 2 * q:2 * q + 2, ds(j * D, D)])\
                      .then_inc(cond0_loaded[q], 16)

            inv = w_in_even[0].rearrange("(k p) n -> p k n", p=P)
            col = {"u": 0, "v": 1, "b": 2, "c": 3, "x": 4}
            for n in "cbu":
                sp.dma_start(in_w[n][:, :, :], inv[:, :, col[n] * A:(col[n] + 1) * A]).then_inc(in_loaded[n], 16)
            sp.wait_ge(cond0_used, 4 * NMOD)
            for n in "xv":
                sp.dma_start(in_w[n][:, :, :], inv[:, :, col[n] * A:(col[n] + 1) * A]).then_inc(in_loaded[n], 16)

            ada1 = w_ada[1].rearrange("(k p) n -> k p n", p=P)
            sp.wait_ge(acc_init, 2)
            sp.dma_start(acc1[0:1, :], b_ada[1:2, :]).then_inc(bada_loaded[1], 16)
            for k in range(2):
                sp.dma_start(cond1[k][:, :], ada1[k, :, 0:D]).then_inc(cond1_loaded[k], 16)
            for k in range(2, KD):
                sp.wait_ge(cond1_used, k - 1)
                sp.dma_start(cond1[k % 2][:, :], ada1[k, :, 0:D]).then_inc(cond1_loaded[k % 2], 16)
            with sp.Fori(1, NMOD) as j:
                for k in range(KD):
                    sp.wait_ge(cond1_used, KD * j + (k - 1))
                    sp.dma_start(cond1[k % 2][:, :], ada1[k, :, ds(j * D, D)]).then_inc(cond1_loaded[k % 2], 16)

            sp.wait_ge(row_kept1, 8)
            for m in (SH_M, SC_M, G_M, G_F):
                sp.dma_start(mod1_dram[m:m + 1, :], acc1[0:1, m * D:(m + 1) * D]).then_inc(row_stored1, 16)
            sp.wait_ge(proj_done, 6 * KA)
            sp.dma_start(out_w[:, :, :], w_out_even[0].rearrange("(k p) n -> p k n", p=P)).then_inc(out_w_loaded, 16)
            sp.wait_ge(row_stored1, 64)
            sp.wait_ge(mod_cols[1], 1)
            sp.dma_start(xr[:, :, :], xv).then_inc(x_reloaded, 16)
            sp.wait_ge(proj_done, 8 * KA)
            sp.dma_start(ws_raw[:, :, :], w_spatial[0].rearrange("h t s -> t h s")).then_inc(sgu_loaded, 16)
            sp.dma_start(gv[:, :], sgu_norm_g[0].partition_broadcast(P)).then_inc(sgu_loaded, 16)
            for h in range(HEADS):
                q = (h % 2) * HD
                sp.dma_start(bsp[q:q + HD, h // 2, :], b_spatial[0, h].partition_broadcast(HD))\
                  .then_inc(sgu_loaded, 16)

            def load_down(l, e, s):
                sp.dma_start(down_w[s][:, :, :], moe_w_down[l, ds(e, 1)].rearrange("o (k p) d -> p (o k) d", p=P))\
                  .then_inc(down_loaded[s], 16)

            def load_expert(l, e, s, n=None, with_down=True):
                if n is not None:
                    sp.wait_ge(g_done, n - 1)
                sp.dma_start(gate_w[s][:, :, :], moe_w_gate[l, ds(e, 1)].rearrange("o (k p) f -> p (o k) f", p=P))\
                  .then_inc(gate_loaded[s], 16)
                if n is not None:
                    sp.wait_ge(u_done, n - 1)
                sp.dma_start(up_w[s][:, :, :], moe_w_up[l, ds(e, 1)].rearrange("o (k p) f -> p (o k) f", p=P))\
                  .then_inc(up_loaded[s], 16)
                if n is not None:
                    sp.wait_ge(y_done, n - 1)
                if with_down:
                    load_down(l, e, s)

            def store_xn(l, t):
                sp.wait_ge(xn_ready, l * NT + t + 1)
                sp.dma_start(xn_dram[l][t * P:(t + 1) * P, :], xn[t % 2][:, :]).then_inc(xn_stored[t % 2], 16)

            def load_y(l, t):
                if t >= YB:
                    if l == 0:
                        sp.wait_ge(x_mixed1, t - YB + 1)
                    else:
                        sp.wait_ge(c_ss, NT + t - YB + 1)
                sp.dma_start(y_in[t % YB][:, :, :],
                             y_dram[l].rearrange("(i t p) d -> t p i d", i=2, p=P)[t]).then_inc(y_in_loaded[t % YB], 16)

            def experts(l):
                sp.wait_ge(scattered, 16 * 2 * NT * (l + 1))
                sp.dma_start(table[:, :, :], tables[l].rearrange("(p b) w -> p b w", p=P)).then_inc(table_loaded, 16)
                with sp.Fori(0, NE // 2 - 1) as i:
                    load_expert(l, 2 * i + 2, 0, 2 * i + (l * NE + 2))
                    load_expert(l, 2 * i + 3, 1, 2 * i + (l * NE + 3))
                m = more[l]
                sp.wait_ge(extra_ready, l + 1)
                count = sp.value_load(extra[l][0:1, XB + 1:XB + 2], min_val=0, max_val=XB)
                with sp.If(count > 0):
                    with sp.Fori(0, XB) as j:
                        with sp.If(j < count):
                            sp.wait_ge(m["free"], j + 1)
                            e = sp.value_load(extra[l][0:1, ds(j, 1)], min_val=0, max_val=NE - 1)
                            for dst, src in ((gate_w, moe_w_gate), (up_w, moe_w_up), (down_w, moe_w_down)):
                                sp.dma_start(dst[0][:, :, :], src[l, ds(e, 1)].rearrange("o (k p) f -> p (o k) f", p=P))\
                                  .then_inc(m["w"], 16)

            for t in range(NT):
                store_xn(0, t)
            sp.wait_ge(mixed_done, NT)
            sp.wait_ge(ya_ready, NT)
            load_expert(0, 0, 0)
            load_expert(0, 1, 1)
            sp.wait_ge(x_mixed, NT)
            sp.dma_start(pool_w[:, :, :, :], w_pool[0].rearrange("g (k p) n -> p g k n", p=P)).then_inc(pool_loaded, 16)
            experts(0)
            sp.wait_ge(more_done, 1)
            sp.wait_ge(y_done, NE)
            load_expert(1, 0, 0)
            load_expert(1, 1, 1, with_down=False)

            sp.wait_ge(moe_done, 1)
            for dst, src in ((grow[0], mod1_dram[G_M]), (grow[1], mod1_dram[G_F]), (b1b, mod1_dram[SH_M]),
                             (a1b, mod1_dram[SC_M]), (h_r[0], norm_mix_g[1]), (h_r[1], pool_scale[0])):
                sp.dma_start(dst[:, :], src.partition_broadcast(P)).then_inc(rows1_loaded, 16)
            for t in range(NT):
                load_y(0, t)
                if t >= 3:
                    store_xn(1, t - 3)
            for t in range(NT - 3, NT):
                store_xn(1, t)
            sp.wait_ge(x_mixed1, NT)
            load_down(1, 1, 1)
            experts(1)

            sp.wait_ge(moe_done, 2)
            sp.dma_start(grow[0][:, :], final_norm_g.partition_broadcast(P)).then_inc(final_loaded, 16)
            for t in range(NT):
                load_y(1, t)
                if t >= 3:
                    sp.wait_ge(out_ready, t - 2)
                    sp.dma_start(outv[:, t - 3, :], xr[:, t - 3, :]).then_inc(out_stored, 16)
            for t in range(NT - 3, NT):
                sp.wait_ge(out_ready, t + 1)
                sp.dma_start(outv[:, t, :], xr[:, t, :]).then_inc(out_stored, 16)
            sp.wait_ge(out_stored, 16 * NT)

        @block.gpsimd
        def _(pool):
            g = nc.gpsimd
            made = [0]
            last_token, last_assignment = pool.to_reg(S - 1), pool.to_reg(ASSIGN - 1)

            def note(ins, chain=pool_chain):
                made[0] += 1
                ins.then_inc(chain, 1)

            def settle():
                pool.wait_ge(pool_chain, made[0])

            g.memset(acc0[:, :], 0.0).then_inc(acc_init, 1)
            note(g.memset(ident[:, :], 0.0))
            note(g.memset(ones[:, :], 1.0))
            note(g.memset(lower[:, :], 1.0))
            note(g.memset(eps[:, :], EPS))
            note(g.memset(table[:, :, :], 0))
            note(g.memset(vec_rows[:, :], 0.0)) if False else None
            note(g.iota(rank_g[:, :], [[-1, NG]], base=NG, channel_multiplier=0, allow_small_or_imprecise_dtypes=True))
            note(g.iota(rank_e[:, :], [[-1, EG]], base=EG, channel_multiplier=0, allow_small_or_imprecise_dtypes=True))
            note(g.iota(e_id[:, :], [[1, NE]], base=0, channel_multiplier=0, allow_small_or_imprecise_dtypes=True))
            note(g.iota(j_id[:, :], [[1, XB + 1]], base=0, channel_multiplier=0, allow_small_or_imprecise_dtypes=True))
            note(g.iota(inv_count[:, :], [[1, REACH]], base=1, channel_multiplier=0, allow_small_or_imprecise_dtypes=True))
            note(g.iota(entry[:, :, :, 0], [[P, NT], [S, 2]], base=0, channel_multiplier=1))
            settle()
            note(g.affine_select(out=ident[:, :], in_=ident[:, :], compare_op=ALU.not_equal, fill=1.0,
                                 base=0, pattern=[[-1, P]], channel_multiplier=1))
            note(g.affine_select(out=lower[:, :], in_=lower[:, :], compare_op=ALU.is_ge, fill=0.0,
                                 base=-1, pattern=[[1, P]], channel_multiplier=-1))
            note(g.iota(table[:, :, 0], [[0, NBLK]], base=PAD, channel_multiplier=0))
            settle()
            g.sem_inc(consts, 1)
            for l in range(LAYERS):
                pool.dma_start(tables[l].rearrange("(p b) w -> p b w", p=P), table[:, :, :]).then_inc(table_init, 16)
            pool.wait_ge(x_T, NT)
            g.memset(acc1[:, :], 0.0).then_inc(acc_init, 1)
            pool.wait_ge(ws_kept, 1)
            g.affine_select(out=wsT[:, :, :], in_=wsT[:, :, :], compare_op=ALU.is_ge, fill=0.0, base=0,
                            pattern=[[0, HEADS], [1, P]], channel_multiplier=-1).then_inc(ws_masked, 1)
            pool.wait_ge(v_done, NT)
            for s in range(2):
                note(g.memset(xg[s][:, :], 0.0))
            settle()

            def bands():
                pool.wait_ge(x_mixed, NT)
                for i, win in enumerate(WINDOWS):
                    note(g.memset(band[:, i, :], 1.0 / win))
                    note(g.memset(band_prev[:, i, :], 1.0 / win))
                settle()
                for i, win in enumerate(WINDOWS):
                    note(g.affine_select(out=band[:, i, :], in_=band[:, i, :], compare_op=ALU.is_ge, fill=0.0,
                                         base=0, pattern=[[1, P]], channel_multiplier=-1))
                    note(g.affine_select(out=band_prev[:, i, :], in_=band_prev[:, i, :], compare_op=ALU.is_ge,
                                         fill=0.0, base=win - 1 - P, pattern=[[-1, REACH]], channel_multiplier=1))
                settle()
                for i, win in enumerate(WINDOWS):
                    note(g.affine_select(out=band[:, i, :], in_=band[:, i, :], compare_op=ALU.is_ge, fill=0.0,
                                         base=win - 1, pattern=[[-1, P]], channel_multiplier=1))
                settle()
                note(g.tensor_copy(band0[:, :, :], band[:, :, :]))
                settle()
                for i, win in enumerate(WINDOWS):
                    note(g.tensor_scalar(band0[:, i, 0:win], band0[:, i, 0:win], float(win), None, ALU.mult))
                settle()
                for i, win in enumerate(WINDOWS):
                    note(g.tensor_tensor(band0[:, i, 0:win], band0[:, i, 0:win], inv_count[:, 0:win], ALU.mult))
                settle()
                for i in range(PG):
                    note(g.tensor_tensor(band[:, i, :], band[:, i, :], ident[:, :], ALU.subtract))
                    note(g.tensor_tensor(band0[:, i, :], band0[:, i, :], ident[:, :], ALU.subtract))
                settle()
                g.sem_inc(bands_ready, 1)

            def gather_rows(l, s, done):
                g.sem_inc(transfers, 1)
                g.indirect_dma_start(out=xg[s][:, :], out_offset=None, in_=xn_dram[l],
                                     in_offset=bass.IndirectOffsetOnAxis(ap=idx_g[s][:, 0:1], axis=0),
                                     bounds_check=last_token, oob_is_err=False).then_inc(done, 16)

            def scatter_rows(l, s, done):
                g.sem_inc(transfers, 1)
                g.indirect_dma_start(out=y_dram[l],
                                     out_offset=bass.IndirectOffsetOnAxis(ap=idx_s[s][:, 0:1], axis=0),
                                     in_=y_o[s][:, :], in_offset=None,
                                     bounds_check=last_assignment, oob_is_err=False).then_inc(done, 16)

            def gather(l, n, s, first=False):
                pool.wait_ge(idx_g_ready, n + 1)
                if not first:
                    pool.wait_ge(b_T, n - 1)
                gather_rows(l, s, xg_loaded[s])

            def scatter(l, n, s):
                pool.wait_ge(y_ready, n + 1)
                scatter_rows(l, s, y_stored[s])

            for l in range(LAYERS):
                pool.wait_ge(entries_ready, l + 1)
                if l == 0:
                    pool.wait_ge(table_init, 32)
                for t in range(NT):
                    for i in range(2):
                        g.indirect_dma_start(out=tables[l],
                                             out_offset=bass.IndirectOffsetOnAxis(ap=slot_u[:, t, i:i + 1], axis=0),
                                             in_=entry[:, t, i, :], in_offset=None,
                                             bounds_check=P * NBLK - 1, oob_is_err=True).then_inc(scattered, 16)
                for s in range(2):
                    pool.wait_ge(xn_stored[s], 16 * (NT // 2) * (l + 1))
                n0 = l * NE
                gather(l, n0, 0, first=True)
                gather(l, n0 + 1, 1, first=True)
                if l == 0:
                    bands()
                for e in range(HEAD):
                    gather(l, n0 + e + 2, e % 2)
                    if e:
                        scatter(l, n0 + e - 1, (e - 1) % 2)
                with pool.Fori(0, PAIRS) as i:
                    for e in PAIR:
                        gather(l, 2 * i + (n0 + e + 2), e % 2)
                        scatter(l, 2 * i + (n0 + e - 1), (e - 1) % 2)
                for e in range(NE - TAIL, NE + 1):
                    if e + 2 < NE:
                        gather(l, n0 + e + 2, e % 2)
                    scatter(l, n0 + e - 1, (e - 1) % 2)
                for s in range(2):
                    pool.wait_ge(y_stored[s], 16 * (NE // 2) * (l + 1))
                m = more[l]
                pool.wait_ge(extra_ready, l + 1)
                count = pool.value_load(extra[l][0:1, XB + 1:XB + 2], min_val=0, max_val=XB)
                with pool.If(count > 0):
                    g.sem_inc(m["free"], 1)
                    with pool.Fori(0, XB) as j:
                        with pool.If(j < count):
                            pool.wait_ge(m["idx"], j + 1)
                            gather_rows(l, 0, m["xg"])
                            pool.wait_ge(m["yr"], j + 1)
                            scatter_rows(l, 0, m["stored"])
                            pool.wait_ge(m["stored"], 16 * j + 16)
                            g.sem_inc(m["free"], 1)
                g.sem_inc(moe_done, 1)

        @block.scalar
        def _(act):
            a = nc.scalar
            ch = Chain(act, act_chain)

            def root(which, t0, t1):
                return a.activation(sd[:, which, t0:t1], ss[:, which, t0:t1], ACT.Sqrt, bias=eps[:, :], scale=1.0 / D)

            act.wait_ge(vec_ready, 1)
            a.activation(c_e[:, :], vc, ACT.Exp, scale=-1.0).then_inc(c_exp_ready, 1)
            act.wait_ge(consts, 1)
            for t in range(NT):
                act.wait_ge(x_loaded[t // 2], 16)
                ch.link(a.activation(hT[:, t, :], xr[:, t, :], ACT.Square, accum_out=ss[:, X_IN, t:t + 1]))
            root(X_IN, 0, NT).then_inc(x_ss, 1)
            act.wait_ge(x_rstd, 1)
            for t in range(NT):
                a.activation(xr[:, t, :], xr[:, t, :], ACT.Copy, scale=rstd[:, X_IN, t:t + 1]).then_inc(x_normed, 1)
            for t in range(NT):
                act.wait_ge(x_T, t + 1)
                src = PT if t % 2 == 0 else PA[1]
                a.activation(hT[:, :, t * P:(t + 1) * P], src.rearrange("p (k q) -> p k q", q=P), ACT.Copy)\
                 .then_inc(x_T_kept, 1)
            act.wait_ge(x_T_kept, NT)
            act.wait_ge(gain_sum0, 1)
            for s in range(2):
                a.activation(grow[s][:, :], PA[s], ACT.Copy).then_inc(gain_ready0, 1)
            act.wait_ge(mod_ready[0], 1)
            for k in range(1, KD, 2):
                a.activation(hT[:, k, :], hT[:, k, :], ACT.Identity, scale=a_m[:, k:k + 1],
                             bias=mod[0][:, SH_M, k:k + 1]).then_inc(h_act, 1)
            for gi, dst in enumerate((zT, ybT, yaT)):
                for m in range(KA):
                    for half in range(2):
                        u = gi * 2 * KA + 2 * m + half
                        act.wait_ge(proj_done, u + 1)
                        a.activation(dst[:, m, half * CH:(half + 1) * CH], BANK[u % 4], ACT.Copy).then_inc(proj_kept, 1)
            act.wait_ge(mod_cols[1], 1)
            for i, (m, half) in enumerate((m, half) for m in (SH_M, SC_M, G_M, G_F) for half in range(2)):
                act.wait_ge(row_sum1, i + 1)
                a.activation(acc1[:, m * D + half * CH:m * D + (half + 1) * CH], BANK[4 + i % 2], ACT.Copy)\
                 .then_inc(row_kept1, 1)
            act.wait_ge(ws_T, 1)
            a.activation(wsT[:, :, :], PT.rearrange("p (k q) -> p k q", q=P), ACT.Copy).then_inc(ws_kept, 1)

            def entry_squares(l, t):
                which = N_FFN0 if l == 0 else N_FFN1
                act.wait_ge(x_mixed if l == 0 else x_mixed1, t + 1)
                if l == 0 and t == 0:
                    act.wait_ge(conv_done, 1)
                if l == 1 and t == 0:
                    act.wait_ge(entries_ready, 1)
                if l or t >= 2:
                    act.wait_ge(xn_stored[t % 2], 16 * (l * NT // 2 + t // 2))
                    act.wait_ge(n_T, l * NT + t - 1)
                ch.link(a.activation(xn[t % 2][:, :], xr[:, t, :], ACT.Square, accum_out=ss[:, which, t:t + 1]))
                root(which, t, t + 1).then_inc(n_ss, 1)

            def entry_rows(l, t):
                which = N_FFN0 if l == 0 else N_FFN1
                act.wait_ge(n_rstd, l * NT + t + 1)
                a.activation(xn[t % 2][:, :], xr[:, t, :], ACT.Copy, scale=rstd[:, which, t:t + 1]).then_inc(xn_ready, 1)

            def columns(dst, src, l):
                for k in range(KD):
                    last = a.activation(dst[:, k, :], src[:, k * P:(k + 1) * P], ACT.Identity,
                                        scale=a_f[l][:, k:k + 1], bias=mod[l][:, SH_F, k:k + 1])
                return last

            def entry_columns(l, t):
                n = l * NT + t
                act.wait_ge(n_T, n + 1)
                if n >= 2:
                    act.wait_ge(logit_done, n - 1)
                if l == 0 and t == 0:
                    act.wait_ge(mod_ready[0], 1)
                if l == 1 and t == 0:
                    act.wait_ge(mod_ready[1], 1)
                columns(hTt[t % 2], PT, l).then_inc(n_T_kept, 1)

            for k in range(NT + 4):
                if k < NT:
                    act.wait_ge(v_done, k + 1)
                    if k:
                        act.wait_ge(v_ms_ready, k)
                    a.activation(v_sq[:, :], BANK[k % 2], ACT.Square).then_inc(v_sq_done, 1)
                    act.wait_ge(v_ms_ready, k + 1)
                    if k:
                        act.wait_ge(v_ready, k)
                    a.activation(vsd[:, :], vss[:, :], ACT.Sqrt, bias=eps[:, :], scale=1.0 / HD).then_inc(v_rs_half, 1)
                if 0 <= k - 4:
                    entry_rows(0, k - 4)
                    entry_columns(0, k - 4)
                if 0 <= k - 3 < NT:
                    entry_squares(0, k - 3)

            def block_columns(l, n, s):
                act.wait_ge(b_T, n + 1)
                columns(xT[s], PT, l).then_inc(xT_ready, 1)

            def sigmoid_part(n, first=False):
                act.wait_ge(g_done, n + 1)
                if not first:
                    act.wait_ge(act_ready, n)
                a.activation(sig[:, :], BANK[0], ACT.Exp, scale=-1.0).then_inc(sig_ready, 1)

            def act_columns(n, s):
                act.wait_ge(act_T, n + 1)
                a.activation(aT[s][:, :, :], PM.rearrange("p (k q) -> p k q", q=P), ACT.Copy).then_inc(aT_ready, 1)

            def act_block(l, n, s, first=False, last=False):
                sigmoid_part(n, first)
                if not last:
                    block_columns(l, n + 1, 1 - s)
                act_columns(n, s)

            def moe(l):
                act.wait_ge(g_diff_ready, l + 1)
                a.activation(g_exp[:, :, :], g_diff[:, :, :], ACT.Exp).then_inc(g_exp_ready, 1)
                act.wait_ge(e_gap_ready, l + 1)
                a.activation(r_e[:, :], r_m[3][:, :], ACT.Exp).then_inc(e_exp_ready, 1)
                n0 = l * NE
                block_columns(l, n0, 0)
                for e in range(HEAD):
                    act_block(l, n0 + e, e % 2, first=n0 + e == 0)
                with act.Fori(0, PAIRS) as i:
                    for e in PAIR:
                        act_block(l, 2 * i + (n0 + e), e % 2)
                for e in range(NE - TAIL, NE):
                    act_block(l, n0 + e, e % 2, last=e == NE - 1)
                m = more[l]
                act.wait_ge(extra_ready, l + 1)
                count = act.value_load(extra[l][0:1, XB + 1:XB + 2], min_val=0, max_val=XB)
                with act.If(count > 0):
                    with act.Fori(0, XB) as j:
                        with act.If(j < count):
                            act.wait_ge(m["T"], j + 1)
                            columns(xT[0], PT, l).then_inc(m["xT"], 1)
                            act.wait_ge(m["gu"], j + 1)
                            a.activation(sig[:, :], BANK[0], ACT.Exp, scale=-1.0).then_inc(m["sig"], 1)
                            act.wait_ge(m["aT_ps"], j + 1)
                            a.activation(aT[0][:, :, :], PM.rearrange("p (k q) -> p k q", q=P), ACT.Copy)\
                             .then_inc(m["aT"], 1)

            moe(0)
            for k in range(NT + 3):
                if k < NT:
                    act.wait_ge(combined, k + 1)
                    ch.link(a.activation(y_in[k % YB][:, 1, :], xr[:, k, :], ACT.Square,
                                         accum_out=ss[:, N_MIX1, k:k + 1]))
                    root(N_MIX1, k, k + 1).then_inc(c_ss, 1)
                if 0 <= k - 1 < NT:
                    act.wait_ge(pool_T, k)
                    if k >= 2:
                        act.wait_ge(mixed1_done, k - 1)
                    a.activation(pooledT[:, :, :], PA[0].rearrange("p (k q) -> p k q", q=P), ACT.Copy)\
                     .then_inc(pool_kept, 1)
                if 0 <= k - 3:
                    entry_rows(1, k - 3)
                if 0 <= k - 2 < NT:
                    entry_squares(1, k - 2)
                if 0 <= k - 3:
                    entry_columns(1, k - 3)
            moe(1)
            for t in range(NT):
                act.wait_ge(combined, NT + t + 1)
                ch.link(a.activation(y_in[t % YB][:, 1, :], xr[:, t, :], ACT.Square, accum_out=ss[:, N_FINAL, t:t + 1]))
                root(N_FINAL, t, t + 1).then_inc(c_ss, 1)

        @block.vector
        def _(dve):
            v = nc.vector
            ch = Chain(dve, dve_chain)

            dve.wait_ge(consts, 1)
            ch.link(v.reciprocal(inv_count[:, :], inv_count[:, :]))
            dve.wait_ge(vec_T, 1)
            v.tensor_copy(vec[:, 0:NVEC], PM[:, 0:NVEC]).then_inc(vec_ready, 1)
            dve.wait_ge(c_exp_ready, 1)
            ch.link(v.tensor_scalar(c_e[:, :], c_e[:, :], 1.0, None, ALU.add))
            ch.link(v.reciprocal(c_e[:, :], c_e[:, :]))
            ch.link(v.tensor_tensor(c_act[:, :], c_e[:, :], vc, ALU.mult))
            dve.wait_ge(x_ss, 1)
            v.reciprocal(rstd[:, X_IN, :], sd[:, X_IN, :]).then_inc(x_rstd, 1)

            dve.wait_ge(bada_loaded[0], 16)
            with dve.Fori(0, NMOD) as j:
                ch.enter(j, KD)
                part = acc0[:, ds(j * D, D)]
                for q in range(4):
                    dve.wait_ge(cond0_loaded[q], 16 * j + 16)
                    for i in range(2):
                        ch.link(v.scalar_tensor_tensor(out=part, in0=cond0[q][:, i, :],
                                                       scalar=c_act[:, 2 * q + i:2 * q + i + 1],
                                                       in1=part, op0=ALU.mult, op1=ALU.add))
                    v.sem_inc(cond0_used, 1)
                v.sem_inc(acc_ready[0], 1)
            ch.leave(NMOD)

            def columns_of_mod(l):
                dve.wait_ge(mod_cols[l], 1)
                view = PM[:, 0:NMOD * KD].rearrange("p (m k) -> p m k", k=KD)
                for m in (SH_M, SC_M, SH_F, SC_F)[2 * l:]:
                    ch.link(v.tensor_copy(mod[l][:, m, :], view[:, m, :]))
                ch.link(v.scalar_tensor_tensor(out=a_f[l][:, :], in0=mod[l][:, SC_F, :], scalar=1.0, in1=vg_ffn[l],
                                               op0=ALU.add, op1=ALU.mult))
                if l == 0:
                    ch.link(v.scalar_tensor_tensor(out=a_m[:, :], in0=mod[l][:, SC_M, :], scalar=1.0, in1=vg_mix[l],
                                                   op0=ALU.add, op1=ALU.mult))
                v.sem_inc(mod_ready[l], 1)

            columns_of_mod(0)
            dve.wait_ge(x_T_kept, NT)
            for k in range(0, KD, 2):
                v.tensor_scalar(hT[:, k, :], hT[:, k, :], a_m[:, k:k + 1], mod[0][:, SH_M, k:k + 1],
                                ALU.mult, ALU.add).then_inc(h_dve, 1)

            dve.wait_ge(bada_loaded[1], 16)
            with dve.Fori(0, NMOD) as j:
                ch.enter(j, KD)
                part = acc1[:, ds(j * D, D)]
                for k in range(KD):
                    dve.wait_ge(cond1_loaded[k % 2], 64 * j + 16 * (k // 2 + 1))
                    ch.link(v.scalar_tensor_tensor(out=part, in0=cond1[k % 2][:, :], scalar=c_act[:, k:k + 1],
                                                   in1=part, op0=ALU.mult, op1=ALU.add))
                    v.sem_inc(cond1_used, 1)
                v.sem_inc(acc_ready[1], 1)
            ch.leave(NMOD)
            columns_of_mod(1)

            dve.wait_ge(proj_kept, 6 * KA)
            for m in range(KA):
                for half in range(2):
                    u = 6 * KA + 2 * m + half
                    dve.wait_ge(proj_done, u + 1)
                    part = zT[:, m, half * CH:(half + 1) * CH]
                    v.tensor_tensor(part, BANK[u % 4], part, ALU.mult).then_inc(z_kept, 1)
            dve.wait_ge(z_kept, 2 * KA)

            def conv(m):
                ch.link(v.tensor_scalar(conv_t[:, :], zT[:, m, :], conv_col(2, m), None, ALU.mult))
                for back in (1, 2):
                    ch.link(v.scalar_tensor_tensor(out=conv_t[:, back:], in0=zT[:, m, 0:S - back],
                                                   scalar=conv_col(2 - back, m), in1=conv_t[:, back:],
                                                   op0=ALU.mult, op1=ALU.add))
                ch.link(v.tensor_tensor(ybT[:, m, :], ybT[:, m, :], conv_t[:, :], ALU.mult))

            def v_norm(t):
                dve.wait_ge(v_sq_done, t + 1)
                v.tensor_reduce(out=vss[:, :], in_=v_sq[:, :].rearrange("p (h d) -> p h d", d=HD),
                                axis=AX.X, op=ALU.add).then_inc(v_ms_ready, 1)
                dve.wait_ge(v_rs_half, t + 1)
                ch.link(v.reciprocal(vrs[:, :], vsd[:, :]))
                if t >= 2:
                    dve.wait_ge(sgu_done, t - 1)
                dst = v_n[t % 2][:, :].rearrange("p (h d) -> p h d", d=HD)
                ch.link(v.tensor_tensor(dst, BANK[t % 2].rearrange("p (h d) -> p h d", d=HD),
                                        bc(vrs[:, :].unsqueeze(2), [P, HEADS, HD]), ALU.mult))
                v.tensor_tensor(v_n[t % 2][:, :], v_n[t % 2][:, :], gv[:, :], ALU.mult).then_inc(v_ready, 1)

            def spatial_gate(t):
                dve.wait_ge(sgu_done, t + 1)
                ch.link(v.tensor_tensor(gated[:, :], PM, bsp[:, :, :].rearrange("p m q -> p (m q)"), ALU.add))
                u = yaT[:, :, t * P:(t + 1) * P]
                v.tensor_tensor(u, u, gated[:, :].rearrange("p (m q) -> p m q", q=P), ALU.mult).then_inc(ya_ready, 1)

            def residual(t):
                dve.wait_ge(mixed_done, t + 1)
                if t == 0:
                    dve.wait_ge(gain_ready0, 2)
                    dve.wait_ge(x_reloaded, 16)
                ch.link(v.tensor_tensor(res_t[:, :], PA[1], grow[0][:, :], ALU.mult))
                v.tensor_tensor(xr[:, t, :], xr[:, t, :], res_t[:, :], ALU.add).then_inc(x_mixed, 1)

            def entry_rstd(l, t):
                which = N_FFN0 if l == 0 else N_FFN1
                dve.wait_ge(n_ss, l * NT + t + 1)
                v.reciprocal(rstd[:, which, t:t + 1], sd[:, which, t:t + 1]).then_inc(n_rstd, 1)

            dve.wait_ge(sgu_loaded, 16 * (2 + HEADS))
            for k in range(NT + 4):
                if k < NT:
                    v_norm(k)
                if 0 <= k - 4:
                    entry_rstd(0, k - 4)
                if 0 <= k - 1 < NT:
                    spatial_gate(k - 1)
                if k == 0:
                    for m in range(KA):
                        conv(m)
                    v.sem_inc(conv_done, 1)
                if 0 <= k - 2 < NT:
                    residual(k - 2)

            def routing_of(l):
                dve.wait_ge(logit_done, (l + 1) * NT)
                for s in range(2):
                    dve.wait_ge(xn_stored[s], 16 * (NT // 2) * (l + 1))
                if l == 0:
                    dve.wait_ge(const_loaded, 16 * 4 * LAYERS)
                ch.link(v.tensor_tensor(logits[:, :, :], PL[:, 0:NT * NR].rearrange("p (t r) -> p t r", r=NR),
                                        bc(r_b[l][:, :].unsqueeze(1), [P, NT, NR]), ALU.add))
                gl = logits[:, :, 0:NG]
                el = logits[:, :, NG:NR].rearrange("p t (g e) -> p t g e", e=EG)
                gshape, eshape = [P, NT, NG], [P, NT, EG]

                def first_max(val, mx, diff, key, rank, hot_, shape):
                    ch.link(v.tensor_reduce(out=mx, in_=val, axis=AX.X, op=ALU.max))
                    ch.link(v.tensor_tensor(diff, val, bc(mx.unsqueeze(2), shape), ALU.subtract))
                    ch.link(v.tensor_scalar(key, diff, 0.0, None, ALU.is_ge))
                    rb = bc(rank.unsqueeze(1), shape)
                    ch.link(v.tensor_tensor(key, key, rb, ALU.mult))
                    ch.link(v.tensor_reduce(out=r_r[:, :], in_=key, axis=AX.X, op=ALU.max))
                    ch.link(v.tensor_tensor(hot_, rb, bc(r_r[:, :].unsqueeze(2), shape), ALU.is_equal))

                first_max(gl, r_m[0][:, :], g_diff[:, :, :], g_key[:, :, :], rank_g[:, :], g_hot[:, :, :], gshape)
                v.sem_inc(g_diff_ready, 1)
                dve.wait_ge(g_exp_ready, l + 1)
                ch.link(v.tensor_reduce(out=g_w[:, :], in_=g_exp[:, :, :], axis=AX.X, op=ALU.add))
                ch.link(v.reciprocal(g_w[:, :], g_w[:, :]))
                ch.link(v.tensor_tensor(e_prod[:, :, :, :], el, bc(g_hot[:, :, :].unsqueeze(3), [P, NT, NG, EG]), ALU.mult))
                ch.link(v.tensor_reduce(out=e_sel[:, :, :], in_=e_prod[:, :, :, :].rearrange("p t g e -> p t e g"),
                                        axis=AX.X, op=ALU.add))
                first_max(e_sel[:, :, :], r_m[1][:, :], e_diff[:, :, :], e_key[:, :, :], rank_e[:, :],
                          e_hot[0][:, :, :], eshape)
                ch.link(v.scalar_tensor_tensor(out=e_sel[:, :, :], in0=e_hot[0][:, :, :], scalar=-3e38,
                                               in1=e_sel[:, :, :], op0=ALU.mult, op1=ALU.add))
                first_max(e_sel[:, :, :], r_m[2][:, :], e_diff[:, :, :], e_key[:, :, :], rank_e[:, :],
                          e_hot[1][:, :, :], eshape)
                ch.link(v.tensor_tensor(r_m[3][:, :], r_m[2][:, :], r_m[1][:, :], ALU.subtract))
                v.sem_inc(e_gap_ready, 1)
                for i in range(2):
                    ch.link(v.tensor_tensor(hot[i][:, :, :].rearrange("p t (g e) -> p t g e", e=EG),
                                            bc(g_hot[:, :, :].unsqueeze(3), [P, NT, NG, EG]),
                                            bc(e_hot[i][:, :, :].unsqueeze(2), [P, NT, NG, EG]), ALU.mult))
                ch.link(v.tensor_tensor(hots[:, :, :], hot[0][:, :, :], hot[1][:, :, :], ALU.add))
                ch.link(v.memset(before[:, 0, :], 0.0))
                for t in range(NT):
                    ch.link(v.tensor_tensor(before[:, t + 1, :], before[:, t, :], hots[:, t, :], ALU.add))
                v.sem_inc(hots_ready, 1)
                dve.wait_ge(e_exp_ready, l + 1)
                ch.link(v.tensor_scalar(r_r[:, :], r_e[:, :], 1.0, None, ALU.add))
                ch.link(v.reciprocal(r_r[:, :], r_r[:, :]))
                ch.link(v.tensor_tensor(r_r[:, :], r_r[:, :], g_w[:, :], ALU.mult))
                gates = entry[:, :, :, 1].bitcast(F32)
                if l:
                    dve.wait_ge(scattered, 16 * 2 * NT * l)
                ch.link(v.tensor_copy(gates[:, :, 0], r_r[:, :]))
                ch.link(v.tensor_tensor(gates[:, :, 1], r_r[:, :], r_e[:, :], ALU.mult))
                dve.wait_ge(rank_done, l + 1)
                cnt = PM[:, NT * NE:(NT + 1) * NE]
                ch.link(v.tensor_scalar(nblk[:, :], cnt, float(P - 1), None, ALU.add))
                ch.link(v.tensor_copy(cnt_i[:, :], nblk[:, :]))
                ch.link(v.tensor_scalar(cnt_i[:, :], cnt_i[:, :], 7, None, ALU.arith_shift_right))
                ch.link(v.tensor_copy(nblk[:, :], cnt_i[:, :]))
                ch.link(v.tensor_scalar(nblk[:, :], nblk[:, :], -1.0, 0.0, ALU.add, ALU.max))
                ch.link(v.tensor_tensor_scan(bend[:, :], ones[:, 0:NE], nblk[:, :], 0.0, ALU.mult, ALU.add))
                ch.link(v.tensor_copy(pos_i[:, :, :], PM[:, 0:NT * NE].rearrange("p (t e) -> p t e", e=NE)))
                ch.link(v.tensor_scalar(quo_i[:, :, :], pos_i[:, :, :], 7, None, ALU.arith_shift_right))
                ch.link(v.tensor_copy(quo[:, :, :], quo_i[:, :, :]))
                ch.link(v.scalar_tensor_tensor(out=slot[:, :, :], in0=quo[:, :, :], scalar=-float(P),
                                               in1=PM[:, 0:NT * NE].rearrange("p (t e) -> p t e", e=NE),
                                               op0=ALU.mult, op1=ALU.add))
                ch.link(v.scalar_tensor_tensor(out=b_off[:, :], in0=bend[:, :], scalar=float(NE - 1), in1=nblk[:, :],
                                               op0=ALU.add, op1=ALU.subtract))
                ch.link(v.tensor_tensor(b_off[:, :], b_off[:, :], e_id[:, :], ALU.subtract))
                sh = [P, NT, NE]
                ch.link(v.scalar_tensor_tensor(out=s_tmp[:, :, :], in0=quo[:, :, :], scalar=0.0,
                                               in1=bc(b_off[:, :].unsqueeze(1), sh), op0=ALU.is_gt, op1=ALU.mult))
                ch.link(v.tensor_tensor(s_tmp[:, :, :], s_tmp[:, :, :], quo[:, :, :], ALU.add))
                ch.link(v.tensor_tensor(s_tmp[:, :, :], s_tmp[:, :, :], bc(e_id[:, :].unsqueeze(1), sh), ALU.add))
                ch.link(v.scalar_tensor_tensor(out=slot[:, :, :], in0=slot[:, :, :], scalar=float(NBLK),
                                               in1=s_tmp[:, :, :], op0=ALU.mult, op1=ALU.add))
                for i in range(2):
                    ch.link(v.tensor_tensor(s_tmp[:, :, :], slot[:, :, :], hot[i][:, :, :], ALU.mult))
                    ch.link(v.tensor_reduce(out=slot_f[:, :, i], in_=s_tmp[:, :, :], axis=AX.X, op=ALU.add))
                ch.link(v.tensor_copy(slot_u[:, :, :], slot_f[:, :, :]))
                v.sem_inc(entries_ready, 1)
                esh = [1, XB + 1, NE]
                ch.link(v.tensor_tensor(cmp_t[0:1, :, :], bc(bend[0:1, :].unsqueeze(1), esh),
                                        bc(j_id[0:1, :].unsqueeze(2), esh), ALU.is_le))
                ch.link(v.tensor_reduce(out=eid_f[0:1, 0:XB + 1], in_=cmp_t[0:1, :, :], axis=AX.X, op=ALU.add))
                ch.link(v.tensor_scalar(eid_f[0:1, 0:XB + 1], eid_f[0:1, 0:XB + 1], float(NE - 1), None, ALU.min))
                ch.link(v.tensor_copy(eid_f[0:1, XB + 1:XB + 2], bend[0:1, NE - 1:NE]))
                ch.link(v.tensor_copy(extra[l][0:1, :], eid_f[0:1, :]))
                v.sem_inc(extra_ready, 1)

            table_f = table[:, :, :].bitcast(F32)

            def gather_index(e, loaded, s):
                if loaded is not None:
                    dve.wait_ge(xg_loaded[s], loaded)
                v.tensor_copy(idx_g[s][:, :], tok[:, ds(e, 1)]).then_inc(idx_g_ready, 1)

            def silu_mul(done, chain):
                chain.link(v.tensor_scalar(sig[:, :], sig[:, :], 1.0, None, ALU.add))
                chain.link(v.reciprocal(sig[:, :], sig[:, :]))
                chain.link(v.tensor_tensor(act_r[:, :], BANK[0], sig[:, :], ALU.mult))
                done()

            def silu(n):
                dve.wait_ge(sig_ready, n + 1)
                silu_mul(lambda: dve.wait_ge(u_done, n + 1), ch)
                v.tensor_tensor(act_r[:, :], act_r[:, :], BANK[1], ALU.mult).then_inc(act_ready, 1)

            def results(e, n, s, stored):
                dve.wait_ge(y_done, n + 1)
                if stored is not None:
                    dve.wait_ge(y_stored[s], stored)
                ch.link(v.tensor_copy(idx_s[s][:, :], table[:, ds(e, 1), 0]))
                ch.link(v.tensor_copy(gate_c[s][:, :], table_f[:, ds(e, 1), 1]))
                v.scalar_tensor_tensor(out=y_o[s][:, :], in0=PA[1], scalar=gate_c[s][:, :], in1=grow[1][:, :],
                                       op0=ALU.mult, op1=ALU.mult).then_inc(y_ready, 1)

            def moe(l):
                routing_of(l)
                n0, c0 = l * NE, 16 * (NE // 2) * l
                dve.wait_ge(table_loaded, 16 * (l + 1))
                ch.link(v.tensor_scalar(tok[:, :], table[:, :, 0], TOKEN_MASK, None, ALU.bitwise_and))
                for e in range(2):
                    gather_index(e, None, e)
                def dve_block(e, i=None):
                    past, n = (0, n0 + e) if i is None else (16 * i, 2 * i + (n0 + e))
                    if e + 2 < NE:
                        nxt = e + 2 if i is None else 2 * i + (e + 2)
                        gather_index(nxt, past + (c0 + 16 * (e // 2 + 1)), e % 2)
                    silu(n)
                    if e:
                        m, before_m = e - 1, (e - 1) // 2
                        results(m if i is None else 2 * i + m, n - 1, m % 2,
                                past + (c0 + 16 * before_m) if c0 + before_m else None)

                for e in range(HEAD):
                    dve_block(e)
                with dve.Fori(0, PAIRS) as i:
                    ch.enter(i, 10)
                    for e in PAIR:
                        dve_block(e, i)
                ch.leave(PAIRS)
                for e in range(NE - TAIL, NE):
                    dve_block(e)
                results(NE - 1, n0 + NE - 1, (NE - 1) % 2, c0 + 16 * ((NE - 1) // 2))
                m = more[l]
                count = dve.value_load(extra[l][0:1, XB + 1:XB + 2], min_val=0, max_val=XB)
                with dve.If(count > 0):
                    xch = Chain(dve, m["dve"])
                    with dve.Fori(0, XB) as j:
                        with dve.If(j < count):
                            xch.enter(j, 6)
                            dve.wait_ge(m["free"], j + 1)
                            xch.link(v.tensor_copy(idx_g[0][:, :], tok[:, ds(j + NE, 1)]))
                            xch.link(v.tensor_copy(idx_s[0][:, :], table[:, ds(j + NE, 1), 0]))
                            xch.link(v.tensor_copy(gate_c[0][:, :], table_f[:, ds(j + NE, 1), 1]))
                            v.sem_inc(m["idx"], 1)
                            dve.wait_ge(m["sig"], j + 1)
                            silu_mul(lambda: None, xch)
                            v.tensor_tensor(act_r[:, :], act_r[:, :], BANK[1], ALU.mult).then_inc(m["act"], 1)
                            dve.wait_ge(m["y"], j + 1)
                            v.scalar_tensor_tensor(out=y_o[0][:, :], in0=PA[1], scalar=gate_c[0][:, :],
                                                   in1=grow[1][:, :], op0=ALU.mult, op1=ALU.mult).then_inc(m["yr"], 1)

            def combine(l, t):
                dve.wait_ge(y_in_loaded[t % YB], 16 * ((l * NT + t) // YB + 1))
                ch.link(v.tensor_tensor(xr[:, t, :], xr[:, t, :], y_in[t % YB][:, 0, :], ALU.add))
                v.tensor_tensor(xr[:, t, :], xr[:, t, :], y_in[t % YB][:, 1, :], ALU.add).then_inc(combined, 1)

            moe(0)
            dve.wait_ge(rows1_loaded, 16 * 6)
            ch.link(v.scalar_tensor_tensor(out=a1b[:, :], in0=a1b[:, :], scalar=1.0, in1=h_r[0][:, :],
                                           op0=ALU.add, op1=ALU.mult))
            ch.link(v.tensor_tensor(grow[0][:, :], grow[0][:, :], h_r[1][:, :], ALU.mult))
            for k in range(NT + 3):
                if k < NT:
                    combine(0, k)
                if 0 <= k - 1 < NT:
                    t = k - 1
                    dve.wait_ge(c_ss, t + 1)
                    ch.link(v.reciprocal(rstd[:, N_MIX1, t:t + 1], sd[:, N_MIX1, t:t + 1]))
                    if t >= 2:
                        dve.wait_ge(pool_T, t)
                    ch.link(v.scalar_tensor_tensor(out=h_r[t % 2][:, :], in0=xr[:, t, :],
                                                   scalar=rstd[:, N_MIX1, t:t + 1], in1=a1b[:, :],
                                                   op0=ALU.mult, op1=ALU.mult))
                    v.tensor_tensor(h_r[t % 2][:, :], h_r[t % 2][:, :], b1b[:, :], ALU.add).then_inc(h_ready, 1)
                if 0 <= k - 3:
                    entry_rstd(1, k - 3)
                if 0 <= k - 2 < NT:
                    t = k - 2
                    dve.wait_ge(mixed1_done, t + 1)
                    tmp = y_in[t % YB][:, 0, :]
                    ch.link(v.tensor_tensor(tmp, PA[1], grow[0][:, :], ALU.mult))
                    v.tensor_tensor(xr[:, t, :], xr[:, t, :], tmp, ALU.add).then_inc(x_mixed1, 1)
            moe(1)
            dve.wait_ge(final_loaded, 16)
            for k in range(NT + 1):
                if k < NT:
                    combine(1, k)
                if k >= 1:
                    t = k - 1
                    dve.wait_ge(c_ss, NT + t + 1)
                    ch.link(v.reciprocal(rstd[:, N_FINAL, t:t + 1], sd[:, N_FINAL, t:t + 1]))
                    v.scalar_tensor_tensor(out=xr[:, t, :], in0=xr[:, t, :], scalar=rstd[:, N_FINAL, t:t + 1],
                                           in1=grow[0][:, :], op0=ALU.mult, op1=ALU.mult).then_inc(out_ready, 1)

        @block.tensor
        def _(pe):
            mm = nc.tensor.matmul

            def rows_to_columns(dst, src):
                for k in range(KD):
                    last = nc.tensor.transpose(dst[:, k * P:(k + 1) * P], src[:, k * P:(k + 1) * P], ident[:, :])
                return last

            pe.wait_ge(consts, 1)
            pe.wait_ge(vec_loaded, 16 * 6)
            nc.tensor.transpose(PM[:, 0:NVEC], vec_rows[0:NVEC, :], ident[0:NVEC, 0:NVEC]).then_inc(vec_T, 1)
            for t in range(NT):
                pe.wait_ge(x_normed, t + 1)
                if t >= 2:
                    pe.wait_ge(x_T_kept, t - 1)
                rows_to_columns(PT if t % 2 == 0 else PA[1], xr[:, t, :]).then_inc(x_T, 1)

            def columns_of_mod(l, acc):
                for m in (SH_M, SC_M, SH_F, SC_F)[2 * l:]:
                    for k in range(KD):
                        last = mm(PM[:, m * KD + k:m * KD + k + 1], acc[:, m * D + k * P:m * D + (k + 1) * P],
                                  ones[:, 0:1], start=True, stop=True)
                last.then_inc(mod_cols[l], 1)

            pe.wait_ge(acc_ready[0], NMOD)
            pe.wait_ge(vec_ready, 1)
            columns_of_mod(0, acc0)
            pe.wait_ge(x_T_kept, NT)
            for s, m in enumerate((G_M, G_F)):
                for half in range(2):
                    last = mm(BANK[2 * s + half], ones[:, :], acc0[:, m * D + half * CH:m * D + (half + 1) * CH],
                              start=True, stop=True)
            last.then_inc(gain_sum0, 1)

            def project(gi, n):
                pe.wait_ge(in_loaded[n], 16)
                for m in range(KA):
                    for half in range(2):
                        u = gi * 2 * KA + 2 * m + half
                        if u >= 4:
                            done = u - 3
                            pe.wait_ge(*((proj_kept, done) if done <= 6 * KA else (z_kept, done - 6 * KA)))
                        for k in range(KD):
                            last = mm(BANK[u % 4], in_w[n][:, k, m * P:(m + 1) * P],
                                      hT[:, k, half * CH:(half + 1) * CH], start=k == 0, stop=k == KD - 1)
                        last.then_inc(proj_done, 1)

            pe.wait_ge(h_act, KD // 2)
            pe.wait_ge(h_dve, KD // 2)
            pe.wait_ge(gain_ready0, 2)
            for gi, n in enumerate("cbu"):
                project(gi, n)
            pe.wait_ge(acc_ready[1], NMOD)
            pe.wait_ge(mod_ready[0], 1)
            columns_of_mod(1, acc1)
            for i, (m, half) in enumerate((m, half) for m in (SH_M, SC_M, G_M, G_F) for half in range(2)):
                if i >= 2:
                    pe.wait_ge(row_kept1, i - 1)
                mm(BANK[4 + i % 2], ones[:, :], acc1[:, m * D + half * CH:m * D + (half + 1) * CH],
                   start=True, stop=True).then_inc(row_sum1, 1)
            project(3, "x")
            pe.wait_ge(sgu_loaded, 16 * (2 + HEADS))
            pe.wait_ge(row_kept1, 8)
            for h in range(HEADS):
                last = nc.tensor.transpose(PT[:, h * P:(h + 1) * P], ws_raw[:, h, :], ident[:, :])
            last.then_inc(ws_T, 1)

            def entry_T(l, t):
                n = l * NT + t
                pe.wait_ge(xn_ready, n + 1)
                if t:
                    pe.wait_ge(n_T_kept, n)
                rows_to_columns(PT, xn[t % 2]).then_inc(n_T, 1)

            def entry_logits(l, t):
                pe.wait_ge(n_T_kept, l * NT + t + 1)
                for k in range(KD):
                    last = mm(PL[:, t * NR:(t + 1) * NR], hTt[t % 2][:, k, :], r_w[l][:, k, :],
                              start=k == 0, stop=k == KD - 1)
                last.then_inc(logit_done, 1)

            pe.wait_ge(in_loaded["v"], 16)
            pe.wait_ge(z_kept, 2 * KA)
            for k in range(NT + 5):
                if k < NT:
                    if k >= 2:
                        pe.wait_ge(v_ready, k - 1)
                    for q in range(KD):
                        last = mm(BANK[k % 2], hT[:, q, k * P:(k + 1) * P], in_w["v"][:, q, :],
                                  start=q == 0, stop=q == KD - 1)
                    last.then_inc(v_done, 1)
                if 0 <= k - 1 < NT:
                    t = k - 1
                    pe.wait_ge(v_ready, t + 1)
                    if t == 0:
                        pe.wait_ge(ws_masked, 1)
                        pe.wait_ge(mod_ready[1], 1)
                    else:
                        pe.wait_ge(ya_ready, t)
                    for h in range(HEADS):
                        q = (h % 2) * HD
                        last = mm(PM[q:q + HD, (h // 2) * P:(h // 2 + 1) * P], v_n[t % 2][:, h * HD:(h + 1) * HD],
                                  wsT[:, h, :], start=True, stop=True)
                    last.then_inc(sgu_done, 1)
                if 0 <= k - 2 < NT:
                    t = k - 2
                    pe.wait_ge(ya_ready, t + 1)
                    if t == 0:
                        pe.wait_ge(conv_done, 1)
                        pe.wait_ge(out_w_loaded, 16)
                    else:
                        pe.wait_ge(x_mixed, t)
                    for half in range(2):
                        for q in range(KD):
                            part = yaT[:, q, t * P:(t + 1) * P] if q < KA else ybT[:, q - KA, t * P:(t + 1) * P]
                            last = mm(BANK[2 + half], part, out_w[:, q, half * CH:(half + 1) * CH],
                                      start=q == 0, stop=q == KD - 1)
                    last.then_inc(mixed_done, 1)
                if k == 4:
                    pe.wait_ge(const_loaded, 16 * 4 * LAYERS)
                    pe.wait_ge(ws_kept, 1)
                if 0 <= k - 4 < NT:
                    entry_T(0, k - 4)
                if 0 <= k - 5:
                    entry_logits(0, k - 5)

            def block_T(n, s, loaded):
                pe.wait_ge(xg_loaded[s], loaded)
                pe.wait_ge(xT_ready, n) if not isinstance(n, int) or n > 0 else None
                rows_to_columns(PT, xg[s]).then_inc(b_T, 1)

            def gate_up(s):
                for q in range(KD):
                    lg = mm(BANK[0], xT[s][:, q, :], gate_w[s][:, q, :], start=q == 0, stop=q == KD - 1)
                yield lg
                for q in range(KD):
                    lu = mm(BANK[1], xT[s][:, q, :], up_w[s][:, q, :], start=q == 0, stop=q == KD - 1)
                yield lu

            def act_transpose():
                for q in range(KF):
                    last = nc.tensor.transpose(PM[:, q * P:(q + 1) * P], act_r[:, q * P:(q + 1) * P], ident[:, :])
                return last

            def down(s):
                for half in range(2):
                    for q in range(KF):
                        last = mm(BANK[2 + half], aT[s][:, q, :], down_w[s][:, q, half * CH:(half + 1) * CH],
                                  start=q == 0, stop=q == KF - 1)
                return last

            def down_block(n, s, loaded):
                pe.wait_ge(aT_ready, n + 1)
                pe.wait_ge(down_loaded[s], loaded)
                if not (isinstance(n, int) and n == 0):
                    pe.wait_ge(y_ready, n)
                down(s).then_inc(y_done, 1)

            def pe_block(n, s, loaded, prev_loaded, next_loaded, first=False, last=False):
                pe.wait_ge(xT_ready, n + 1)
                pe.wait_ge(gate_loaded[s], loaded)
                if not (isinstance(n, int) and n == 0):
                    pe.wait_ge(act_ready, n)
                parts = gate_up(s)
                next(parts).then_inc(g_done, 1)
                pe.wait_ge(up_loaded[s], loaded)
                next(parts).then_inc(u_done, 1)
                if not last:
                    block_T(n + 1, 1 - s, next_loaded)
                if not first:
                    down_block(n - 1, 1 - s, prev_loaded)
                pe.wait_ge(act_ready, n + 1)
                act_transpose().then_inc(act_T, 1)

            def moe(l):
                pe.wait_ge(hots_ready, l + 1)
                if l == 0:
                    pe.wait_ge(ya_ready, NT)
                flat = hots[:, :, :].rearrange("p t e -> p (t e)")
                bflat = before[:, :, :].rearrange("p t e -> p (t e)")
                mm(PM[:, 0:NT * NE], lower[:, :], flat, start=True, stop=False)
                mm(PM[:, 0:NT * NE], ones[:, :], bflat[:, 0:NT * NE], start=False, stop=True)
                mm(PM[:, NT * NE:(NT + 1) * NE], ones[:, :], bflat[:, NT * NE:(NT + 1) * NE],
                   start=True, stop=True).then_inc(rank_done, 1)
                n0, c0 = l * NE, 16 * (NE // 2) * l
                pe.wait_ge(n_T_kept, (l + 1) * NT)
                block_T(n0, 0, c0 + 16)
                pe.wait_ge(entries_ready, l + 1)
                def one(e, i=None):
                    n, past = (n0 + e, c0) if i is None else (2 * i + (n0 + e), 16 * i + c0)
                    pe_block(n, e % 2, past + 16 * (e // 2 + 1), past + 16 * ((e - 1) // 2 + 1),
                             past + 16 * ((e + 1) // 2 + 1), first=e == 0, last=e == NE - 1)

                for e in range(HEAD):
                    one(e)
                with pe.Fori(0, PAIRS) as i:
                    for e in PAIR:
                        one(e, i)
                for e in range(NE - TAIL, NE):
                    one(e)
                down_block(n0 + NE - 1, (NE - 1) % 2, c0 + 16 * (NE // 2))
                m = more[l]
                pe.wait_ge(extra_ready, l + 1)
                count = pe.value_load(extra[l][0:1, XB + 1:XB + 2], min_val=0, max_val=XB)
                with pe.If(count > 0):
                    with pe.Fori(0, XB) as j:
                        with pe.If(j < count):
                            pe.wait_ge(m["xg"], 16 * j + 16)
                            rows_to_columns(PT, xg[0]).then_inc(m["T"], 1)
                            pe.wait_ge(m["xT"], j + 1)
                            pe.wait_ge(m["w"], 48 * j + 48)
                            parts = gate_up(0)
                            next(parts)
                            next(parts).then_inc(m["gu"], 1)
                            pe.wait_ge(m["act"], j + 1)
                            act_transpose().then_inc(m["aT_ps"], 1)
                            pe.wait_ge(m["aT"], j + 1)
                            down(0).then_inc(m["y"], 1)
                            pe.wait_ge(m["y"], j + 1)
                nc.tensor.sem_inc(more_done, 1)

            moe(0)
            pe.wait_ge(bands_ready, 1)
            pe.wait_ge(pool_loaded, 16)
            for k in range(NT + 4):
                if 0 <= k - 1 < NT:
                    t = k - 1
                    pe.wait_ge(h_ready, t + 1)
                    if t:
                        pe.wait_ge(pool_kept, t)
                    for q in range(KD):
                        g = q // 2
                        part = PA[0][:, q * P:(q + 1) * P]
                        last = mm(part, h_r[t % 2][:, q * P:(q + 1) * P], (band if t else band0)[:, g, :],
                                  start=True, stop=t == 0)
                        if t:
                            last = mm(part[:, 0:REACH], h_r[1 - t % 2][:, q * P:(q + 1) * P], band_prev[:, g, :],
                                      start=False, stop=True)
                    last.then_inc(pool_T, 1)
                    pe.wait_ge(pool_kept, t + 1)
                    if t:
                        pe.wait_ge(x_mixed1, t)
                    for g in range(PG):
                        for q in range(2):
                            last = mm(PA[1][:, g * PD:(g + 1) * PD], pooledT[:, 2 * g + q, :], pool_w[:, g, q, :],
                                      start=q == 0, stop=q == 1)
                    last.then_inc(mixed1_done, 1)
                if 0 <= k - 3 < NT:
                    entry_T(1, k - 3)
                if 0 <= k - 4:
                    entry_logits(1, k - 4)
            moe(1)


_INS = ["x", "c", "w_ada", "b_ada", "norm_mix_g", "norm_ffn_g", "w_in_even", "sgu_norm_g", "w_spatial",
        "b_spatial", "conv_w", "w_out_even", "w_pool", "pool_scale", "w_group_router", "b_group_router",
        "w_expert_router", "b_expert_router", "moe_w_gate", "moe_w_up", "moe_w_down", "final_norm_g"]


def kernel(**inputs):
    import numpy as _np
    import concourse.bacc as _bacc
    from concourse import mybir as _mybir
    from concourse.bass_utils import run_bass_kernel_spmd as _run

    nc = _bacc.Bacc("TRN2", target_bir_lowering=False, num_devices=1)
    arrays, args = {}, []
    for name in _INS:
        a = _np.ascontiguousarray(inputs[name])
        arrays[f"in_{name}_dram"] = a
        args.append(nc.dram_tensor(f"in_{name}_dram", a.shape, _mybir.dt.from_np(a.dtype), kind="ExternalInput").ap())
    shape = tuple(inputs["x"].shape)
    args.append(nc.dram_tensor("out_0_dram", shape, _mybir.dt.from_np(_np.dtype("float32")), kind="ExternalOutput").ap())
    hybrid_trunk(nc, *args)
    r = _run(nc, [arrays], core_ids=[0])
    return r.results[0]["out_0_dram"]
```

```python
import concourse.bass as bass
from concourse import mybir
from contextlib import ExitStack


class Chain:

    def __init__(self, engine, sem):
        self.engine, self.sem, self.count, self.index = engine, sem, 0, None

    def value(self):
        return self.count if self.index is None else self.index * self.per + self.count

    def link(self, ins):
        self.count += 1
        ins.then_inc(self.sem, 1)
        self.engine.wait_ge(self.sem, self.value())

    def enter(self, index, per):
        self.index, self.per, self.start = index, per, self.count

    def leave(self, trips):
        assert self.count - self.start == self.per, (self.count - self.start, self.per)
        self.count, self.index = self.start + trips * self.per, None


def hybrid_trunk(nc, x, c, w_ada, b_ada, norm_mix_g, norm_ffn_g, w_in_even, sgu_norm_g, w_spatial,
                 b_spatial, conv_w, w_out_even, w_pool, pool_scale, w_group_router, b_group_router,
                 w_expert_router, b_expert_router, moe_w_gate, moe_w_up, moe_w_down, final_norm_g, out):
    F32, I32, U32, F32R = mybir.dt.float32, mybir.dt.int32, mybir.dt.uint32, mybir.dt.float32r
    ALU, ACT, AX = mybir.AluOpType, mybir.ActivationFunctionType, mybir.AxisListType
    ds = bass.ds

    P = 128
    S, D = x.shape[1], x.shape[2]
    NT, KD = S // P, D // P
    LAYERS = w_ada.shape[0]
    A = D // 2
    KA = A // P
    HEADS = w_spatial.shape[1]
    HD = A // HEADS
    NG, NE = w_group_router.shape[2], w_expert_router.shape[2]
    EG = NE // NG
    FE = moe_w_gate.shape[3]
    KF = FE // P
    NR = NG + NE
    PG = w_pool.shape[1]
    PD = D // PG
    WINDOWS = (2, 4, 8, 16)
    REACH = max(WINDOWS)
    EPS = 1e-6
    ASSIGN = 2 * S
    XB = ASSIGN // P - 1
    NBLK = NE + XB + 1
    PAD = 4096
    TOKEN_MASK = PAD | (S - 1)
    CH = 512
    HALF = D // 2
    assert NT == KD == 8 and LAYERS == 2 and P == w_spatial.shape[2] and CH == FE == A
    NMOD = 6
    SH_M, SC_M, G_M, SH_F, SC_F, G_F = range(NMOD)
    HEAD, TAIL = 3, 3
    PAIRS = (NE - HEAD - TAIL) // 2
    PAIR = (HEAD, HEAD + 1)

    xv = x[0].rearrange("(t p) d -> p t d", p=P)
    outv = out[0].rearrange("(t p) d -> p t d", p=P)

    xn_dram = [nc.dram_tensor(f"normed_rows{l}", [S, D], F32, kind="Internal").ap() for l in range(LAYERS)]
    y_dram = [nc.dram_tensor(f"expert_rows{l}", [ASSIGN, D], F32, kind="Internal").ap() for l in range(LAYERS)]
    mod1_dram = nc.dram_tensor("mod_rows1", [NMOD, D], F32, kind="Internal").ap()

    ctx = ExitStack()
    with ctx:
        KB = 1024
        base = (nc.sbuf_base + 31) // 32 * 32
        X0 = base
        W0 = X0 + 32 * KB
        Z0 = W0 + 96 * KB
        H0 = Z0 + 16 * KB
        G0 = H0 + 32 * KB
        T0 = G0 + 8 * KB
        C0 = T0 + 16 * KB + 256
        END = nc.sbuf_top
        cursor = [C0]

        def at(name, shape, off, dt=F32):
            return nc.alloc_sbuf_tensor_at(name, shape, dt, offset=off)

        def small(name, shape, dt=F32):
            n = 4
            for s in shape[1:]:
                n *= s
            off = cursor[0]
            cursor[0] = (off + n + 31) // 32 * 32
            assert cursor[0] <= END, (name, cursor[0], END)
            return at(name, shape, off, dt)

        xr = at("x_rows", [P, NT, D], X0)
        SLOT = 16 * KB
        SA, SB_, SC, SD, SE, SF = [W0 + i * SLOT for i in range(6)]
        gate_w = [at(f"gate_w{s}", [P, KD, FE], o) for s, o in enumerate((SD, SA))]
        up_w = [at(f"up_w{s}", [P, KD, FE], o) for s, o in enumerate((SE, SB_))]
        down_w = [at(f"down_w{s}", [P, KF, D], o) for s, o in enumerate((SF, SC))]
        acc0 = at("cond_acc0", [P, 2 * D], SF)
        cond0 = [at(f"cond0_w{q}", [P, 2, D], SD + q * 8 * KB) for q in range(4)]
        acc = [at(f"cond_acc{q}", [P, D], X0 + 4 * q * KB) for q in range(2)]
        bias = [at(f"cond_bias{q}", [P, D], X0 + (8 + 4 * q) * KB) for q in range(2)]
        UNITS = 4
        cond = [at(f"cond_w{q}", [P, D], X0 + (16 + 4 * q) * KB) for q in range(UNITS)]
        row_kept = at("mod_row", [1, D], T0)
        PARTS = [(0, m) for m in range(2, NMOD)] + [(1, m) for m in range(NMOD)]
        N0 = NMOD - 2

        def as_columns(l, m):
            return m in (SH_F, SC_F)

        PART_BEHIND = {4 + 2 * n: n for n in range(len(PARTS))}
        ROWS_BEFORE = [sum(not as_columns(*q) for q in PARTS[:n]) for n in range(len(PARTS) + 1)]
        hT = at("h_columns", [P, KD, S], H0)
        in_w = {n: at(f"in_w_{n}", [P, KD, A], o) for n, o in zip("cbuxv", (SA, SB_, SC, SD, SE))}
        zT = at("conv_in", [P, KA, S], Z0)
        ybT = at("mix_b", [P, KA, S], SF)
        yaT = at("mix_a", [P, KA, S], SA)
        out_w = at("out_w", [P, KD, D], SB_)
        ws_raw = at("spatial_w", [P, HEADS, P], SD)
        wsT = at("spatial_wT", [P, HEADS, P], SD + 4 * KB)
        bsp = at("spatial_bias", [P, KA, P], SD + 8 * KB)
        gv = at("sgu_gain", [P, A], SD + 10 * KB)
        conv_t = at("conv_out", [P, S], T0)
        v_sq = at("v_squares", [P, A], T0 + 4 * KB)
        v_n = [at(f"v_normed{s}", [P, A], T0 + (6 + 2 * s) * KB) for s in range(2)]
        gated = at("gate_tmp", [P, KA * P], T0 + 10 * KB)
        res_t = at("residual_tmp", [P, D], T0 + 12 * KB)
        a1b = at("scale_row1", [P, D], H0)
        b1b = at("shift_row1", [P, D], H0 + 8 * KB)
        YB = 4
        y_in = [at("y_in0", [P, 2, 2, D], H0)[:, :, 1, :]]
        y_in += [at(f"y_in{s}", [P, 2, D], o)[:, :, :] for s, o in enumerate((H0 + 16 * KB, SC, SC + 8 * KB), 1)]
        h_r = [at(f"h_rows{s}", [P, D], H0 + (24 + 4 * s) * KB) for s in range(2)]
        pool_w = at("pool_w", [P, PG, 2, PD], T0)
        pooledT = at("pooled_columns", [P, KD, P], T0 + 8 * KB)
        factor = at("row_factor", [P, D], T0 + 8 * KB)
        band = at("band", [P, PG, P], T0 + 12 * KB)
        band0 = at("band_first", [P, PG, P], T0 + 14 * KB)
        band_prev = at("band_previous", [P, PG, REACH], T0 + 16 * KB)
        xn = [at(f"xn{s}", [P, D], Z0 + 4 * KB * s) for s in range(2)]
        hTt = [at(f"h_tile_columns{s}", [P, KD, P], Z0 + (8 + 4 * s) * KB) for s in range(2)]
        xg = [at(f"gathered{s}", [P, D], H0 + 4 * KB * s) for s in range(2)]
        xT = [at(f"block_columns{s}", [P, KD, P], H0 + (8 + 4 * s) * KB) for s in range(2)]
        y_o = [at(f"y_out{s}", [P, D], H0 + (16 + 4 * s) * KB) for s in range(2)]
        aT_hi = at("act_columns_high", [P, KF, P], H0 + 24 * KB, F32R)
        aT_lo = at("act_columns_low", [P, KF, P], H0 + 26 * KB, F32R)
        down_hi = at("down_w_high", [P, KF, D], Z0, F32R)
        down_lo = [at(f"down_w_low{s}", [P, KF, D], o, F32R) for s, o in enumerate((SF, SC))]
        act_r = at("act_rows", [P, FE], H0 + 28 * KB)
        sig = at("sigmoid_tmp", [P, FE], H0 + 30 * KB)
        grow = [at(f"gain_row{s}", [P, D], G0 + 4 * KB * s) for s in range(2)]

        rcur = [Z0]

        def routing(name, shape, dt=F32):
            n = 4
            for s in shape[1:]:
                n *= s
            off = rcur[0]
            rcur[0] = (off + n + 31) // 32 * 32
            assert rcur[0] <= H0, name
            return at(name, shape, off, dt)

        g_diff = routing("g_diff", [P, NT, NG])
        g_exp = routing("g_exp", [P, NT, NG])
        g_key = routing("g_key", [P, NT, NG])
        g_hot = routing("g_hot", [P, NT, NG])
        g_w = routing("g_weight", [P, NT])
        e_prod = routing("e_prod", [P, NT, NG, EG])
        e_sel = routing("e_sel", [P, NT, EG])
        e_diff = routing("e_diff", [P, NT, EG])
        e_key = routing("e_key", [P, NT, EG])
        e_hot = [routing(f"e_hot{i}", [P, NT, EG]) for i in range(2)]
        r_m = [routing(f"r_max{i}", [P, NT]) for i in range(4)]
        r_e = routing("r_exp", [P, NT])
        r_r = routing("r_recip", [P, NT])
        hot = [routing(f"hot{i}", [P, NT, NE]) for i in range(2)]
        hots = routing("hots", [P, NT, NE])
        before = routing("tiles_before", [P, NT + 1, NE])
        s_tmp = routing("slot_tmp", [P, NT, NE])
        cnt_i = routing("cnt_int", [P, NE], I32)
        nblk = routing("more_blocks", [P, NE])
        bend = routing("blocks_end", [P, NE])
        b_off = routing("block_offset", [P, NE])
        kg_hot = routing("rank_of_group", [P, NT])
        ke_hot = [routing(f"rank_of_expert{i}", [P, NT]) for i in range(2)]
        a_pos = routing("a_position", [P, NT, 2])
        a_posi = routing("a_position_int", [P, NT, 2], I32)
        a_quo = routing("a_quotient", [P, NT, 2])
        a_row = routing("a_row", [P, NT, 2])
        a_exp = routing("a_expert", [P, NT, 2])
        a_blk = routing("a_block", [P, NT, 2])
        gates = routing("gates", [P, NT, 2])
        empty = routing("empty", [P, NBLK])
        asg_f = routing("assignment_float", [P, NBLK])
        row_hot = at("row_hot", [P, 2 * NT, P], H0 + 8 * KB)
        blk_hot = at("block_hot", [P, 2 * NT, NBLK], H0 + 16 * KB)
        blk_val = at("block_values", [P, 2 * NT, 2, NBLK], H0 + 19 * KB)

        ident = small("ident", [P, P])
        ones = small("ones", [P, P])
        lower = small("strictly_before", [P, P])
        vec_rows = at("vector_rows", [P, P], T0)
        vec = small("vector_columns", [P, 64])
        c_e = small("c_exp", [P, KD])
        c_act = small("c_act", [P, KD])
        mod = [small(f"mod_columns{l}", [P, NMOD, KD]) for l in range(LAYERS)]
        a_m = small("a_mix", [P, KD])
        a_f = [small(f"a_ffn{l}", [P, KD]) for l in range(LAYERS)]
        r_w = [small(f"router_w{l}", [P, KD, NR]) for l in range(LAYERS)]
        r_b = [small(f"router_b{l}", [P, NR]) for l in range(LAYERS)]
        logits = routing("logits", [P, NT, NR])
        rank_g = small("rank_g", [P, NG])
        rank_e = small("rank_e", [P, EG])
        e_id = small("expert_ids", [P, NE])
        j_id = small("block_ids", [P, XB + 1])
        eps = small("eps", [P, 1])
        X_IN, N_FFN0, N_MIX1, N_FFN1, N_FINAL = range(5)
        ss = small("sum_squares", [P, 5, NT])
        sd = small("root_mean_square", [P, 5, NT])
        rstd = small("rstd", [P, 5, NT])
        vss = small("v_sum_squares", [P, HEADS])
        vsd = small("v_root_mean_square", [P, HEADS])
        vrs = small("v_rstd", [P, HEADS])
        row_id = small("row_ids", [P, P])
        number = small("assignment_numbers", [P, NT, 2])
        asg = small("assignment", [P, NBLK], U32)
        slot_gate = small("slot_gate", [P, NBLK])
        tok = small("token", [P, NBLK], U32)
        idx_g = [small(f"gather_index{s}", [P, 1], U32) for s in range(2)]
        idx_s = [small(f"scatter_index{s}", [P, 1], U32) for s in range(2)]
        gate_c = [small(f"block_gate{s}", [P, 1]) for s in range(2)]
        cmp_t = routing("block_compare", [1, XB + 1, NE])
        eid_f = routing("extra_expert_f", [1, XB + 2])
        extra = [small(f"extra_experts{l}", [1, XB + 2], I32) for l in range(LAYERS)]
        inv_count = small("inverse_counts", [P, REACH])
        vg_mix = [vec[:, l * KD:(l + 1) * KD] for l in range(LAYERS)]
        vg_ffn = [vec[:, (2 + l) * KD:(3 + l) * KD] for l in range(LAYERS)]
        vc = vec[:, 4 * KD:5 * KD]
        NVEC = 5 * KD + 3 * KA

        def conv_col(k, m):
            return vec[:, 5 * KD + k * KA + m:5 * KD + k * KA + m + 1]

        ps = ctx.enter_context(nc.psum_tensor("ps", [P, 8 * CH], F32))
        BANK = [ps[:, i * CH:(i + 1) * CH] for i in range(8)]
        PA = [ps[:, 0:D], ps[:, D:2 * D]]
        PT = ps[:, 4 * CH:6 * CH]
        PM = BANK[6]
        PL = BANK[7]

        def sem(name):
            return ctx.enter_context(nc.semaphore(name))

        vec_loaded, const_loaded = sem("vec_loaded"), sem("const_loaded")
        x_loaded = [sem(f"x_loaded{i}") for i in range(4)]
        bada_loaded = sem("bada_loaded")
        bias_loaded = [sem(f"bias_loaded{q}") for q in range(2)]
        cond0_loaded = [sem(f"cond0_loaded{q}") for q in range(4)]
        cond_loaded = [sem(f"cond_loaded{q}") for q in range(UNITS)]
        in_loaded = {n: sem(f"in_loaded_{n}") for n in "cbuxv"}
        sgu_loaded, out_w_loaded, x_reloaded = sem("sgu_loaded"), sem("out_w_loaded"), sem("x_reloaded")
        pool_loaded, rows1_loaded = sem("pool_loaded"), sem("rows1_loaded")
        final_loaded, gain1_loaded = sem("final_loaded"), sem("gain1_loaded")
        gate_loaded = [sem(f"gate_loaded{s}") for s in range(2)]
        up_loaded = [sem(f"up_loaded{s}") for s in range(2)]
        down_loaded = [sem(f"down_loaded{s}") for s in range(2)]
        consts = sem("consts")
        bands_ready = sem("bands_ready")
        dve_chain, act_chain, pool_chain = sem("dve_chain"), sem("act_chain"), sem("pool_chain")
        vec_T, vec_ready, c_exp_ready = sem("vec_T"), sem("vec_ready"), sem("c_exp_ready")
        acc_init = sem("acc_init")
        cond0_used, cond_used = sem("cond0_used"), sem("cond_used")
        acc0_ready, acc_ready, part_summed = sem("acc0_ready"), sem("acc_ready"), sem("part_summed")
        mod_cols0, mod_ready0, mod_ready = sem("mod_cols0"), sem("mod_ready0"), sem("mod_ready")
        row_out, row_stored = sem("row_out"), sem("row_stored")
        x_ss, x_rstd, x_normed = sem("x_ss"), sem("x_rstd"), sem("x_normed")
        x_T, x_T_kept, h_act, h_dve = sem("x_T"), sem("x_T_kept"), sem("h_act"), sem("h_dve")
        proj_done, proj_kept, z_kept = sem("proj_done"), sem("proj_kept"), sem("z_kept")
        conv_done = sem("conv_done")
        ws_T, ws_kept, ws_masked = sem("ws_T"), sem("ws_kept"), sem("ws_masked")
        v_done, v_sq_done, v_rs_half, v_ready = sem("v_done"), sem("v_sq_done"), sem("v_rs_half"), sem("v_ready")
        v_ms_ready = sem("v_ms_ready")
        sgu_done, ya_ready = sem("sgu_done"), sem("ya_ready")
        mixed_done, x_mixed = sem("mixed_done"), sem("x_mixed")
        n_ss, n_rstd, xn_ready = sem("n_ss"), sem("n_rstd"), sem("xn_ready")
        xn_stored = [sem(f"xn_stored{s}") for s in range(2)]
        n_T, n_T_kept, logit_done = sem("n_T"), sem("n_T_kept"), sem("logit_done")
        g_diff_ready, g_exp_ready = sem("g_diff_ready"), sem("g_exp_ready")
        e_gap_ready, e_exp_ready = sem("e_gap_ready"), sem("e_exp_ready")
        hots_ready, rank_done, entries_ready = sem("hots_ready"), sem("rank_done"), sem("entries_ready")
        table_summed, extra_ready = sem("table_summed"), sem("extra_ready")
        idx_g_ready = sem("idx_g_ready")
        xg_loaded = [sem(f"xg_loaded{s}") for s in range(2)]
        y_stored = [sem(f"y_stored{s}") for s in range(2)]
        b_T, xT_ready = sem("b_T"), sem("xT_ready")
        g_done, u_done, sig_ready, act_ready = sem("g_done"), sem("u_done"), sem("sig_ready"), sem("act_ready")
        hi_ready, lo_ready, aT_hi_ready = sem("hi_ready"), sem("lo_ready"), sem("aT_hi_ready")
        act_T, aT_ready, y_done, y_ready = sem("act_T"), sem("aT_ready"), sem("y_done"), sem("y_ready")
        names = ("w", "idx", "xg", "T", "xT", "gu", "act", "aT_ps", "dve", "y", "yr", "stored", "free", "chain")
        more = [{n: sem(f"more{l}_{n}") for n in names} for l in range(LAYERS)]
        transfers = sem("transfers")
        moe_done, more_done = sem("moe_done"), sem("more_done")
        y_in_loaded = [sem(f"y_in_loaded{s}") for s in range(4)]
        combined, c_ss = sem("combined"), sem("c_ss")
        h_ready, pool_T, pool_kept = sem("h_ready"), sem("pool_T"), sem("pool_kept")
        mixed1_done, x_mixed1 = sem("mixed1_done"), sem("x_mixed1")
        out_ready, out_stored = sem("out_ready"), sem("out_stored")

        block = ctx.enter_context(nc.Block())

        def bc(ap, shape):
            return ap.to_broadcast(shape)

        @block.sync
        def _(sp):
            for l in range(LAYERS):
                sp.dma_start(vec_rows[l * KD:(l + 1) * KD, :],
                             norm_mix_g[l].rearrange("(m p) -> m p", p=P)).then_inc(vec_loaded, 16)
                sp.dma_start(vec_rows[(2 + l) * KD:(3 + l) * KD, :],
                             norm_ffn_g[l].rearrange("(m p) -> m p", p=P)).then_inc(vec_loaded, 16)
            sp.dma_start(vec_rows[4 * KD:5 * KD, :], c[0].rearrange("(m p) -> m p", p=P)).then_inc(vec_loaded, 16)
            sp.dma_start(vec_rows[5 * KD:NVEC, :],
                         conv_w[0].rearrange("k (m p) -> (k m) p", p=P)).then_inc(vec_loaded, 16)
            for i in range(4):
                sp.dma_start(xr[:, 2 * i:2 * i + 2, :], xv[:, 2 * i:2 * i + 2, :]).then_inc(x_loaded[i], 16)
            ada0 = w_ada[0].rearrange("(k p) n -> p k n", p=P)
            for q in range(4):
                sp.dma_start(cond0[q][:, :, :], ada0[:, 2 * q:2 * q + 2, 0:D]).then_inc(cond0_loaded[q], 16)
            sp.wait_ge(acc_init, 1)
            sp.dma_start(acc0[0:1, :], b_ada[0:1, 0:2 * D]).then_inc(bada_loaded, 16)
            for l in range(LAYERS):
                sp.dma_start(r_w[l][:, :, 0:NG],
                             w_group_router[l].rearrange("(k p) n -> p k n", p=P)).then_inc(const_loaded, 16)
                sp.dma_start(r_w[l][:, :, NG:NR],
                             w_expert_router[l].rearrange("(k p) n -> p k n", p=P)).then_inc(const_loaded, 16)
                sp.dma_start(r_b[l][:, 0:NG], b_group_router[l].partition_broadcast(P)).then_inc(const_loaded, 16)
                sp.dma_start(r_b[l][:, NG:NR], b_expert_router[l].partition_broadcast(P)).then_inc(const_loaded, 16)
            for q in range(4):
                sp.wait_ge(cond0_used, q + 1)
                sp.dma_start(cond0[q][:, :, :], ada0[:, 2 * q:2 * q + 2, D:2 * D]).then_inc(cond0_loaded[q], 16)

            inv = w_in_even[0].rearrange("(k p) n -> p k n", p=P)
            col = {"u": 0, "v": 1, "b": 2, "c": 3, "x": 4}
            for n in "cbu":
                sp.dma_start(in_w[n][:, :, :], inv[:, :, col[n] * A:(col[n] + 1) * A]).then_inc(in_loaded[n], 16)

            def part_loads(l, off, n, parity):
                if not isinstance(n, int) or n >= 2:
                    sp.wait_ge(cond_used, KD * n + (1 - 2 * KD))
                sp.dma_start(bias[parity][0:1, :], b_ada[l:l + 1, ds(off, D)]).then_inc(bias_loaded[parity], 16)
                for k in range(KD):
                    if not isinstance(n, int) or KD * n + k >= UNITS:
                        sp.wait_ge(cond_used, KD * n + (k - UNITS + 1))
                    sp.dma_start(cond[k % UNITS][:, :], w_ada[l].rearrange("(k p) n -> k p n", p=P)[k, :, ds(off, D)])\
                      .then_inc(cond_loaded[k % UNITS], 16)

            sp.wait_ge(acc_init, 2)
            for n in range(N0):
                part_loads(0, (n + 2) * D, n, n % 2)
            with sp.Fori(0, NMOD // 2) as j:
                for q in range(2):
                    part_loads(1, j * (2 * D) + q * D, 2 * j + (N0 + q), q)
            for n in "xv":
                sp.dma_start(in_w[n][:, :, :], inv[:, :, col[n] * A:(col[n] + 1) * A]).then_inc(in_loaded[n], 16)
            sp.wait_ge(proj_done, 6 * KA)
            sp.dma_start(out_w[:, :, :], w_out_even[0].rearrange("(k p) n -> p k n", p=P)).then_inc(out_w_loaded, 16)
            sp.wait_ge(part_summed, len(PARTS))
            sp.dma_start(xr[:, :, :], xv).then_inc(x_reloaded, 16)
            sp.wait_ge(proj_done, 8 * KA)
            sp.dma_start(ws_raw[:, :, :], w_spatial[0].rearrange("h t s -> t h s")).then_inc(sgu_loaded, 16)
            sp.dma_start(gv[:, :], sgu_norm_g[0].partition_broadcast(P)).then_inc(sgu_loaded, 16)
            for h in range(HEADS):
                q = (h % 2) * HD
                sp.dma_start(bsp[q:q + HD, h // 2, :], b_spatial[0, h].partition_broadcast(HD))\
                  .then_inc(sgu_loaded, 16)

            def load_down(l, e, s):
                sp.dma_start(down_w[s][:, :, :], moe_w_down[l, ds(e, 1)].rearrange("o (k p) d -> p (o k) d", p=P))\
                  .then_inc(down_loaded[s], 16)

            def load_expert(l, e, s, n=None, with_down=True):
                if n is not None:
                    sp.wait_ge(g_done, n - 1)
                sp.dma_start(gate_w[s][:, :, :], moe_w_gate[l, ds(e, 1)].rearrange("o (k p) f -> p (o k) f", p=P))\
                  .then_inc(gate_loaded[s], 16)
                if n is not None:
                    sp.wait_ge(u_done, n - 1)
                sp.dma_start(up_w[s][:, :, :], moe_w_up[l, ds(e, 1)].rearrange("o (k p) f -> p (o k) f", p=P))\
                  .then_inc(up_loaded[s], 16)
                if n is not None:
                    sp.wait_ge(y_done, n - 1)
                if with_down:
                    load_down(l, e, s)

            def load_y(l, t):
                if t >= YB:
                    if l == 0:
                        sp.wait_ge(x_mixed1, t - YB + 1)
                    else:
                        sp.wait_ge(c_ss, NT + t - YB + 1)
                sp.dma_start(y_in[t % YB],
                             y_dram[l].rearrange("(i t p) d -> t p i d", i=2, p=P)[t]).then_inc(y_in_loaded[t % YB], 16)

            def experts(l):
                with sp.Fori(0, NE // 2 - 1) as i:
                    load_expert(l, 2 * i + 2, 0, 2 * i + (l * NE + 2))
                    load_expert(l, 2 * i + 3, 1, 2 * i + (l * NE + 3))
                if l == 0:
                    load_expert(1, 0, 0, NE)
                    for dst, src in ((a1b, mod1_dram[SC_M]), (factor, norm_mix_g[1]), (b1b, mod1_dram[SH_M])):
                        sp.dma_start(dst[:, :], src.partition_broadcast(P)).then_inc(rows1_loaded, 16)
                m = more[l]
                sp.wait_ge(extra_ready, l + 1)
                count = sp.value_load(extra[l][0:1, XB + 1:XB + 2], min_val=0, max_val=XB)
                with sp.If(count > 0):
                    with sp.Fori(0, XB) as j:
                        with sp.If(j < count):
                            sp.wait_ge(m["free"], j + 1)
                            e = sp.value_load(extra[l][0:1, ds(j, 1)], min_val=0, max_val=NE - 1)
                            for dst, src in ((gate_w, moe_w_gate), (up_w, moe_w_up), (down_w, moe_w_down)):
                                sp.dma_start(dst[1][:, :, :], src[l, ds(e, 1)].rearrange("o (k p) f -> p (o k) f", p=P))\
                                  .then_inc(m["w"], 16)

            for t in range(NT):
                sp.wait_ge(xn_ready, t + 1)
                sp.dma_start(xn_dram[0][t * P:(t + 1) * P, :], xn[t % 2][:, :]).then_inc(xn_stored[t % 2], 16)
            sp.wait_ge(mixed_done, NT)
            sp.wait_ge(ya_ready, NT)
            load_expert(0, 0, 0)
            load_expert(0, 1, 1)
            sp.wait_ge(x_mixed, NT)
            sp.dma_start(pool_w[:, :, :, :], w_pool[0].rearrange("g (k p) n -> p g k n", p=P)).then_inc(pool_loaded, 16)
            sp.wait_ge(row_stored, 16 * 4)
            for dst, src in ((grow[0], mod1_dram[G_M]), (factor, pool_scale[0])):
                sp.dma_start(dst[:, :], src.partition_broadcast(P)).then_inc(rows1_loaded, 16)
            experts(0)

            sp.wait_ge(moe_done, 1)
            for t in range(NT):
                load_y(0, t)
                if t == YB - 1:
                    sp.wait_ge(more_done, 1)
                    load_expert(1, 1, 1, with_down=False)
                    sp.dma_start(grow[1][:, :], mod1_dram[G_F].partition_broadcast(P)).then_inc(gain1_loaded, 16)
            sp.wait_ge(x_mixed1, NT)
            load_down(1, 1, 1)
            sp.dma_start(grow[0][:, :], final_norm_g.partition_broadcast(P)).then_inc(final_loaded, 16)
            experts(1)

            sp.wait_ge(moe_done, 2)
            for t in range(NT):
                load_y(1, t)
            sp.wait_ge(out_stored, 16 * NT)

        @block.gpsimd
        def _(pool):
            g = nc.gpsimd
            made = [0]
            last_token, last_assignment = pool.to_reg(S - 1), pool.to_reg(ASSIGN - 1)

            def note(ins, chain=pool_chain):
                made[0] += 1
                ins.then_inc(chain, 1)

            def settle():
                pool.wait_ge(pool_chain, made[0])

            g.memset(acc0[:, :], 0.0).then_inc(acc_init, 1)
            note(g.memset(ident[:, :], 0.0))
            note(g.memset(ones[:, :], 1.0))
            note(g.memset(lower[:, :], 1.0))
            note(g.memset(eps[:, :], EPS))
            note(g.iota(rank_g[:, :], [[-1, NG]], base=NG, channel_multiplier=0, allow_small_or_imprecise_dtypes=True))
            note(g.iota(rank_e[:, :], [[-1, EG]], base=EG, channel_multiplier=0, allow_small_or_imprecise_dtypes=True))
            note(g.iota(e_id[:, :], [[1, NE]], base=0, channel_multiplier=0, allow_small_or_imprecise_dtypes=True))
            note(g.iota(j_id[:, :], [[1, XB + 1]], base=0, channel_multiplier=0, allow_small_or_imprecise_dtypes=True))
            note(g.iota(inv_count[:, :], [[1, REACH]], base=1, channel_multiplier=0, allow_small_or_imprecise_dtypes=True))
            note(g.iota(number[:, :, :], [[P, NT], [S, 2]], base=1, channel_multiplier=1,
                        allow_small_or_imprecise_dtypes=True))
            note(g.iota(row_id[:, :], [[1, P]], base=0, channel_multiplier=0, allow_small_or_imprecise_dtypes=True))
            settle()
            note(g.affine_select(out=ident[:, :], in_=ident[:, :], compare_op=ALU.not_equal, fill=1.0,
                                 base=0, pattern=[[-1, P]], channel_multiplier=1))
            note(g.affine_select(out=lower[:, :], in_=lower[:, :], compare_op=ALU.is_ge, fill=0.0,
                                 base=-1, pattern=[[1, P]], channel_multiplier=-1))
            settle()
            g.sem_inc(consts, 1)
            pool.wait_ge(x_T, NT)
            for q in range(2):
                note(g.memset(bias[q][:, :], 0.0))
            settle()
            g.sem_inc(acc_init, 1)
            pool.wait_ge(ws_kept, 1)
            g.affine_select(out=wsT[:, :, :], in_=wsT[:, :, :], compare_op=ALU.is_ge, fill=0.0, base=0,
                            pattern=[[0, HEADS], [1, P]], channel_multiplier=-1).then_inc(ws_masked, 1)
            def clear_gathered():
                for s in range(2):
                    note(g.memset(xg[s][:, :], 0.0))
                settle()

            pool.wait_ge(v_done, NT)
            clear_gathered()

            def bands():
                pool.wait_ge(x_mixed, NT)
                for i, win in enumerate(WINDOWS):
                    note(g.memset(band[:, i, :], 1.0 / win))
                    note(g.memset(band_prev[:, i, :], 1.0 / win))
                settle()
                for i, win in enumerate(WINDOWS):
                    note(g.affine_select(out=band[:, i, :], in_=band[:, i, :], compare_op=ALU.is_ge, fill=0.0,
                                         base=0, pattern=[[1, P]], channel_multiplier=-1))
                    note(g.affine_select(out=band_prev[:, i, :], in_=band_prev[:, i, :], compare_op=ALU.is_ge,
                                         fill=0.0, base=win - 1 - P, pattern=[[-1, REACH]], channel_multiplier=1))
                settle()
                for i, win in enumerate(WINDOWS):
                    note(g.affine_select(out=band[:, i, :], in_=band[:, i, :], compare_op=ALU.is_ge, fill=0.0,
                                         base=win - 1, pattern=[[-1, P]], channel_multiplier=1))
                settle()
                note(g.tensor_copy(band0[:, :, :], band[:, :, :]))
                settle()
                for i, win in enumerate(WINDOWS):
                    note(g.tensor_scalar(band0[:, i, 0:win], band0[:, i, 0:win], float(win), None, ALU.mult))
                settle()
                for i, win in enumerate(WINDOWS):
                    note(g.tensor_tensor(band0[:, i, 0:win], band0[:, i, 0:win], inv_count[:, 0:win], ALU.mult))
                settle()
                for i in range(PG):
                    note(g.tensor_tensor(band[:, i, :], band[:, i, :], ident[:, :], ALU.subtract))
                    note(g.tensor_tensor(band0[:, i, :], band0[:, i, :], ident[:, :], ALU.subtract))
                settle()
                g.sem_inc(bands_ready, 1)

            def gather_rows(l, s, done):
                g.sem_inc(transfers, 1)
                g.indirect_dma_start(out=xg[s][:, :], out_offset=None, in_=xn_dram[l],
                                     in_offset=bass.IndirectOffsetOnAxis(ap=idx_g[s][:, 0:1], axis=0),
                                     bounds_check=last_token, oob_is_err=False).then_inc(done, 16)

            def scatter_rows(l, s, done):
                g.sem_inc(transfers, 1)
                g.indirect_dma_start(out=y_dram[l],
                                     out_offset=bass.IndirectOffsetOnAxis(ap=idx_s[s][:, 0:1], axis=0),
                                     in_=y_o[s][:, :], in_offset=None,
                                     bounds_check=last_assignment, oob_is_err=False).then_inc(done, 16)

            def gather(l, n, s, first=False):
                pool.wait_ge(idx_g_ready, n + 1)
                if not first:
                    pool.wait_ge(b_T, n - 1)
                gather_rows(l, s, xg_loaded[s])

            def scatter(l, n, s):
                pool.wait_ge(y_ready, n + 1)
                scatter_rows(l, s, y_stored[s])

            for l in range(LAYERS):
                if l:
                    pool.wait_ge(h_ready, NT)
                    pool.wait_ge(x_mixed1, YB + 1)
                    clear_gathered()
                for s in range(2):
                    pool.wait_ge(xn_stored[s], 16 * (NT // 2) * (l + 1))
                n0 = l * NE
                gather(l, n0, 0, first=True)
                gather(l, n0 + 1, 1, first=True)
                if l == 0:
                    bands()
                for e in range(HEAD):
                    gather(l, n0 + e + 2, e % 2)
                    if e:
                        scatter(l, n0 + e - 1, (e - 1) % 2)
                with pool.Fori(0, PAIRS) as i:
                    for e in PAIR:
                        gather(l, 2 * i + (n0 + e + 2), e % 2)
                        scatter(l, 2 * i + (n0 + e - 1), (e - 1) % 2)
                for e in range(NE - TAIL, NE + 1):
                    if e + 2 < NE:
                        gather(l, n0 + e + 2, e % 2)
                    scatter(l, n0 + e - 1, (e - 1) % 2)
                for s in range(2):
                    pool.wait_ge(y_stored[s], 16 * (NE // 2) * (l + 1))
                m = more[l]
                pool.wait_ge(extra_ready, l + 1)
                count = pool.value_load(extra[l][0:1, XB + 1:XB + 2], min_val=0, max_val=XB)
                with pool.If(count > 0):
                    g.sem_inc(m["free"], 1)
                    with pool.Fori(0, XB) as j:
                        with pool.If(j < count):
                            pool.wait_ge(m["idx"], j + 1)
                            gather_rows(l, 1, m["xg"])
                            pool.wait_ge(m["yr"], j + 1)
                            scatter_rows(l, 1, m["stored"])
                            pool.wait_ge(m["stored"], 16 * j + 16)
                            g.sem_inc(m["free"], 1)
                g.sem_inc(moe_done, 1)

        @block.scalar
        def _(act):
            a = nc.scalar
            ch = Chain(act, act_chain)

            def root(which, t0, t1):
                return a.activation(sd[:, which, t0:t1], ss[:, which, t0:t1], ACT.Sqrt, bias=eps[:, :], scale=1.0 / D)

            act.wait_ge(vec_ready, 1)
            a.activation(c_e[:, :], vc, ACT.Exp, scale=-1.0).then_inc(c_exp_ready, 1)
            act.wait_ge(consts, 1)
            for t in range(NT):
                act.wait_ge(x_loaded[t // 2], 16)
                ch.link(a.activation(hT[:, t, :], xr[:, t, :], ACT.Square, accum_out=ss[:, X_IN, t:t + 1]))
            root(X_IN, 0, NT).then_inc(x_ss, 1)
            act.wait_ge(x_rstd, 1)
            for t in range(NT):
                a.activation(xr[:, t, :], xr[:, t, :], ACT.Copy, scale=rstd[:, X_IN, t:t + 1]).then_inc(x_normed, 1)
            for t in range(NT):
                act.wait_ge(x_T, t + 1)
                src = PT if t % 2 == 0 else PA[1]
                a.activation(hT[:, :, t * P:(t + 1) * P], src.rearrange("p (k q) -> p k q", q=P), ACT.Copy)\
                 .then_inc(x_T_kept, 1)
            act.wait_ge(x_T_kept, NT)
            act.wait_ge(mod_ready0, 1)
            for k in range(1, KD, 2):
                a.activation(hT[:, k, :], hT[:, k, :], ACT.Identity, scale=a_m[:, k:k + 1],
                             bias=mod[0][:, SH_M, k:k + 1]).then_inc(h_act, 1)
            dst = (zT, ybT, yaT)
            for u in range(6 * KA):
                act.wait_ge(proj_done, u + 1)
                m, half = u % (2 * KA) // 2, u % 2
                a.activation(dst[u // (2 * KA)][:, m, half * CH:(half + 1) * CH], BANK[u % 4], ACT.Copy)\
                 .then_inc(proj_kept, 1)
                n = PART_BEHIND.get(u)
                if n is not None and not as_columns(*PARTS[n]):
                    l, m = PARTS[n]
                    act.wait_ge(part_summed, n + 1)
                    if l == 0:
                        a.activation(grow[0 if m == G_M else 1][:, :], PT, ACT.Copy).then_inc(row_out, 1)
                    else:
                        before = ROWS_BEFORE[n] - ROWS_BEFORE[N0]
                        if before:
                            act.wait_ge(row_stored, 16 * before)
                        a.activation(row_kept[0:1, :], PT[0:1, :], ACT.Copy).then_inc(row_out, 1)
                        act.wait_ge(row_out, ROWS_BEFORE[n] + 1)
                        act.dma_start(mod1_dram[m:m + 1, :], row_kept[0:1, :]).then_inc(row_stored, 16)
            act.wait_ge(ws_T, 1)
            a.activation(wsT[:, :, :], PT.rearrange("p (k q) -> p k q", q=P), ACT.Copy).then_inc(ws_kept, 1)

            def entry_squares(l, t):
                which = N_FFN0 if l == 0 else N_FFN1
                act.wait_ge(x_mixed if l == 0 else x_mixed1, t + 1)
                if l == 0 and t == 0:
                    act.wait_ge(conv_done, 1)
                if l == 1 and t == 0:
                    act.wait_ge(entries_ready, 1)
                if l or t >= 2:
                    act.wait_ge(xn_stored[t % 2], 16 * (l * NT // 2 + t // 2))
                    act.wait_ge(n_T, l * NT + t - 1)
                ch.link(a.activation(xn[t % 2][:, :], xr[:, t, :], ACT.Square, accum_out=ss[:, which, t:t + 1]))
                root(which, t, t + 1).then_inc(n_ss, 1)

            def entry_rows(l, t):
                which = N_FFN0 if l == 0 else N_FFN1
                act.wait_ge(n_rstd, l * NT + t + 1)
                a.activation(xn[t % 2][:, :], xr[:, t, :], ACT.Copy, scale=rstd[:, which, t:t + 1]).then_inc(xn_ready, 1)

            def columns(dst, src, l):
                for k in range(KD):
                    last = a.activation(dst[:, k, :], src[:, k * P:(k + 1) * P], ACT.Identity,
                                        scale=a_f[l][:, k:k + 1], bias=mod[l][:, SH_F, k:k + 1])
                return last

            def entry_columns(l, t):
                n = l * NT + t
                act.wait_ge(n_T, n + 1)
                if n >= 2:
                    act.wait_ge(logit_done, n - 1)
                if n == 0:
                    act.wait_ge(mod_ready, 1)
                columns(hTt[t % 2], PT, l).then_inc(n_T_kept, 1)

            for k in range(NT + 4):
                if k < NT:
                    act.wait_ge(v_done, k + 1)
                    if k:
                        act.wait_ge(v_ms_ready, k)
                    a.activation(v_sq[:, :], BANK[k % 2], ACT.Square).then_inc(v_sq_done, 1)
                    act.wait_ge(v_ms_ready, k + 1)
                    if k:
                        act.wait_ge(v_ready, k)
                    a.activation(vsd[:, :], vss[:, :], ACT.Sqrt, bias=eps[:, :], scale=1.0 / HD).then_inc(v_rs_half, 1)
                if 0 <= k - 4:
                    entry_rows(0, k - 4)
                    entry_columns(0, k - 4)
                if 0 <= k - 3 < NT:
                    entry_squares(0, k - 3)

            def block_columns(l, n, s):
                act.wait_ge(b_T, n + 1)
                columns(xT[s], PT, l).then_inc(xT_ready, 1)

            def sigmoid_part(n, first=False):
                act.wait_ge(g_done, n + 1)
                if not first:
                    act.wait_ge(act_ready, n)
                a.activation(sig[:, :], BANK[0], ACT.Exp, scale=-1.0).then_inc(sig_ready, 1)

            def act_high():
                return a.activation(aT_hi[:, :, :], PM.rearrange("p (k q) -> p k q", q=P), ACT.Copy)

            def weights_high(s):
                return a.activation(down_hi[:, :, :], down_w[s][:, :, :], ACT.Copy)

            def act_block(l, n, s, loaded, first=False, last=False):
                sigmoid_part(n, first)
                if not last:
                    block_columns(l, n + 1, 1 - s)
                if not first:
                    act.wait_ge(y_done, n)
                act.wait_ge(down_loaded[s], loaded)
                weights_high(s).then_inc(hi_ready, 1)
                act.wait_ge(act_T, n + 1)
                act_high().then_inc(aT_hi_ready, 1)

            def moe(l):
                act.wait_ge(g_diff_ready, l + 1)
                a.activation(g_exp[:, :, :], g_diff[:, :, :], ACT.Exp).then_inc(g_exp_ready, 1)
                act.wait_ge(e_gap_ready, l + 1)
                a.activation(r_e[:, :], r_m[3][:, :], ACT.Exp).then_inc(e_exp_ready, 1)
                n0 = l * NE
                block_columns(l, n0, 0)
                c0 = 16 * (NE // 2) * l
                act.wait_ge(extra_ready, l + 1)
                for e in range(HEAD):
                    act_block(l, n0 + e, e % 2, c0 + 16 * (e // 2 + 1), first=n0 + e == 0)
                with act.Fori(0, PAIRS) as i:
                    for e in PAIR:
                        act_block(l, 2 * i + (n0 + e), e % 2, 16 * i + (c0 + 16 * (e // 2 + 1)))
                for e in range(NE - TAIL, NE):
                    act_block(l, n0 + e, e % 2, c0 + 16 * (e // 2 + 1), last=e == NE - 1)
                m = more[l]
                act.wait_ge(extra_ready, l + 1)
                count = act.value_load(extra[l][0:1, XB + 1:XB + 2], min_val=0, max_val=XB)
                with act.If(count > 0):
                    with act.Fori(0, XB) as j:
                        with act.If(j < count):
                            act.wait_ge(m["T"], j + 1)
                            columns(xT[1], PT, l).then_inc(m["xT"], 1)
                            act.wait_ge(m["gu"], j + 1)
                            a.activation(sig[:, :], BANK[0], ACT.Exp, scale=-1.0).then_inc(m["act"], 1)
                            act.wait_ge(m["w"], 48 * j + 48)
                            weights_high(1).then_inc(m["act"], 1)
                            act.wait_ge(m["aT_ps"], j + 1)
                            act_high().then_inc(m["act"], 1)

            moe(0)
            for k in range(NT + 3):
                if k < NT:
                    act.wait_ge(combined, k + 1)
                    ch.link(a.activation(y_in[k % YB][:, 1, :], xr[:, k, :], ACT.Square,
                                         accum_out=ss[:, N_MIX1, k:k + 1]))
                    root(N_MIX1, k, k + 1).then_inc(c_ss, 1)
                if 0 <= k - 1 < NT:
                    act.wait_ge(pool_T, k)
                    if k >= 2:
                        act.wait_ge(mixed1_done, k - 1)
                    a.activation(pooledT[:, :, :], PA[0].rearrange("p (k q) -> p k q", q=P), ACT.Copy)\
                     .then_inc(pool_kept, 1)
                if 0 <= k - 3:
                    entry_rows(1, k - 3)
                if 0 <= k - 2 < NT:
                    entry_squares(1, k - 2)
                if 0 <= k - 3:
                    act.wait_ge(xn_ready, NT + k - 2)
                    act.dma_start(xn_dram[1][(k - 3) * P:(k - 2) * P, :], xn[(k - 3) % 2][:, :])\
                       .then_inc(xn_stored[(k - 3) % 2], 16)
                    entry_columns(1, k - 3)
            moe(1)
            for k in range(NT + 2):
                if k < NT:
                    act.wait_ge(combined, NT + k + 1)
                    ch.link(a.activation(y_in[k % YB][:, 1, :], xr[:, k, :], ACT.Square,
                                         accum_out=ss[:, N_FINAL, k:k + 1]))
                    root(N_FINAL, k, k + 1).then_inc(c_ss, 1)
                if k >= 2:
                    act.wait_ge(out_ready, k - 1)
                    act.dma_start(outv[:, k - 2, :], xr[:, k - 2, :]).then_inc(out_stored, 16)

        @block.vector
        def _(dve):
            v = nc.vector
            ch = Chain(dve, dve_chain)

            dve.wait_ge(consts, 1)
            ch.link(v.reciprocal(inv_count[:, :], inv_count[:, :]))
            dve.wait_ge(vec_T, 1)
            v.tensor_copy(vec[:, 0:NVEC], PM[:, 0:NVEC]).then_inc(vec_ready, 1)
            dve.wait_ge(c_exp_ready, 1)
            ch.link(v.tensor_scalar(c_e[:, :], c_e[:, :], 1.0, None, ALU.add))
            ch.link(v.reciprocal(c_e[:, :], c_e[:, :]))
            ch.link(v.tensor_tensor(c_act[:, :], c_e[:, :], vc, ALU.mult))
            dve.wait_ge(x_ss, 1)
            v.reciprocal(rstd[:, X_IN, :], sd[:, X_IN, :]).then_inc(x_rstd, 1)

            dve.wait_ge(bada_loaded, 16)
            for j in range(2):
                part = acc0[:, j * D:(j + 1) * D]
                for q in range(4):
                    dve.wait_ge(cond0_loaded[q], 16 * j + 16)
                    for i in range(2):
                        ch.link(v.scalar_tensor_tensor(out=part, in0=cond0[q][:, i, :],
                                                       scalar=c_act[:, 2 * q + i:2 * q + i + 1],
                                                       in1=part, op0=ALU.mult, op1=ALU.add))
                    v.sem_inc(cond0_used, 1)
                v.sem_inc(acc0_ready, 1)
            dve.wait_ge(mod_cols0, 1)
            ch.link(v.tensor_copy(mod[0][:, 0:2, :], PM[:, 0:2 * KD].rearrange("p (m k) -> p m k", k=KD)))
            ch.link(v.scalar_tensor_tensor(out=a_m[:, :], in0=mod[0][:, SC_M, :], scalar=1.0, in1=vg_mix[0],
                                           op0=ALU.add, op1=ALU.mult))
            v.sem_inc(mod_ready0, 1)
            dve.wait_ge(x_T_kept, NT)
            for k in range(0, KD, 2):
                v.tensor_scalar(hT[:, k, :], hT[:, k, :], a_m[:, k:k + 1], mod[0][:, SH_M, k:k + 1],
                                ALU.mult, ALU.add).then_inc(h_dve, 1)

            def part_sum(n, parity):
                static = isinstance(n, int)
                if not static or n >= 2:
                    dve.wait_ge(part_summed, n - 1)
                past = 16 * (n // 2 + 1) if static else n * 8 + (16 - 8 * parity)
                dve.wait_ge(bias_loaded[parity], past)
                for k in range(KD):
                    dve.wait_ge(cond_loaded[k % UNITS], n * 32 + 16 * (k // UNITS + 1))
                    ch.link(v.scalar_tensor_tensor(out=acc[parity][:, :], in0=cond[k % UNITS][:, :],
                                                   scalar=c_act[:, k:k + 1],
                                                   in1=acc[parity][:, :] if k else bias[parity][:, :],
                                                   op0=ALU.mult, op1=ALU.add))
                    v.sem_inc(cond_used, 1)
                v.sem_inc(acc_ready, 1)

            for n in range(N0):
                part_sum(n, n % 2)
            with dve.Fori(0, NMOD // 2) as j:
                ch.enter(j, 2 * KD)
                for q in range(2):
                    part_sum(2 * j + (N0 + q), q)
            ch.leave(NMOD // 2)
            dve.wait_ge(part_summed, len(PARTS))
            for l in range(LAYERS):
                lo = (l * NMOD + SH_F) * KD
                ch.link(v.tensor_copy(mod[l][:, SH_F:SC_F + 1, :],
                                      PM[:, lo:lo + 2 * KD].rearrange("p (m k) -> p m k", k=KD)))
                ch.link(v.scalar_tensor_tensor(out=a_f[l][:, :], in0=mod[l][:, SC_F, :], scalar=1.0, in1=vg_ffn[l],
                                               op0=ALU.add, op1=ALU.mult))
            v.sem_inc(mod_ready, 1)

            dve.wait_ge(proj_kept, 6 * KA)
            for m in range(KA):
                for half in range(2):
                    u = 6 * KA + 2 * m + half
                    dve.wait_ge(proj_done, u + 1)
                    part = zT[:, m, half * CH:(half + 1) * CH]
                    v.tensor_tensor(part, BANK[u % 4], part, ALU.mult).then_inc(z_kept, 1)
            dve.wait_ge(z_kept, 2 * KA)

            dve.wait_ge(row_stored, 16 * 4)

            def conv(m):
                ch.link(v.tensor_scalar(conv_t[:, :], zT[:, m, :], conv_col(2, m), None, ALU.mult))
                for back in (1, 2):
                    ch.link(v.scalar_tensor_tensor(out=conv_t[:, back:], in0=zT[:, m, 0:S - back],
                                                   scalar=conv_col(2 - back, m), in1=conv_t[:, back:],
                                                   op0=ALU.mult, op1=ALU.add))
                ch.link(v.tensor_tensor(ybT[:, m, :], ybT[:, m, :], conv_t[:, :], ALU.mult))

            def v_norm(t):
                dve.wait_ge(v_sq_done, t + 1)
                v.tensor_reduce(out=vss[:, :], in_=v_sq[:, :].rearrange("p (h d) -> p h d", d=HD),
                                axis=AX.X, op=ALU.add).then_inc(v_ms_ready, 1)
                dve.wait_ge(v_rs_half, t + 1)
                ch.link(v.reciprocal(vrs[:, :], vsd[:, :]))
                if t >= 2:
                    dve.wait_ge(sgu_done, t - 1)
                dst = v_n[t % 2][:, :].rearrange("p (h d) -> p h d", d=HD)
                ch.link(v.tensor_tensor(dst, BANK[t % 2].rearrange("p (h d) -> p h d", d=HD),
                                        bc(vrs[:, :].unsqueeze(2), [P, HEADS, HD]), ALU.mult))
                v.tensor_tensor(v_n[t % 2][:, :], v_n[t % 2][:, :], gv[:, :], ALU.mult).then_inc(v_ready, 1)

            def spatial_gate(t):
                dve.wait_ge(sgu_done, t + 1)
                ch.link(v.tensor_tensor(gated[:, :], PM, bsp[:, :, :].rearrange("p m q -> p (m q)"), ALU.add))
                u = yaT[:, :, t * P:(t + 1) * P]
                v.tensor_tensor(u, u, gated[:, :].rearrange("p (m q) -> p m q", q=P), ALU.mult).then_inc(ya_ready, 1)

            def residual(t):
                dve.wait_ge(mixed_done, t + 1)
                if t == 0:
                    dve.wait_ge(row_out, 1)
                    dve.wait_ge(x_reloaded, 16)
                ch.link(v.tensor_tensor(res_t[:, :], PA[1], grow[0][:, :], ALU.mult))
                v.tensor_tensor(xr[:, t, :], xr[:, t, :], res_t[:, :], ALU.add).then_inc(x_mixed, 1)

            def entry_rstd(l, t):
                which = N_FFN0 if l == 0 else N_FFN1
                dve.wait_ge(n_ss, l * NT + t + 1)
                v.reciprocal(rstd[:, which, t:t + 1], sd[:, which, t:t + 1]).then_inc(n_rstd, 1)

            dve.wait_ge(sgu_loaded, 16 * (2 + HEADS))
            for k in range(NT + 4):
                if k < NT:
                    v_norm(k)
                if 0 <= k - 4:
                    entry_rstd(0, k - 4)
                if 0 <= k - 1 < NT:
                    spatial_gate(k - 1)
                if k == 0:
                    for m in range(KA):
                        conv(m)
                    v.sem_inc(conv_done, 1)
                if 0 <= k - 2 < NT:
                    residual(k - 2)

            def routing_of(l):
                dve.wait_ge(logit_done, (l + 1) * NT)
                for s in range(2):
                    dve.wait_ge(xn_stored[s], 16 * (NT // 2) * (l + 1))
                if l == 0:
                    dve.wait_ge(const_loaded, 16 * 4 * LAYERS)
                ch.link(v.tensor_tensor(logits[:, :, :], PL[:, 0:NT * NR].rearrange("p (t r) -> p t r", r=NR),
                                        bc(r_b[l][:, :].unsqueeze(1), [P, NT, NR]), ALU.add))
                gl = logits[:, :, 0:NG]
                el = logits[:, :, NG:NR].rearrange("p t (g e) -> p t g e", e=EG)
                gshape, eshape = [P, NT, NG], [P, NT, EG]

                def first_max(val, mx, diff, key, rank, top, hot_, shape):
                    ch.link(v.tensor_reduce(out=mx, in_=val, axis=AX.X, op=ALU.max))
                    ch.link(v.tensor_tensor(diff, val, bc(mx.unsqueeze(2), shape), ALU.subtract))
                    ch.link(v.tensor_scalar(key, diff, 0.0, None, ALU.is_ge))
                    rb = bc(rank.unsqueeze(1), shape)
                    ch.link(v.tensor_tensor(key, key, rb, ALU.mult))
                    ch.link(v.tensor_reduce(out=top, in_=key, axis=AX.X, op=ALU.max))
                    ch.link(v.tensor_tensor(hot_, rb, bc(top.unsqueeze(2), shape), ALU.is_equal))

                first_max(gl, r_m[0][:, :], g_diff[:, :, :], g_key[:, :, :], rank_g[:, :],
                          kg_hot[:, :], g_hot[:, :, :], gshape)
                v.sem_inc(g_diff_ready, 1)
                dve.wait_ge(g_exp_ready, l + 1)
                ch.link(v.tensor_reduce(out=g_w[:, :], in_=g_exp[:, :, :], axis=AX.X, op=ALU.add))
                ch.link(v.reciprocal(g_w[:, :], g_w[:, :]))
                ch.link(v.tensor_tensor(e_prod[:, :, :, :], el, bc(g_hot[:, :, :].unsqueeze(3), [P, NT, NG, EG]), ALU.mult))
                ch.link(v.tensor_reduce(out=e_sel[:, :, :], in_=e_prod[:, :, :, :].rearrange("p t g e -> p t e g"),
                                        axis=AX.X, op=ALU.add))
                first_max(e_sel[:, :, :], r_m[1][:, :], e_diff[:, :, :], e_key[:, :, :], rank_e[:, :],
                          ke_hot[0][:, :], e_hot[0][:, :, :], eshape)
                ch.link(v.scalar_tensor_tensor(out=e_sel[:, :, :], in0=e_hot[0][:, :, :], scalar=-3e38,
                                               in1=e_sel[:, :, :], op0=ALU.mult, op1=ALU.add))
                first_max(e_sel[:, :, :], r_m[2][:, :], e_diff[:, :, :], e_key[:, :, :], rank_e[:, :],
                          ke_hot[1][:, :], e_hot[1][:, :, :], eshape)
                ch.link(v.tensor_tensor(r_m[3][:, :], r_m[2][:, :], r_m[1][:, :], ALU.subtract))
                v.sem_inc(e_gap_ready, 1)
                for i in range(2):
                    ch.link(v.tensor_tensor(hot[i][:, :, :].rearrange("p t (g e) -> p t g e", e=EG),
                                            bc(g_hot[:, :, :].unsqueeze(3), [P, NT, NG, EG]),
                                            bc(e_hot[i][:, :, :].unsqueeze(2), [P, NT, NG, EG]), ALU.mult))
                ch.link(v.tensor_tensor(hots[:, :, :], hot[0][:, :, :], hot[1][:, :, :], ALU.add))
                ch.link(v.memset(before[:, 0, :], 0.0))
                for t in range(NT):
                    ch.link(v.tensor_tensor(before[:, t + 1, :], before[:, t, :], hots[:, t, :], ALU.add))
                v.sem_inc(hots_ready, 1)
                dve.wait_ge(e_exp_ready, l + 1)
                ch.link(v.tensor_scalar(r_r[:, :], r_e[:, :], 1.0, None, ALU.add))
                ch.link(v.reciprocal(r_r[:, :], r_r[:, :]))
                ch.link(v.tensor_tensor(r_r[:, :], r_r[:, :], g_w[:, :], ALU.mult))
                ch.link(v.tensor_copy(gates[:, :, 0], r_r[:, :]))
                ch.link(v.tensor_tensor(gates[:, :, 1], r_r[:, :], r_e[:, :], ALU.mult))
                ch.link(v.tensor_scalar(kg_hot[:, :], kg_hot[:, :], -float(EG), float(NE + EG), ALU.mult, ALU.add))
                for i in range(2):
                    ch.link(v.tensor_tensor(a_exp[:, :, i], kg_hot[:, :], ke_hot[i][:, :], ALU.subtract))
                dve.wait_ge(rank_done, l + 1)
                cnt = PM[:, NT * NE:(NT + 1) * NE]
                ch.link(v.tensor_scalar(nblk[:, :], cnt, float(P - 1), None, ALU.add))
                ch.link(v.tensor_copy(cnt_i[:, :], nblk[:, :]))
                ch.link(v.tensor_scalar(cnt_i[:, :], cnt_i[:, :], 7, None, ALU.arith_shift_right))
                ch.link(v.tensor_copy(nblk[:, :], cnt_i[:, :]))
                ch.link(v.tensor_scalar(nblk[:, :], nblk[:, :], -1.0, 0.0, ALU.add, ALU.max))
                ch.link(v.tensor_tensor_scan(bend[:, :], ones[:, 0:NE], nblk[:, :], 0.0, ALU.mult, ALU.add))
                ranks = PM[:, 0:NT * NE].rearrange("p (t e) -> p t e", e=NE)
                for i in range(2):
                    ch.link(v.tensor_tensor(s_tmp[:, :, :], ranks, hot[i][:, :, :], ALU.mult))
                    ch.link(v.tensor_reduce(out=a_pos[:, :, i], in_=s_tmp[:, :, :], axis=AX.X, op=ALU.add))
                ch.link(v.tensor_copy(a_posi[:, :, :], a_pos[:, :, :]))
                ch.link(v.tensor_scalar(a_posi[:, :, :], a_posi[:, :, :], 7, None, ALU.arith_shift_right))
                ch.link(v.tensor_copy(a_quo[:, :, :], a_posi[:, :, :]))
                ch.link(v.scalar_tensor_tensor(out=a_row[:, :, :], in0=a_quo[:, :, :], scalar=-float(P),
                                               in1=a_pos[:, :, :], op0=ALU.mult, op1=ALU.add))
                ch.link(v.tensor_tensor(b_off[:, :], bend[:, :], nblk[:, :], ALU.subtract))
                for i in range(2):
                    ch.link(v.tensor_tensor(s_tmp[:, :, :], hot[i][:, :, :], bc(b_off[:, :].unsqueeze(1), [P, NT, NE]),
                                            ALU.mult))
                    ch.link(v.tensor_reduce(out=a_blk[:, :, i], in_=s_tmp[:, :, :], axis=AX.X, op=ALU.add))
                ch.link(v.scalar_tensor_tensor(out=a_blk[:, :, :], in0=a_blk[:, :, :], scalar=float(NE - 1),
                                               in1=a_exp[:, :, :], op0=ALU.add, op1=ALU.subtract))
                ch.link(v.scalar_tensor_tensor(out=a_blk[:, :, :], in0=a_quo[:, :, :], scalar=0.0,
                                               in1=a_blk[:, :, :], op0=ALU.is_gt, op1=ALU.mult))
                ch.link(v.tensor_tensor(a_blk[:, :, :], a_blk[:, :, :], a_exp[:, :, :], ALU.add))
                ch.link(v.tensor_tensor(a_blk[:, :, :], a_blk[:, :, :], a_quo[:, :, :], ALU.add))
                two = lambda ap: ap.rearrange("p t i -> p (t i)").unsqueeze(2)
                bsh = [P, 2 * NT, NBLK]
                ch.link(v.tensor_tensor(blk_hot[:, :, :], bc(two(a_blk[:, :, :]), bsh),
                                        bc(row_id[:, 0:NBLK].unsqueeze(1), bsh), ALU.is_equal))
                for i, val in enumerate((number, gates)):
                    ch.link(v.tensor_tensor(blk_val[:, :, i, :], blk_hot[:, :, :], bc(two(val[:, :, :]), bsh), ALU.mult))
                rsh = [P, 2 * NT, P]
                ch.link(v.tensor_tensor(row_hot[:, :, :], bc(two(a_row[:, :, :]), rsh),
                                        bc(row_id[:, :].unsqueeze(1), rsh), ALU.is_equal))
                v.sem_inc(entries_ready, 1)

            def further_blocks(l):
                esh = [1, XB + 1, NE]
                ch.link(v.tensor_tensor(cmp_t[0:1, :, :], bc(bend[0:1, :].unsqueeze(1), esh),
                                        bc(j_id[0:1, :].unsqueeze(2), esh), ALU.is_le))
                ch.link(v.tensor_reduce(out=eid_f[0:1, 0:XB + 1], in_=cmp_t[0:1, :, :], axis=AX.X, op=ALU.add))
                ch.link(v.tensor_scalar(eid_f[0:1, 0:XB + 1], eid_f[0:1, 0:XB + 1], float(NE - 1), None, ALU.min))
                ch.link(v.tensor_copy(eid_f[0:1, XB + 1:XB + 2], bend[0:1, NE - 1:NE]))
                ch.link(v.tensor_copy(extra[l][0:1, :], eid_f[0:1, :]))
                v.sem_inc(extra_ready, 1)

            def gather_index(e, loaded, s):
                if loaded is not None:
                    dve.wait_ge(xg_loaded[s], loaded)
                v.tensor_copy(idx_g[s][:, :], tok[:, ds(e, 1)]).then_inc(idx_g_ready, 1)

            def silu_mul(done, chain):
                chain.link(v.tensor_scalar(sig[:, :], sig[:, :], 1.0, None, ALU.add))
                chain.link(v.reciprocal(sig[:, :], sig[:, :]))
                chain.link(v.tensor_tensor(act_r[:, :], BANK[0], sig[:, :], ALU.mult))
                done()

            def silu(n):
                dve.wait_ge(sig_ready, n + 1)
                silu_mul(lambda: dve.wait_ge(u_done, n + 1), ch)
                v.tensor_tensor(act_r[:, :], act_r[:, :], BANK[1], ALU.mult).then_inc(act_ready, 1)

            def weights_low(s):
                return v.tensor_tensor(down_lo[s][:, :, :], down_w[s][:, :, :], down_hi[:, :, :].bitcast(F32),
                                       ALU.subtract)

            def act_low():
                return v.tensor_tensor(aT_lo[:, :, :], PM.rearrange("p (k q) -> p k q", q=P),
                                       aT_hi[:, :, :].bitcast(F32), ALU.subtract)

            def low_parts(n, s):
                dve.wait_ge(hi_ready, n + 1)
                weights_low(s).then_inc(lo_ready, 1)
                dve.wait_ge(aT_hi_ready, n + 1)
                act_low().then_inc(aT_ready, 1)

            def results(e, n, s, stored):
                dve.wait_ge(y_done, n + 1)
                if stored is not None:
                    dve.wait_ge(y_stored[s], stored)
                ch.link(v.tensor_copy(idx_s[s][:, :], asg[:, ds(e, 1)]))
                ch.link(v.tensor_copy(gate_c[s][:, :], slot_gate[:, ds(e, 1)]))
                v.scalar_tensor_tensor(out=y_o[s][:, :], in0=PA[1], scalar=gate_c[s][:, :], in1=grow[1][:, :],
                                       op0=ALU.mult, op1=ALU.mult).then_inc(y_ready, 1)

            def moe(l):
                routing_of(l)
                n0, c0 = l * NE, 16 * (NE // 2) * l
                dve.wait_ge(table_summed, l + 1)
                ch.link(v.tensor_scalar(empty[:, :], PL[:, 0:NBLK], 0.0, float(PAD + 1), ALU.is_equal, ALU.mult))
                ch.link(v.tensor_tensor(asg_f[:, :], PL[:, 0:NBLK], empty[:, :], ALU.add))
                ch.link(v.tensor_scalar(asg[:, :], asg_f[:, :], -1.0, None, ALU.add))
                ch.link(v.tensor_scalar(tok[:, :], asg[:, :], TOKEN_MASK, None, ALU.bitwise_and))
                ch.link(v.tensor_copy(slot_gate[:, :], PL[:, NBLK:2 * NBLK]))
                for e in range(2):
                    gather_index(e, None, e)
                further_blocks(l)
                if l == 0:
                    dve.wait_ge(rows1_loaded, 16 * 2)
                    ch.link(v.tensor_tensor(grow[0][:, :], grow[0][:, :], factor[:, :], ALU.mult))
                else:
                    dve.wait_ge(gain1_loaded, 16)
                def dve_block(e, i=None):
                    past, n = (0, n0 + e) if i is None else (16 * i, 2 * i + (n0 + e))
                    if e + 2 < NE:
                        nxt = e + 2 if i is None else 2 * i + (e + 2)
                        gather_index(nxt, past + (c0 + 16 * (e // 2 + 1)), e % 2)
                    silu(n)
                    if e:
                        m, before_m = e - 1, (e - 1) // 2
                        results(m if i is None else 2 * i + m, n - 1, m % 2,
                                past + (c0 + 16 * before_m) if c0 + before_m else None)
                    low_parts(n, e % 2)

                for e in range(HEAD):
                    dve_block(e)
                with dve.Fori(0, PAIRS) as i:
                    ch.enter(i, 10)
                    for e in PAIR:
                        dve_block(e, i)
                ch.leave(PAIRS)
                for e in range(NE - TAIL, NE):
                    dve_block(e)
                results(NE - 1, n0 + NE - 1, (NE - 1) % 2, c0 + 16 * ((NE - 1) // 2))
                m = more[l]
                count = dve.value_load(extra[l][0:1, XB + 1:XB + 2], min_val=0, max_val=XB)
                with dve.If(count > 0):
                    xch = Chain(dve, m["chain"])
                    with dve.Fori(0, XB) as j:
                        with dve.If(j < count):
                            xch.enter(j, 6)
                            dve.wait_ge(m["free"], j + 1)
                            xch.link(v.tensor_copy(idx_g[1][:, :], tok[:, ds(j + NE, 1)]))
                            xch.link(v.tensor_copy(idx_s[1][:, :], asg[:, ds(j + NE, 1)]))
                            xch.link(v.tensor_copy(gate_c[1][:, :], slot_gate[:, ds(j + NE, 1)]))
                            v.sem_inc(m["idx"], 1)
                            dve.wait_ge(m["act"], 3 * j + 1)
                            silu_mul(lambda: None, xch)
                            v.tensor_tensor(act_r[:, :], act_r[:, :], BANK[1], ALU.mult).then_inc(m["dve"], 1)
                            dve.wait_ge(m["act"], 3 * j + 2)
                            weights_low(1).then_inc(m["dve"], 1)
                            dve.wait_ge(m["act"], 3 * j + 3)
                            act_low().then_inc(m["dve"], 1)
                            dve.wait_ge(m["y"], j + 1)
                            v.scalar_tensor_tensor(out=y_o[1][:, :], in0=PA[1], scalar=gate_c[1][:, :],
                                                   in1=grow[1][:, :], op0=ALU.mult, op1=ALU.mult).then_inc(m["yr"], 1)

            def combine(l, t):
                dve.wait_ge(y_in_loaded[t % YB], 16 * ((l * NT + t) // YB + 1))
                ch.link(v.tensor_tensor(xr[:, t, :], xr[:, t, :], y_in[t % YB][:, 0, :], ALU.add))
                v.tensor_tensor(xr[:, t, :], xr[:, t, :], y_in[t % YB][:, 1, :], ALU.add).then_inc(combined, 1)

            moe(0)
            dve.wait_ge(rows1_loaded, 16 * 5)
            ch.link(v.scalar_tensor_tensor(out=a1b[:, :], in0=a1b[:, :], scalar=1.0, in1=factor[:, :],
                                           op0=ALU.add, op1=ALU.mult))
            for k in range(NT + 3):
                if k < NT:
                    combine(0, k)
                if 0 <= k - 1 < NT:
                    t = k - 1
                    dve.wait_ge(c_ss, t + 1)
                    ch.link(v.reciprocal(rstd[:, N_MIX1, t:t + 1], sd[:, N_MIX1, t:t + 1]))
                    if t >= 2:
                        dve.wait_ge(pool_T, t)
                    ch.link(v.scalar_tensor_tensor(out=h_r[t % 2][:, :], in0=xr[:, t, :],
                                                   scalar=rstd[:, N_MIX1, t:t + 1], in1=a1b[:, :],
                                                   op0=ALU.mult, op1=ALU.mult))
                    v.tensor_tensor(h_r[t % 2][:, :], h_r[t % 2][:, :], b1b[:, :], ALU.add).then_inc(h_ready, 1)
                if 0 <= k - 3:
                    entry_rstd(1, k - 3)
                if 0 <= k - 2 < NT:
                    t = k - 2
                    dve.wait_ge(mixed1_done, t + 1)
                    tmp = y_in[t % YB][:, 0, :]
                    ch.link(v.tensor_tensor(tmp, PA[1], grow[0][:, :], ALU.mult))
                    v.tensor_tensor(xr[:, t, :], xr[:, t, :], tmp, ALU.add).then_inc(x_mixed1, 1)
            moe(1)
            dve.wait_ge(final_loaded, 16)
            for k in range(NT + 1):
                if k < NT:
                    combine(1, k)
                if k >= 1:
                    t = k - 1
                    dve.wait_ge(c_ss, NT + t + 1)
                    ch.link(v.reciprocal(rstd[:, N_FINAL, t:t + 1], sd[:, N_FINAL, t:t + 1]))
                    v.scalar_tensor_tensor(out=xr[:, t, :], in0=xr[:, t, :], scalar=rstd[:, N_FINAL, t:t + 1],
                                           in1=grow[0][:, :], op0=ALU.mult, op1=ALU.mult).then_inc(out_ready, 1)

        @block.tensor
        def _(pe):
            mm = nc.tensor.matmul

            def rows_to_columns(dst, src):
                for k in range(KD):
                    last = nc.tensor.transpose(dst[:, k * P:(k + 1) * P], src[:, k * P:(k + 1) * P], ident[:, :])
                return last

            pe.wait_ge(consts, 1)
            pe.wait_ge(vec_loaded, 16 * 6)
            nc.tensor.transpose(PM[:, 0:NVEC], vec_rows[0:NVEC, :], ident[0:NVEC, 0:NVEC]).then_inc(vec_T, 1)
            for t in range(NT):
                pe.wait_ge(x_normed, t + 1)
                if t >= 2:
                    pe.wait_ge(x_T_kept, t - 1)
                rows_to_columns(PT if t % 2 == 0 else PA[1], xr[:, t, :]).then_inc(x_T, 1)

            def to_columns(col, rows_):
                for k in range(KD):
                    last = mm(PM[:, col * KD + k:col * KD + k + 1], rows_[:, k * P:(k + 1) * P], ones[:, 0:1],
                              start=True, stop=True)
                return last

            pe.wait_ge(acc0_ready, 2)
            pe.wait_ge(vec_ready, 1)
            for m in range(2):
                last = to_columns(m, acc0[:, m * D:(m + 1) * D])
            last.then_inc(mod_cols0, 1)

            def sum_part(n):
                l, m = PARTS[n]
                pe.wait_ge(acc_ready, n + 1)
                if as_columns(l, m):
                    to_columns(l * NMOD + m, acc[n % 2][:, :]).then_inc(part_summed, 1)
                else:
                    if ROWS_BEFORE[n]:
                        pe.wait_ge(row_out, ROWS_BEFORE[n])
                    for half in range(2):
                        last = mm(PT[:, half * CH:(half + 1) * CH], ones[:, :],
                                  acc[n % 2][:, half * CH:(half + 1) * CH], start=True, stop=True)
                    last.then_inc(part_summed, 1)

            def project(gi, n):
                pe.wait_ge(in_loaded[n], 16)
                for m in range(KA):
                    for half in range(2):
                        u = gi * 2 * KA + 2 * m + half
                        if u >= 4:
                            done = u - 3
                            pe.wait_ge(*((proj_kept, done) if done <= 6 * KA else (z_kept, done - 6 * KA)))
                        for k in range(KD):
                            last = mm(BANK[u % 4], in_w[n][:, k, m * P:(m + 1) * P],
                                      hT[:, k, half * CH:(half + 1) * CH], start=k == 0, stop=k == KD - 1)
                        last.then_inc(proj_done, 1)
                        if u in PART_BEHIND:
                            sum_part(PART_BEHIND[u])

            pe.wait_ge(h_act, KD // 2)
            pe.wait_ge(h_dve, KD // 2)
            pe.wait_ge(x_T_kept, NT)
            pe.wait_ge(mod_ready0, 1)
            for gi, n in enumerate("cbu"):
                project(gi, n)
            project(3, "x")
            pe.wait_ge(sgu_loaded, 16 * (2 + HEADS))
            pe.wait_ge(row_out, ROWS_BEFORE[-1])
            for h in range(HEADS):
                last = nc.tensor.transpose(PT[:, h * P:(h + 1) * P], ws_raw[:, h, :], ident[:, :])
            last.then_inc(ws_T, 1)

            def entry_T(l, t):
                n = l * NT + t
                pe.wait_ge(xn_ready, n + 1)
                if t:
                    pe.wait_ge(n_T_kept, n)
                rows_to_columns(PT, xn[t % 2]).then_inc(n_T, 1)

            def entry_logits(l, t):
                pe.wait_ge(n_T_kept, l * NT + t + 1)
                for k in range(KD):
                    last = mm(PL[:, t * NR:(t + 1) * NR], hTt[t % 2][:, k, :], r_w[l][:, k, :],
                              start=k == 0, stop=k == KD - 1)
                last.then_inc(logit_done, 1)

            pe.wait_ge(in_loaded["v"], 16)
            pe.wait_ge(z_kept, 2 * KA)
            for k in range(NT + 5):
                if k < NT:
                    if k >= 2:
                        pe.wait_ge(v_ready, k - 1)
                    for q in range(KD):
                        last = mm(BANK[k % 2], hT[:, q, k * P:(k + 1) * P], in_w["v"][:, q, :],
                                  start=q == 0, stop=q == KD - 1)
                    last.then_inc(v_done, 1)
                if 0 <= k - 1 < NT:
                    t = k - 1
                    pe.wait_ge(v_ready, t + 1)
                    if t == 0:
                        pe.wait_ge(ws_masked, 1)
                        pe.wait_ge(mod_ready, 1)
                    else:
                        pe.wait_ge(ya_ready, t)
                    for h in range(HEADS):
                        q = (h % 2) * HD
                        last = mm(PM[q:q + HD, (h // 2) * P:(h // 2 + 1) * P], v_n[t % 2][:, h * HD:(h + 1) * HD],
                                  wsT[:, h, :], start=True, stop=True)
                    last.then_inc(sgu_done, 1)
                if 0 <= k - 2 < NT:
                    t = k - 2
                    pe.wait_ge(ya_ready, t + 1)
                    if t == 0:
                        pe.wait_ge(conv_done, 1)
                        pe.wait_ge(out_w_loaded, 16)
                    else:
                        pe.wait_ge(x_mixed, t)
                    for half in range(2):
                        for q in range(KD):
                            part = yaT[:, q, t * P:(t + 1) * P] if q < KA else ybT[:, q - KA, t * P:(t + 1) * P]
                            last = mm(BANK[2 + half], part, out_w[:, q, half * CH:(half + 1) * CH],
                                      start=q == 0, stop=q == KD - 1)
                    last.then_inc(mixed_done, 1)
                if k == 4:
                    pe.wait_ge(const_loaded, 16 * 4 * LAYERS)
                    pe.wait_ge(ws_kept, 1)
                if 0 <= k - 4 < NT:
                    entry_T(0, k - 4)
                if 0 <= k - 5:
                    entry_logits(0, k - 5)

            def block_T(n, s, loaded):
                pe.wait_ge(xg_loaded[s], loaded)
                pe.wait_ge(xT_ready, n) if not isinstance(n, int) or n > 0 else None
                rows_to_columns(PT, xg[s]).then_inc(b_T, 1)

            def gate_up(s):
                for q in range(KD):
                    lg = mm(BANK[0], xT[s][:, q, :], gate_w[s][:, q, :], start=q == 0, stop=q == KD - 1)
                yield lg
                for q in range(KD):
                    lu = mm(BANK[1], xT[s][:, q, :], up_w[s][:, q, :], start=q == 0, stop=q == KD - 1)
                yield lu

            def act_transpose():
                for q in range(KF):
                    last = nc.tensor.transpose(PM[:, q * P:(q + 1) * P], act_r[:, q * P:(q + 1) * P], ident[:, :])
                return last

            def down(s):
                for half in range(2):
                    part = slice(half * CH, (half + 1) * CH)
                    for q in range(KF):
                        mm(BANK[2 + half], aT_hi[:, q, :], down_hi[:, q, part], start=q == 0, stop=False)
                        mm(BANK[2 + half], aT_hi[:, q, :], down_lo[s][:, q, part], start=False, stop=False)
                        last = mm(BANK[2 + half], aT_lo[:, q, :], down_hi[:, q, part], start=False, stop=q == KF - 1)
                return last

            def down_block(n, s):
                pe.wait_ge(lo_ready, n + 1)
                pe.wait_ge(aT_ready, n + 1)
                if not (isinstance(n, int) and n == 0):
                    pe.wait_ge(y_ready, n)
                down(s).then_inc(y_done, 1)

            def pe_block(n, s, loaded, next_loaded, first=False, last=False):
                pe.wait_ge(xT_ready, n + 1)
                pe.wait_ge(gate_loaded[s], loaded)
                if not (isinstance(n, int) and n == 0):
                    pe.wait_ge(act_ready, n)
                parts = gate_up(s)
                next(parts).then_inc(g_done, 1)
                pe.wait_ge(up_loaded[s], loaded)
                next(parts).then_inc(u_done, 1)
                if not last:
                    block_T(n + 1, 1 - s, next_loaded)
                if not first:
                    down_block(n - 1, 1 - s)
                pe.wait_ge(act_ready, n + 1)
                act_transpose().then_inc(act_T, 1)

            def moe(l):
                pe.wait_ge(hots_ready, l + 1)
                if l == 0:
                    pe.wait_ge(ya_ready, NT)
                flat = hots[:, :, :].rearrange("p t e -> p (t e)")
                bflat = before[:, :, :].rearrange("p t e -> p (t e)")
                mm(PM[:, 0:NT * NE], lower[:, :], flat, start=True, stop=False)
                mm(PM[:, 0:NT * NE], ones[:, :], bflat[:, 0:NT * NE], start=False, stop=True)
                mm(PM[:, NT * NE:(NT + 1) * NE], ones[:, :], bflat[:, NT * NE:(NT + 1) * NE],
                   start=True, stop=True).then_inc(rank_done, 1)
                n0, c0 = l * NE, 16 * (NE // 2) * l
                pe.wait_ge(n_T_kept, (l + 1) * NT)
                pe.wait_ge(entries_ready, l + 1)
                for q in range(2 * NT):
                    last = mm(PL[:, 0:2 * NBLK], row_hot[:, q, :],
                              blk_val[:, q, :, :].rearrange("p i b -> p (i b)"), start=q == 0, stop=q == 2 * NT - 1)
                last.then_inc(table_summed, 1)
                block_T(n0, 0, c0 + 16)
                def one(e, i=None):
                    n, past = (n0 + e, c0) if i is None else (2 * i + (n0 + e), 16 * i + c0)
                    pe_block(n, e % 2, past + 16 * (e // 2 + 1), past + 16 * ((e + 1) // 2 + 1),
                             first=e == 0, last=e == NE - 1)

                for e in range(HEAD):
                    one(e)
                with pe.Fori(0, PAIRS) as i:
                    for e in PAIR:
                        one(e, i)
                for e in range(NE - TAIL, NE):
                    one(e)
                down_block(n0 + NE - 1, (NE - 1) % 2)
                m = more[l]
                pe.wait_ge(extra_ready, l + 1)
                count = pe.value_load(extra[l][0:1, XB + 1:XB + 2], min_val=0, max_val=XB)
                with pe.If(count > 0):
                    with pe.Fori(0, XB) as j:
                        with pe.If(j < count):
                            pe.wait_ge(m["xg"], 16 * j + 16)
                            rows_to_columns(PT, xg[1]).then_inc(m["T"], 1)
                            pe.wait_ge(m["xT"], j + 1)
                            pe.wait_ge(m["w"], 48 * j + 48)
                            parts = gate_up(1)
                            next(parts)
                            next(parts).then_inc(m["gu"], 1)
                            pe.wait_ge(m["dve"], 3 * j + 1)
                            act_transpose().then_inc(m["aT_ps"], 1)
                            pe.wait_ge(m["dve"], 3 * j + 3)
                            down(1).then_inc(m["y"], 1)
                            pe.wait_ge(m["y"], j + 1)
                nc.tensor.sem_inc(more_done, 1)

            moe(0)
            pe.wait_ge(bands_ready, 1)
            pe.wait_ge(pool_loaded, 16)
            for k in range(NT + 4):
                if 0 <= k - 1 < NT:
                    t = k - 1
                    pe.wait_ge(h_ready, t + 1)
                    if t:
                        pe.wait_ge(pool_kept, t)
                    for q in range(KD):
                        g = q // 2
                        part = PA[0][:, q * P:(q + 1) * P]
                        last = mm(part, h_r[t % 2][:, q * P:(q + 1) * P], (band if t else band0)[:, g, :],
                                  start=True, stop=t == 0)
                        if t:
                            last = mm(part[:, 0:REACH], h_r[1 - t % 2][:, q * P:(q + 1) * P], band_prev[:, g, :],
                                      start=False, stop=True)
                    last.then_inc(pool_T, 1)
                    pe.wait_ge(pool_kept, t + 1)
                    if t:
                        pe.wait_ge(x_mixed1, t)
                    for g in range(PG):
                        for q in range(2):
                            last = mm(PA[1][:, g * PD:(g + 1) * PD], pooledT[:, 2 * g + q, :], pool_w[:, g, q, :],
                                      start=q == 0, stop=q == 1)
                    last.then_inc(mixed1_done, 1)
                if 0 <= k - 3 < NT:
                    entry_T(1, k - 3)
                if 0 <= k - 4:
                    entry_logits(1, k - 4)
            moe(1)


_INS = ["x", "c", "w_ada", "b_ada", "norm_mix_g", "norm_ffn_g", "w_in_even", "sgu_norm_g", "w_spatial",
        "b_spatial", "conv_w", "w_out_even", "w_pool", "pool_scale", "w_group_router", "b_group_router",
        "w_expert_router", "b_expert_router", "moe_w_gate", "moe_w_up", "moe_w_down", "final_norm_g"]


def kernel(**inputs):
    import numpy as _np
    import concourse.bacc as _bacc
    from concourse import mybir as _mybir
    from concourse.bass_utils import run_bass_kernel_spmd as _run

    nc = _bacc.Bacc("TRN2", target_bir_lowering=False, num_devices=1)
    arrays, args = {}, []
    for name in _INS:
        a = _np.ascontiguousarray(inputs[name])
        arrays[f"in_{name}_dram"] = a
        args.append(nc.dram_tensor(f"in_{name}_dram", a.shape, _mybir.dt.from_np(a.dtype), kind="ExternalInput").ap())
    shape = tuple(inputs["x"].shape)
    args.append(nc.dram_tensor("out_0_dram", shape, _mybir.dt.from_np(_np.dtype("float32")), kind="ExternalOutput").ap())
    hybrid_trunk(nc, *args)
    r = _run(nc, [arrays], core_ids=[0])
    return r.results[0]["out_0_dram"]
```

```python
import concourse.bass as bass
from concourse import mybir
from contextlib import ExitStack


class Chain:

    def __init__(self, engine, sem):
        self.engine, self.sem, self.count, self.index = engine, sem, 0, None

    def value(self):
        return self.count if self.index is None else self.index * self.per + self.count

    def link(self, ins):
        self.count += 1
        ins.then_inc(self.sem, 1)
        self.engine.wait_ge(self.sem, self.value())

    def enter(self, index, per):
        self.index, self.per, self.start = index, per, self.count

    def leave(self, trips):
        assert self.count - self.start == self.per, (self.count - self.start, self.per)
        self.count, self.index = self.start + trips * self.per, None


def hybrid_trunk(nc, x, c, w_ada, b_ada, norm_mix_g, norm_ffn_g, w_in_even, sgu_norm_g, w_spatial,
                 b_spatial, conv_w, w_out_even, w_pool, pool_scale, w_group_router, b_group_router,
                 w_expert_router, b_expert_router, moe_w_gate, moe_w_up, moe_w_down, final_norm_g, out):
    F32, I32, U32, F32R = mybir.dt.float32, mybir.dt.int32, mybir.dt.uint32, mybir.dt.float32r
    ALU, ACT, AX = mybir.AluOpType, mybir.ActivationFunctionType, mybir.AxisListType
    ds = bass.ds

    P = 128
    S, D = x.shape[1], x.shape[2]
    NT, KD = S // P, D // P
    LAYERS = w_ada.shape[0]
    A = D // 2
    KA = A // P
    HEADS = w_spatial.shape[1]
    HD = A // HEADS
    NG, NE = w_group_router.shape[2], w_expert_router.shape[2]
    EG = NE // NG
    FE = moe_w_gate.shape[3]
    KF = FE // P
    NR = NG + NE
    PG = w_pool.shape[1]
    PD = D // PG
    WINDOWS = (2, 4, 8, 16)
    REACH = max(WINDOWS)
    EPS = 1e-6
    ASSIGN = 2 * S
    XB = ASSIGN // P - 1
    NBLK = NE + XB + 1
    PAD = 4096
    TOKEN_MASK = PAD | (S - 1)
    CH = 512
    assert NT == KD == 8 and LAYERS == 2 and P == w_spatial.shape[2] and CH == FE == A
    NMOD = 6
    SH_M, SC_M, G_M, SH_F, SC_F, G_F = range(NMOD)
    HEAD, TAIL = 3, 3
    PAIRS = (NE - HEAD - TAIL) // 2
    PAIR = (HEAD, HEAD + 1)

    xv = x[0].rearrange("(t p) d -> p t d", p=P)
    outv = out[0].rearrange("(t p) d -> p t d", p=P)

    xn_dram = [nc.dram_tensor(f"normed_rows{l}", [S, D], F32, kind="Internal").ap() for l in range(LAYERS)]
    y_dram = [nc.dram_tensor(f"expert_rows{l}", [ASSIGN, D], F32, kind="Internal").ap() for l in range(LAYERS)]
    mod1_dram = nc.dram_tensor("mod_rows1", [NMOD, D], F32, kind="Internal").ap()

    ctx = ExitStack()
    with ctx:
        KB = 1024
        base = (nc.sbuf_base + 31) // 32 * 32
        X0 = base
        W0 = X0 + 32 * KB
        Z0 = W0 + 96 * KB
        H0 = Z0 + 16 * KB
        G0 = H0 + 32 * KB
        T0 = G0 + 8 * KB
        C0 = T0 + 16 * KB + 256
        END = nc.sbuf_top
        cursor = [C0]

        def at(name, shape, off, dt=F32):
            return nc.alloc_sbuf_tensor_at(name, shape, dt, offset=off)

        def small(name, shape, dt=F32):
            n = 4
            for s in shape[1:]:
                n *= s
            off = cursor[0]
            cursor[0] = (off + n + 31) // 32 * 32
            assert cursor[0] <= END, (name, cursor[0], END)
            return at(name, shape, off, dt)

        xr = at("x_rows", [P, NT, D], X0)
        SLOT = 16 * KB
        SA, SB_, SC, SD, SE, SF = [W0 + i * SLOT for i in range(6)]
        gate_w = [at(f"gate_w{s}", [P, KD, FE], o) for s, o in enumerate((SD, SA))]
        up_w = [at(f"up_w{s}", [P, KD, FE], o) for s, o in enumerate((SE, SB_))]
        down_w = [at(f"down_w{s}", [P, KF, D], o) for s, o in enumerate((SF, SC))]
        acc0 = at("cond_acc0", [P, 2 * D], SF)
        cond0 = [at(f"cond0_w{q}", [P, 2, D], SD + q * 8 * KB) for q in range(4)]
        acc = [at(f"cond_acc{q}", [P, D], X0 + 4 * q * KB) for q in range(2)]
        bias = [at(f"cond_bias{q}", [P, D], X0 + (8 + 4 * q) * KB) for q in range(2)]
        UNITS = 4
        cond = [at(f"cond_w{q}", [P, D], X0 + (16 + 4 * q) * KB) for q in range(UNITS)]
        row_kept = at("mod_row", [1, D], T0 + 4 * KB)
        PARTS = [(0, m) for m in range(2, NMOD)] + [(1, m) for m in range(NMOD)]
        N0 = NMOD - 2

        def as_columns(l, m):
            return m in (SH_F, SC_F)

        PART_BEHIND = {4 + 9 * n // 4: n for n in range(len(PARTS))}
        ROWS_BEFORE = [sum(not as_columns(*q) for q in PARTS[:n]) for n in range(len(PARTS) + 1)]
        hT = at("h_columns", [P, KD, S], H0)
        h_lo = at("h_columns_low", [P, KD, S], H0, F32R)
        h_hi = at("h_columns_high", [P, KD, S], SA, F32R)
        RING, HRING = 4, 2
        HI0 = SF + 8 * KB
        piece = [at(f"in_w{q}", [P, KD, P], SC + 4 * q * KB) for q in range(RING)]
        piece_lo = [at(f"in_w_low{q}", [P, KD, P], SC + 4 * q * KB, F32R) for q in range(RING)]
        piece_hi = [at(f"in_w_high{q}", [P, KD, P], HI0 + 4 * q * KB, F32R) for q in range(HRING)]
        PIECES = 4 * KA
        v_w = at("v_w", [P, KD, A], X0)
        v_lo = at("v_w_low", [P, KD, A], X0, F32R)
        v_hi = at("v_w_high", [P, KD, A], X0 + 16 * KB, F32R)
        zT = at("conv_in", [P, KA, S], Z0)
        yaT = at("mix_a", [P, KA, S], SD + 8 * KB)
        ybT = at("mix_b", [P, KA, S], SE + 8 * KB)
        out_parts = [at("out_w0", [P, 4, D], SC), at("out_w4", [P, 2, D], HI0),
                     at("out_w6", [P, 1, D], SD + 4 * KB), at("out_w7", [P, 1, D], T0)]
        out_w = [part[:, q, :] for part, n in zip(out_parts, (4, 2, 1, 1)) for q in range(n)]
        low_parts = [at(f"out_w_low{i}", [P, n, D], o, F32R)
                     for i, (n, o) in enumerate(((4, SC), (2, HI0), (1, SD + 4 * KB), (1, T0)))]
        out_lo = [part[:, q, :] for part, n in zip(low_parts, (4, 2, 1, 1)) for q in range(n)]
        out_hi = at("out_w_high", [P, KD, D], SA, F32R)
        y_hi = [at(f"mix_high{i}", [P, KD, P], H0 + (8 + 4 * i) * KB, F32R) for i in range(2)]
        y_lo = [at(f"mix_low{i}", [P, KD, P], H0 + (16 + 4 * i) * KB, F32R) for i in range(2)]
        LOW_BY_DVE, LOW_BY_POOL = (0, 2, 4, 5, 6), (1, 3, 7)
        ws_raw = at("spatial_w", [P, HEADS, P], T0 + 12 * KB)
        wsT = at("spatial_wT", [P, HEADS, P], Z0)
        bsp = at("spatial_bias", [P, KA, P], SD)
        gv = at("sgu_gain", [P, A], SD + 2 * KB)
        conv_t = at("conv_out", [P, S], T0)
        v_sq = at("v_squares", [P, A], T0 + 4 * KB)
        v_n = [at(f"v_normed{s}", [P, A], T0 + (6 + 2 * s) * KB) for s in range(2)]
        gated = at("gate_tmp", [P, KA * P], T0 + 10 * KB)
        res_t = at("residual_tmp", [P, D], T0 + 12 * KB)
        a1b = at("scale_row1", [P, D], H0)
        b1b = at("shift_row1", [P, D], H0 + 8 * KB)
        YB = 4
        y_in = [at("y_in0", [P, 2, 2, D], H0)[:, :, 1, :]]
        y_in += [at(f"y_in{s}", [P, 2, D], o)[:, :, :] for s, o in enumerate((H0 + 16 * KB, SC, SC + 8 * KB), 1)]
        h_r = [at(f"h_rows{s}", [P, D], H0 + (24 + 4 * s) * KB) for s in range(2)]
        pool_w = at("pool_w", [P, PG, 2, PD], T0)
        pooledT = at("pooled_columns", [P, KD, P], T0 + 8 * KB)
        factor = at("row_factor", [P, D], T0 + 8 * KB)
        band = at("band", [P, PG, P], T0 + 12 * KB)
        band0 = at("band_first", [P, PG, P], T0 + 14 * KB)
        band_prev = at("band_previous", [P, PG, REACH], T0 + 16 * KB)
        xn = [at(f"xn{s}", [P, D], Z0 + 4 * KB * s) for s in range(2)]
        hTt = [at(f"h_tile_columns{s}", [P, KD, P], Z0 + (8 + 4 * s) * KB) for s in range(2)]
        xg = [at(f"gathered{s}", [P, D], H0 + 4 * KB * s) for s in range(2)]
        xT = [at(f"block_columns{s}", [P, KD, P], H0 + (8 + 4 * s) * KB) for s in range(2)]
        y_o = [at(f"y_out{s}", [P, D], H0 + (16 + 4 * s) * KB) for s in range(2)]
        aT_hi = at("act_columns_high", [P, KF, P], H0 + 24 * KB, F32R)
        aT_lo = at("act_columns_low", [P, KF, P], H0 + 26 * KB, F32R)
        down_hi = at("down_w_high", [P, KF, D], Z0, F32R)
        down_hi_last = at("down_w_high_last", [P, KF, D], SD, F32R)
        down_lo = [at(f"down_w_low{s}", [P, KF, D], o, F32R) for s, o in enumerate((SF, SC))]
        act_r = at("act_rows", [P, FE], H0 + 28 * KB)
        sig = at("sigmoid_tmp", [P, FE], H0 + 30 * KB)
        grow = [at(f"gain_row{s}", [P, D], G0 + 4 * KB * s) for s in range(2)]

        rcur = [Z0]

        def routing(name, shape, dt=F32):
            n = 4
            for s in shape[1:]:
                n *= s
            off = rcur[0]
            rcur[0] = (off + n + 31) // 32 * 32
            assert rcur[0] <= H0, name
            return at(name, shape, off, dt)

        g_diff = routing("g_diff", [P, NT, NG])
        g_exp = routing("g_exp", [P, NT, NG])
        g_key = routing("g_key", [P, NT, NG])
        g_hot = routing("g_hot", [P, NT, NG])
        g_w = routing("g_weight", [P, NT])
        e_prod = routing("e_prod", [P, NT, NG, EG])
        e_sel = routing("e_sel", [P, NT, EG])
        e_diff = routing("e_diff", [P, NT, EG])
        e_key = routing("e_key", [P, NT, EG])
        e_hot = [routing(f"e_hot{i}", [P, NT, EG]) for i in range(2)]
        r_m = [routing(f"r_max{i}", [P, NT]) for i in range(4)]
        r_e = routing("r_exp", [P, NT])
        r_r = routing("r_recip", [P, NT])
        hot = [routing(f"hot{i}", [P, NT, NE]) for i in range(2)]
        hots = routing("hots", [P, NT, NE])
        before = routing("tiles_before", [P, NT + 1, NE])
        s_tmp = routing("slot_tmp", [P, NT, NE])
        cnt_i = routing("cnt_int", [P, NE], I32)
        nblk = routing("more_blocks", [P, NE])
        bend = routing("blocks_end", [P, NE])
        b_off = routing("block_offset", [P, NE])
        kg_hot = routing("rank_of_group", [P, NT])
        ke_hot = [routing(f"rank_of_expert{i}", [P, NT]) for i in range(2)]
        a_pos = routing("a_position", [P, NT, 2])
        a_posi = routing("a_position_int", [P, NT, 2], I32)
        a_quo = routing("a_quotient", [P, NT, 2])
        a_row = routing("a_row", [P, NT, 2])
        a_exp = routing("a_expert", [P, NT, 2])
        a_blk = routing("a_block", [P, NT, 2])
        gates = routing("gates", [P, NT, 2])
        empty = routing("empty", [P, NBLK])
        asg_f = routing("assignment_float", [P, NBLK])
        row_hot = at("row_hot", [P, 2 * NT, P], H0 + 8 * KB)
        blk_hot = at("block_hot", [P, 2 * NT, NBLK], H0 + 16 * KB)
        blk_val = at("block_values", [P, 2 * NT, 2, NBLK], H0 + 19 * KB)

        ident = small("ident", [P, P])
        ones = small("ones", [P, P])
        lower = small("strictly_before", [P, P])
        vec_rows = at("vector_rows", [P, P], T0)
        vec = small("vector_columns", [P, 64])
        c_e = small("c_exp", [P, KD])
        c_act = small("c_act", [P, KD])
        mod = [small(f"mod_columns{l}", [P, NMOD, KD]) for l in range(LAYERS)]
        a_m = small("a_mix", [P, KD])
        a_f = [small(f"a_ffn{l}", [P, KD]) for l in range(LAYERS)]
        r_w = [small(f"router_w{l}", [P, KD, NR]) for l in range(LAYERS)]
        r_b = [small(f"router_b{l}", [P, NR]) for l in range(LAYERS)]
        logits = routing("logits", [P, NT, NR])
        rank_g = small("rank_g", [P, NG])
        rank_e = small("rank_e", [P, EG])
        e_id = small("expert_ids", [P, NE])
        j_id = small("block_ids", [P, XB + 1])
        eps = small("eps", [P, 1])
        X_IN, N_FFN0, N_MIX1, N_FFN1, N_FINAL = range(5)
        ss = small("sum_squares", [P, 5, NT])
        sd = small("root_mean_square", [P, 5, NT])
        rstd = small("rstd", [P, 5, NT])
        vss = small("v_sum_squares", [P, HEADS])
        vsd = small("v_root_mean_square", [P, HEADS])
        vrs = small("v_rstd", [P, HEADS])
        row_id = small("row_ids", [P, P])
        number = small("assignment_numbers", [P, NT, 2])
        asg = small("assignment", [P, NBLK], U32)
        slot_gate = small("slot_gate", [P, NBLK])
        tok = small("token", [P, NBLK], U32)
        idx_g = [small(f"gather_index{s}", [P, 1], U32) for s in range(2)]
        idx_s = [small(f"scatter_index{s}", [P, 1], U32) for s in range(2)]
        gate_c = [small(f"block_gate{s}", [P, 1]) for s in range(2)]
        cmp_t = routing("block_compare", [1, XB + 1, NE])
        eid_f = routing("extra_expert_f", [1, XB + 2])
        extra = [small(f"extra_experts{l}", [1, XB + 2], I32) for l in range(LAYERS)]
        inv_count = small("inverse_counts", [P, REACH])
        vg_mix = [vec[:, l * KD:(l + 1) * KD] for l in range(LAYERS)]
        vg_ffn = [vec[:, (2 + l) * KD:(3 + l) * KD] for l in range(LAYERS)]
        vc = vec[:, 4 * KD:5 * KD]
        NVEC = 5 * KD + 3 * KA

        def conv_col(k, m):
            return vec[:, 5 * KD + k * KA + m:5 * KD + k * KA + m + 1]

        ps = ctx.enter_context(nc.psum_tensor("ps", [P, 8 * CH], F32))
        BANK = [ps[:, i * CH:(i + 1) * CH] for i in range(8)]
        PA = [ps[:, 0:D], ps[:, D:2 * D]]
        PT = ps[:, 4 * CH:6 * CH]
        PM = BANK[6]
        PL = BANK[7]

        def sem(name):
            return ctx.enter_context(nc.semaphore(name))

        vec_loaded, const_loaded = sem("vec_loaded"), sem("const_loaded")
        x_loaded = [sem(f"x_loaded{i}") for i in range(4)]
        bias_loaded = [sem(f"bias_loaded{q}") for q in range(2)]
        cond0_loaded = [sem(f"cond0_loaded{q}") for q in range(4)]
        cond_loaded = [sem(f"cond_loaded{q}") for q in range(UNITS)]
        piece_loaded = [sem(f"piece_loaded{q}") for q in range(RING)]
        v_loaded = sem("v_loaded")
        ws_loaded = sem("ws_loaded")
        sgu_loaded, out_w_loaded = sem("sgu_loaded"), sem("out_w_loaded")
        pool_loaded, rows1_loaded = sem("pool_loaded"), sem("rows1_loaded")
        final_loaded, gain1_loaded = sem("final_loaded"), sem("gain1_loaded")
        gate_loaded = [sem(f"gate_loaded{s}") for s in range(2)]
        up_loaded = [sem(f"up_loaded{s}") for s in range(2)]
        down_loaded = [sem(f"down_loaded{s}") for s in range(2)]
        consts = sem("consts")
        bands_ready = sem("bands_ready")
        dve_chain, act_chain, pool_chain = sem("dve_chain"), sem("act_chain"), sem("pool_chain")
        vec_T, vec_ready, c_exp_ready = sem("vec_T"), sem("vec_ready"), sem("c_exp_ready")
        acc_init = sem("acc_init")
        cond0_used, cond_used = sem("cond0_used"), sem("cond_used")
        acc0_ready, acc_ready, part_summed = sem("acc0_ready"), sem("acc_ready"), sem("part_summed")
        mod_cols0, mod_ready0, mod_ready = sem("mod_cols0"), sem("mod_ready0"), sem("mod_ready")
        row_out, row_stored = sem("row_out"), sem("row_stored")
        x_ss, x_rstd, x_normed = sem("x_ss"), sem("x_rstd"), sem("x_normed")
        x_T, x_T_kept = sem("x_T"), sem("x_T_kept")
        h_act, h_dve, h_pool = sem("h_act"), sem("h_dve"), sem("h_pool")
        w_high, w_low, out_low = sem("w_high"), sem("w_low"), sem("out_low")
        proj_done, proj_kept, z_kept = sem("proj_done"), sem("proj_kept"), sem("z_kept")
        conv_done = sem("conv_done")
        ws_T, ws_kept, ws_masked = sem("ws_T"), sem("ws_kept"), sem("ws_masked")
        v_done, v_sq_done, v_rs_half, v_ready = sem("v_done"), sem("v_sq_done"), sem("v_rs_half"), sem("v_ready")
        v_ms_ready = sem("v_ms_ready")
        sgu_done, ya_ready = sem("sgu_done"), sem("ya_ready")
        mixed_done, x_mixed = sem("mixed_done"), sem("x_mixed")
        n_ss, n_rstd, xn_ready = sem("n_ss"), sem("n_rstd"), sem("xn_ready")
        xn_stored = [sem(f"xn_stored{s}") for s in range(2)]
        n_T, n_T_kept, logit_done = sem("n_T"), sem("n_T_kept"), sem("logit_done")
        exp_in_ready, exp_ready = sem("exp_in_ready"), sem("exp_ready")
        hots_ready, rank_done, entries_ready = sem("hots_ready"), sem("rank_done"), sem("entries_ready")
        table_summed, extra_ready = sem("table_summed"), sem("extra_ready")
        idx_g_ready = sem("idx_g_ready")
        xg_loaded = [sem(f"xg_loaded{s}") for s in range(2)]
        y_stored = [sem(f"y_stored{s}") for s in range(2)]
        b_T, xT_ready = sem("b_T"), sem("xT_ready")
        g_done, u_done, sig_ready, act_ready = sem("g_done"), sem("u_done"), sem("sig_ready"), sem("act_ready")
        hi_ready, lo_ready, aT_hi_ready = sem("hi_ready"), sem("lo_ready"), sem("aT_hi_ready")
        act_T, aT_ready, y_done, y_ready = sem("act_T"), sem("aT_ready"), sem("y_done"), sem("y_ready")
        names = ("w", "idx", "xg", "T", "xT", "gu", "act", "aT_ps", "dve", "y", "yr", "stored", "free", "chain")
        more = [{n: sem(f"more{l}_{n}") for n in names} for l in range(LAYERS)]
        transfers = sem("transfers")
        moe_done, more_done = sem("moe_done"), sem("more_done")
        y_in_loaded = [sem(f"y_in_loaded{s}") for s in range(4)]
        combined, c_ss = sem("combined"), sem("c_ss")
        h_ready, pool_T, pool_kept = sem("h_ready"), sem("pool_T"), sem("pool_kept")
        mixed1_done, x_mixed1 = sem("mixed1_done"), sem("x_mixed1")
        out_ready, out_stored = sem("out_ready"), sem("out_stored")

        block = ctx.enter_context(nc.Block())

        def bc(ap, shape):
            return ap.to_broadcast(shape)

        def h_made(k):
            return k + (k + 1) // 2 + 1

        inv = w_in_even[0].rearrange("(k p) n -> p k n", p=P)
        col = {"u": 0, "v": 1, "b": 2, "c": 3, "x": 4}

        def out_high(q):
            return PIECES + 3 + q

        def mix_high(t):
            return PIECES + 2 + (KD + t if t else 0)

        def mix_low(t):
            return PIECES + 2 + (len(LOW_BY_POOL) + t if t else 0)

        def mix_tile(part, t):
            return (yaT if part == 0 else ybT)[:, :, t * P:(t + 1) * P]

        def load_piece(queue, w):
            at_col = col["cbux"[w // KA]] * A + w % KA * P
            queue.dma_start(piece[w % RING][:, :, :], inv[:, :, at_col:at_col + P])\
                 .then_inc(piece_loaded[w % RING], 16)

        @block.sync
        def _(sp):
            for l in range(LAYERS):
                sp.dma_start(vec_rows[l * KD:(l + 1) * KD, :],
                             norm_mix_g[l].rearrange("(m p) -> m p", p=P)).then_inc(vec_loaded, 16)
                sp.dma_start(vec_rows[(2 + l) * KD:(3 + l) * KD, :],
                             norm_ffn_g[l].rearrange("(m p) -> m p", p=P)).then_inc(vec_loaded, 16)
            sp.dma_start(vec_rows[4 * KD:5 * KD, :], c[0].rearrange("(m p) -> m p", p=P)).then_inc(vec_loaded, 16)
            sp.dma_start(vec_rows[5 * KD:NVEC, :],
                         conv_w[0].rearrange("k (m p) -> (k m) p", p=P)).then_inc(vec_loaded, 16)
            for i in range(4):
                sp.dma_start(xr[:, 2 * i:2 * i + 2, :], xv[:, 2 * i:2 * i + 2, :]).then_inc(x_loaded[i], 16)
            sp.wait_ge(acc_init, 1)
            sp.dma_start(acc0[0:1, :], b_ada[0:1, 0:2 * D]).then_inc(cond0_loaded[0], 16)
            ada0 = w_ada[0].rearrange("(k p) n -> p k n", p=P)
            for q in range(4):
                sp.dma_start(cond0[q][:, :, :], ada0[:, 2 * q:2 * q + 2, 0:D]).then_inc(cond0_loaded[q], 16)
            for q in range(4):
                sp.wait_ge(cond0_used, q + 1)
                sp.dma_start(cond0[q][:, :, :], ada0[:, 2 * q:2 * q + 2, D:2 * D]).then_inc(cond0_loaded[q], 16)

            for w in range(RING):
                load_piece(sp, w)
            sp.dma_start(ws_raw[:, :, :], w_spatial[0].rearrange("h t s -> t h s")).then_inc(ws_loaded, 16)

            def part_loads(l, off, n, parity):
                if not isinstance(n, int) or n >= 2:
                    sp.wait_ge(cond_used, KD * n + (1 - 2 * KD))
                sp.dma_start(bias[parity][0:1, :], b_ada[l:l + 1, ds(off, D)]).then_inc(bias_loaded[parity], 16)
                for k in range(KD):
                    if not isinstance(n, int) or KD * n + k >= UNITS:
                        sp.wait_ge(cond_used, KD * n + (k - UNITS + 1))
                    sp.dma_start(cond[k % UNITS][:, :], w_ada[l].rearrange("(k p) n -> k p n", p=P)[k, :, ds(off, D)])\
                      .then_inc(cond_loaded[k % UNITS], 16)

            for l in range(LAYERS):
                sp.dma_start(r_w[l][:, :, 0:NG],
                             w_group_router[l].rearrange("(k p) n -> p k n", p=P)).then_inc(const_loaded, 16)
                sp.dma_start(r_w[l][:, :, NG:NR],
                             w_expert_router[l].rearrange("(k p) n -> p k n", p=P)).then_inc(const_loaded, 16)
                sp.dma_start(r_b[l][:, 0:NG], b_group_router[l].partition_broadcast(P)).then_inc(const_loaded, 16)
                sp.dma_start(r_b[l][:, NG:NR], b_expert_router[l].partition_broadcast(P)).then_inc(const_loaded, 16)
            sp.wait_ge(acc_init, 2)
            for n in range(N0):
                part_loads(0, (n + 2) * D, n, n % 2)
            with sp.Fori(0, NMOD // 2) as j:
                for q in range(2):
                    part_loads(1, j * (2 * D) + q * D, 2 * j + (N0 + q), q)
            sp.wait_ge(part_summed, len(PARTS))
            sp.dma_start(v_w[:, :, :], inv[:, :, col["v"] * A:(col["v"] + 1) * A]).then_inc(v_loaded, 16)
            sp.dma_start(gv[:, :], sgu_norm_g[0].partition_broadcast(P)).then_inc(sgu_loaded, 16)
            for h in range(HEADS):
                q = (h % 2) * HD
                sp.dma_start(bsp[q:q + HD, h // 2, :], b_spatial[0, h].partition_broadcast(HD))\
                  .then_inc(sgu_loaded, 16)
            sp.wait_ge(proj_done, 8 * KA)
            sp.wait_ge(conv_done, 1)
            ow = w_out_even[0].rearrange("(k p) n -> p k n", p=P)
            for part, q0, n in zip(out_parts, (0, 4, 6, 7), (4, 2, 1, 1)):
                sp.dma_start(part[:, :, :], ow[:, q0:q0 + n, :]).then_inc(out_w_loaded, 16)
            sp.wait_ge(v_done, NT)
            for i in range(4):
                sp.dma_start(xr[:, 2 * i:2 * i + 2, :], xv[:, 2 * i:2 * i + 2, :]).then_inc(x_loaded[i], 16)

            def load_down(l, e, s):
                sp.dma_start(down_w[s][:, :, :], moe_w_down[l, ds(e, 1)].rearrange("o (k p) d -> p (o k) d", p=P))\
                  .then_inc(down_loaded[s], 16)

            def load_gate(l, e, s):
                sp.dma_start(gate_w[s][:, :, :], moe_w_gate[l, ds(e, 1)].rearrange("o (k p) f -> p (o k) f", p=P))\
                  .then_inc(gate_loaded[s], 16)

            def load_up(l, e, s):
                sp.dma_start(up_w[s][:, :, :], moe_w_up[l, ds(e, 1)].rearrange("o (k p) f -> p (o k) f", p=P))\
                  .then_inc(up_loaded[s], 16)

            def load_expert(l, e, s, n):
                sp.wait_ge(g_done, n - 1)
                load_gate(l, e, s)
                sp.wait_ge(u_done, n - 1)
                load_up(l, e, s)
                sp.wait_ge(y_done, n - 1)
                load_down(l, e, s)

            def load_y(l, t):
                if t >= YB:
                    if l == 0:
                        sp.wait_ge(x_mixed1, t - YB + 1)
                    else:
                        sp.wait_ge(c_ss, NT + t - YB + 1)
                sp.dma_start(y_in[t % YB],
                             y_dram[l].rearrange("(i t p) d -> t p i d", i=2, p=P)[t]).then_inc(y_in_loaded[t % YB], 16)

            def experts(l):
                with sp.Fori(0, NE // 2 - 1) as i:
                    load_expert(l, 2 * i + 2, 0, 2 * i + (l * NE + 2))
                    load_expert(l, 2 * i + 3, 1, 2 * i + (l * NE + 3))
                if l == 0:
                    sp.wait_ge(u_done, NE - 1)
                    load_up(1, 0, 0)
                    sp.wait_ge(y_done, NE - 1)
                    load_down(1, 0, 0)
                    for dst, src in ((a1b, mod1_dram[SC_M]), (factor, norm_mix_g[1]), (b1b, mod1_dram[SH_M])):
                        sp.dma_start(dst[:, :], src.partition_broadcast(P)).then_inc(rows1_loaded, 16)
                m = more[l]
                sp.wait_ge(extra_ready, l + 1)
                count = sp.value_load(extra[l][0:1, XB + 1:XB + 2], min_val=0, max_val=XB)
                with sp.If(count > 0):
                    with sp.Fori(0, XB) as j:
                        with sp.If(j < count):
                            sp.wait_ge(m["free"], j + 1)
                            e = sp.value_load(extra[l][0:1, ds(j, 1)], min_val=0, max_val=NE - 1)
                            for dst, src in ((gate_w, moe_w_gate), (up_w, moe_w_up), (down_w, moe_w_down)):
                                sp.dma_start(dst[1][:, :, :], src[l, ds(e, 1)].rearrange("o (k p) f -> p (o k) f", p=P))\
                                  .then_inc(m["w"], 16)

            for t in range(NT):
                sp.wait_ge(xn_ready, t + 1)
                sp.dma_start(xn_dram[0][t * P:(t + 1) * P, :], xn[t % 2][:, :]).then_inc(xn_stored[t % 2], 16)
            sp.wait_ge(mixed_done, NT)
            sp.wait_ge(ya_ready, NT)
            for e in range(2):
                load_gate(0, e, e)
                load_up(0, e, e)
                load_down(0, e, e)
            sp.wait_ge(x_mixed, NT)
            sp.dma_start(pool_w[:, :, :, :], w_pool[0].rearrange("g (k p) n -> p g k n", p=P)).then_inc(pool_loaded, 16)
            sp.wait_ge(row_stored, 16 * 4)
            for dst, src in ((grow[0], mod1_dram[G_M]), (factor, pool_scale[0])):
                sp.dma_start(dst[:, :], src.partition_broadcast(P)).then_inc(rows1_loaded, 16)
            experts(0)

            sp.wait_ge(moe_done, 1)
            for t in range(NT):
                load_y(0, t)
                if t == YB - 1:
                    sp.wait_ge(more_done, 1)
                    load_gate(1, 0, 0)
                    load_gate(1, 1, 1)
                    load_up(1, 1, 1)
                    sp.dma_start(grow[1][:, :], mod1_dram[G_F].partition_broadcast(P)).then_inc(gain1_loaded, 16)
            sp.wait_ge(x_mixed1, NT)
            load_down(1, 1, 1)
            sp.dma_start(grow[0][:, :], final_norm_g.partition_broadcast(P)).then_inc(final_loaded, 16)
            experts(1)

            sp.wait_ge(moe_done, 2)
            for t in range(NT):
                load_y(1, t)
            sp.wait_ge(out_stored, 16 * NT)

        @block.gpsimd
        def _(pool):
            g = nc.gpsimd
            made = [0]
            last_token, last_assignment = pool.to_reg(S - 1), pool.to_reg(ASSIGN - 1)

            def note(ins, chain=pool_chain):
                made[0] += 1
                ins.then_inc(chain, 1)

            def settle():
                pool.wait_ge(pool_chain, made[0])

            g.memset(acc0[:, :], 0.0).then_inc(acc_init, 1)
            note(g.memset(ident[:, :], 0.0))
            note(g.memset(ones[:, :], 1.0))
            note(g.memset(lower[:, :], 1.0))
            note(g.memset(eps[:, :], EPS))
            note(g.iota(rank_g[:, :], [[-1, NG]], base=NG, channel_multiplier=0, allow_small_or_imprecise_dtypes=True))
            note(g.iota(rank_e[:, :], [[-1, EG]], base=EG, channel_multiplier=0, allow_small_or_imprecise_dtypes=True))
            note(g.iota(e_id[:, :], [[1, NE]], base=0, channel_multiplier=0, allow_small_or_imprecise_dtypes=True))
            note(g.iota(j_id[:, :], [[1, XB + 1]], base=0, channel_multiplier=0, allow_small_or_imprecise_dtypes=True))
            note(g.iota(inv_count[:, :], [[1, REACH]], base=1, channel_multiplier=0, allow_small_or_imprecise_dtypes=True))
            note(g.iota(number[:, :, :], [[P, NT], [S, 2]], base=1, channel_multiplier=1,
                        allow_small_or_imprecise_dtypes=True))
            note(g.iota(row_id[:, :], [[1, P]], base=0, channel_multiplier=0, allow_small_or_imprecise_dtypes=True))
            settle()
            note(g.affine_select(out=ident[:, :], in_=ident[:, :], compare_op=ALU.not_equal, fill=1.0,
                                 base=0, pattern=[[-1, P]], channel_multiplier=1))
            note(g.affine_select(out=lower[:, :], in_=lower[:, :], compare_op=ALU.is_ge, fill=0.0,
                                 base=-1, pattern=[[1, P]], channel_multiplier=-1))
            settle()
            g.sem_inc(consts, 1)
            pool.wait_ge(x_T, NT)
            for q in range(2):
                note(g.memset(bias[q][:, :], 0.0))
            settle()
            g.sem_inc(acc_init, 1)

            def piece_low(w):
                pool.wait_ge(w_high, w + 1)
                g.tensor_tensor(piece_lo[w % RING][:, :, :], piece[w % RING][:, :, :],
                                piece_hi[w % HRING][:, :, :].bitcast(F32), ALU.subtract).then_inc(w_low, 1)

            piece_low(0)
            for k in range(1, KD, 2):
                pool.wait_ge(h_dve, h_made(k))
                g.tensor_tensor(h_lo[:, k, :], hT[:, k, :], h_hi[:, k, :].bitcast(F32), ALU.subtract).then_inc(h_pool, 1)
            for w in range(1, PIECES):
                piece_low(w)
            pool.wait_ge(w_high, PIECES + 1)
            g.tensor_tensor(v_lo[:, :, :], v_w[:, :, :], v_hi[:, :, :].bitcast(F32), ALU.subtract).then_inc(w_low, 1)
            pool.wait_ge(ws_kept, 1)
            g.affine_select(out=wsT[:, :, :], in_=wsT[:, :, :], compare_op=ALU.is_ge, fill=0.0, base=0,
                            pattern=[[0, HEADS], [1, P]], channel_multiplier=-1).then_inc(ws_masked, 1)
            def clear_gathered():
                for s in range(2):
                    note(g.memset(xg[s][:, :], 0.0))
                settle()

            def tile_low(t):
                pool.wait_ge(w_high, mix_high(t))
                for part in range(2):
                    half = slice(part * KA, (part + 1) * KA)
                    last = g.tensor_tensor(y_lo[t % 2][:, half, :], mix_tile(part, t),
                                           y_hi[t % 2][:, half, :].bitcast(F32), ALU.subtract)
                last.then_inc(w_low, 1)

            tile_low(0)
            for q in LOW_BY_POOL:
                pool.wait_ge(w_high, out_high(q))
                g.tensor_tensor(out_lo[q], out_w[q], out_hi[:, q, :].bitcast(F32), ALU.subtract).then_inc(w_low, 1)
            for t in range(1, NT):
                tile_low(t)
            clear_gathered()

            def bands():
                pool.wait_ge(x_mixed, NT)
                for i, win in enumerate(WINDOWS):
                    note(g.memset(band[:, i, :], 1.0 / win))
                    note(g.memset(band_prev[:, i, :], 1.0 / win))
                settle()
                for i, win in enumerate(WINDOWS):
                    note(g.affine_select(out=band[:, i, :], in_=band[:, i, :], compare_op=ALU.is_ge, fill=0.0,
                                         base=0, pattern=[[1, P]], channel_multiplier=-1))
                    note(g.affine_select(out=band_prev[:, i, :], in_=band_prev[:, i, :], compare_op=ALU.is_ge,
                                         fill=0.0, base=win - 1 - P, pattern=[[-1, REACH]], channel_multiplier=1))
                settle()
                for i, win in enumerate(WINDOWS):
                    note(g.affine_select(out=band[:, i, :], in_=band[:, i, :], compare_op=ALU.is_ge, fill=0.0,
                                         base=win - 1, pattern=[[-1, P]], channel_multiplier=1))
                settle()
                note(g.tensor_copy(band0[:, :, :], band[:, :, :]))
                settle()
                for i, win in enumerate(WINDOWS):
                    note(g.tensor_scalar(band0[:, i, 0:win], band0[:, i, 0:win], float(win), None, ALU.mult))
                settle()
                for i, win in enumerate(WINDOWS):
                    note(g.tensor_tensor(band0[:, i, 0:win], band0[:, i, 0:win], inv_count[:, 0:win], ALU.mult))
                settle()
                for i in range(PG):
                    note(g.tensor_tensor(band[:, i, :], band[:, i, :], ident[:, :], ALU.subtract))
                    note(g.tensor_tensor(band0[:, i, :], band0[:, i, :], ident[:, :], ALU.subtract))
                settle()
                g.sem_inc(bands_ready, 1)

            def gather_rows(l, s, done):
                g.sem_inc(transfers, 1)
                g.indirect_dma_start(out=xg[s][:, :], out_offset=None, in_=xn_dram[l],
                                     in_offset=bass.IndirectOffsetOnAxis(ap=idx_g[s][:, 0:1], axis=0),
                                     bounds_check=last_token, oob_is_err=False).then_inc(done, 16)

            def scatter_rows(l, s, done):
                g.sem_inc(transfers, 1)
                g.indirect_dma_start(out=y_dram[l],
                                     out_offset=bass.IndirectOffsetOnAxis(ap=idx_s[s][:, 0:1], axis=0),
                                     in_=y_o[s][:, :], in_offset=None,
                                     bounds_check=last_assignment, oob_is_err=False).then_inc(done, 16)

            def gather(l, n, s, first=False):
                pool.wait_ge(idx_g_ready, n + 1)
                if not first:
                    pool.wait_ge(b_T, n - 1)
                gather_rows(l, s, xg_loaded[s])

            def scatter(l, n, s):
                pool.wait_ge(y_ready, n + 1)
                scatter_rows(l, s, y_stored[s])

            for l in range(LAYERS):
                if l:
                    pool.wait_ge(h_ready, NT)
                    pool.wait_ge(x_mixed1, YB + 1)
                    clear_gathered()
                for s in range(2):
                    pool.wait_ge(xn_stored[s], 16 * (NT // 2) * (l + 1))
                n0 = l * NE
                gather(l, n0, 0, first=True)
                gather(l, n0 + 1, 1, first=True)
                if l == 0:
                    bands()
                for e in range(HEAD):
                    gather(l, n0 + e + 2, e % 2)
                    if e:
                        scatter(l, n0 + e - 1, (e - 1) % 2)
                with pool.Fori(0, PAIRS) as i:
                    for e in PAIR:
                        gather(l, 2 * i + (n0 + e + 2), e % 2)
                        scatter(l, 2 * i + (n0 + e - 1), (e - 1) % 2)
                for e in range(NE - TAIL, NE + 1):
                    if e + 2 < NE:
                        gather(l, n0 + e + 2, e % 2)
                    scatter(l, n0 + e - 1, (e - 1) % 2)
                for s in range(2):
                    pool.wait_ge(y_stored[s], 16 * (NE // 2) * (l + 1))
                m = more[l]
                pool.wait_ge(extra_ready, l + 1)
                count = pool.value_load(extra[l][0:1, XB + 1:XB + 2], min_val=0, max_val=XB)
                with pool.If(count > 0):
                    g.sem_inc(m["free"], 1)
                    with pool.Fori(0, XB) as j:
                        with pool.If(j < count):
                            pool.wait_ge(m["idx"], j + 1)
                            gather_rows(l, 1, m["xg"])
                            pool.wait_ge(m["yr"], j + 1)
                            scatter_rows(l, 1, m["stored"])
                            pool.wait_ge(m["stored"], 16 * j + 16)
                            g.sem_inc(m["free"], 1)
                g.sem_inc(moe_done, 1)

        @block.scalar
        def _(act):
            a = nc.scalar
            ch = Chain(act, act_chain)

            def root(which, t0, t1):
                return a.activation(sd[:, which, t0:t1], ss[:, which, t0:t1], ACT.Sqrt, bias=eps[:, :], scale=1.0 / D)

            act.wait_ge(vec_ready, 1)
            a.activation(c_e[:, :], vc, ACT.Exp, scale=-1.0).then_inc(c_exp_ready, 1)
            act.wait_ge(consts, 1)
            for t in range(NT):
                act.wait_ge(x_loaded[t // 2], 16)
                ch.link(a.activation(hT[:, t, :], xr[:, t, :], ACT.Square, accum_out=ss[:, X_IN, t:t + 1]))
            root(X_IN, 0, NT).then_inc(x_ss, 1)
            act.wait_ge(x_rstd, 1)
            for t in range(NT):
                a.activation(xr[:, t, :], xr[:, t, :], ACT.Copy, scale=rstd[:, X_IN, t:t + 1]).then_inc(x_normed, 1)
            for t in range(NT):
                act.wait_ge(x_T, t + 1)
                src = PT if t % 2 == 0 else PA[1]
                a.activation(hT[:, :, t * P:(t + 1) * P], src.rearrange("p (k q) -> p k q", q=P), ACT.Copy)\
                 .then_inc(x_T_kept, 1)
            act.wait_ge(x_T_kept, NT)

            def piece_high(w):
                act.wait_ge(piece_loaded[w % RING], 16 * (w // RING + 1))
                a.activation(piece_hi[w % HRING][:, :, :], piece[w % RING][:, :, :], ACT.Copy).then_inc(w_high, 1)

            act.wait_ge(mod_ready0, 1)
            piece_high(0)
            for k in range(KD):
                a.activation(h_hi[:, k, :], hT[:, k, :], ACT.Identity, scale=a_m[:, k:k + 1],
                             bias=mod[0][:, SH_M, k:k + 1]).then_inc(h_act, 1)
            piece_high(1)
            dst = (zT, ybT, yaT)
            for u in range(8 * KA):
                m, half = u % (2 * KA) // 2, u % 2
                if u < 6 * KA:
                    act.wait_ge(proj_done, u + 1)
                    a.activation(dst[u // (2 * KA)][:, m, half * CH:(half + 1) * CH], BANK[u % 4], ACT.Copy)\
                     .then_inc(proj_kept, 1)
                if half:
                    act.wait_ge(proj_done, u + 1)
                    if u // 2 + RING < PIECES:
                        act.wait_ge(w_low, u // 2 + 1)
                        load_piece(act, u // 2 + RING)
                    if u // 2 + HRING < PIECES:
                        piece_high(u // 2 + HRING)
                n = PART_BEHIND.get(u)
                if n is not None and not as_columns(*PARTS[n]):
                    l, m = PARTS[n]
                    act.wait_ge(part_summed, n + 1)
                    if l == 0:
                        a.activation(grow[0 if m == G_M else 1][:, :], PT, ACT.Copy).then_inc(row_out, 1)
                    else:
                        before = ROWS_BEFORE[n] - ROWS_BEFORE[N0]
                        if before:
                            act.wait_ge(row_stored, 16 * before)
                        a.activation(row_kept[0:1, :], PT[0:1, :], ACT.Copy).then_inc(row_out, 1)
                        act.wait_ge(row_out, ROWS_BEFORE[n] + 1)
                        act.dma_start(mod1_dram[m:m + 1, :], row_kept[0:1, :]).then_inc(row_stored, 16)
                if u == 8 * KA - 4:
                    act.wait_ge(v_loaded, 16)
                    a.activation(v_hi[:, :, :], v_w[:, :, :], ACT.Copy).then_inc(w_high, 1)
            act.wait_ge(ws_T, 1)
            act.wait_ge(conv_done, 1)
            a.activation(wsT[:, :, :], PT.rearrange("p (k q) -> p k q", q=P), ACT.Copy).then_inc(ws_kept, 1)
            act.wait_ge(row_stored, 16 * 4)

            def entry_squares(l, t):
                which = N_FFN0 if l == 0 else N_FFN1
                act.wait_ge(x_mixed if l == 0 else x_mixed1, t + 1)
                if l == 0 and t == 0:
                    act.wait_ge(conv_done, 1)
                if l == 1 and t == 0:
                    act.wait_ge(entries_ready, 1)
                if l or t >= 2:
                    act.wait_ge(xn_stored[t % 2], 16 * (l * NT // 2 + t // 2))
                    act.wait_ge(n_T, l * NT + t - 1)
                ch.link(a.activation(xn[t % 2][:, :], xr[:, t, :], ACT.Square, accum_out=ss[:, which, t:t + 1]))
                root(which, t, t + 1).then_inc(n_ss, 1)

            def entry_rows(l, t):
                which = N_FFN0 if l == 0 else N_FFN1
                act.wait_ge(n_rstd, l * NT + t + 1)
                a.activation(xn[t % 2][:, :], xr[:, t, :], ACT.Copy, scale=rstd[:, which, t:t + 1]).then_inc(xn_ready, 1)

            def columns(dst, src, l):
                for k in range(KD):
                    last = a.activation(dst[:, k, :], src[:, k * P:(k + 1) * P], ACT.Identity,
                                        scale=a_f[l][:, k:k + 1], bias=mod[l][:, SH_F, k:k + 1])
                return last

            def entry_columns(l, t):
                n = l * NT + t
                act.wait_ge(n_T, n + 1)
                if n >= 2:
                    act.wait_ge(logit_done, n - 1)
                if n == 0:
                    act.wait_ge(mod_ready, 1)
                columns(hTt[t % 2], PT, l).then_inc(n_T_kept, 1)

            for k in range(NT):
                act.wait_ge(v_done, k + 1)
                if k:
                    act.wait_ge(v_ms_ready, k)
                a.activation(v_sq[:, :], BANK[k % 2], ACT.Square).then_inc(v_sq_done, 1)
                act.wait_ge(v_ms_ready, k + 1)
                if k:
                    act.wait_ge(v_ready, k)
                a.activation(vsd[:, :], vss[:, :], ACT.Sqrt, bias=eps[:, :], scale=1.0 / HD).then_inc(v_rs_half, 1)

            def tile_high(t):
                act.wait_ge(ya_ready, t + 1)
                if t >= 2:
                    act.wait_ge(mixed_done, t - 1)
                for part in range(2):
                    last = a.activation(y_hi[t % 2][:, part * KA:(part + 1) * KA, :], mix_tile(part, t), ACT.Copy)
                last.then_inc(w_high, 1)

            tile_high(0)
            act.wait_ge(out_w_loaded, 16 * 4)
            for q in range(KD):
                a.activation(out_hi[:, q, :], out_w[q], ACT.Copy).then_inc(w_high, 1)
            for k in range(NT + 2):
                if k + 1 < NT:
                    tile_high(k + 1)
                if 0 <= k - 2:
                    entry_rows(0, k - 2)
                    entry_columns(0, k - 2)
                if 0 <= k - 1 < NT:
                    entry_squares(0, k - 1)

            def block_columns(l, n, s):
                act.wait_ge(b_T, n + 1)
                columns(xT[s], PT, l).then_inc(xT_ready, 1)

            def sigmoid_part(n, first=False):
                act.wait_ge(g_done, n + 1)
                if not first:
                    act.wait_ge(act_ready, n)
                a.activation(sig[:, :], BANK[0], ACT.Exp, scale=-1.0).then_inc(sig_ready, 1)

            def act_high():
                return a.activation(aT_hi[:, :, :], PM.rearrange("p (k q) -> p k q", q=P), ACT.Copy)

            def weights_high(s, dst=down_hi):
                return a.activation(dst[:, :, :], down_w[s][:, :, :], ACT.Copy)

            def act_block(l, n, s, loaded, first=False, last=False):
                sigmoid_part(n, first)
                if last:
                    act.wait_ge(down_loaded[s], loaded)
                    weights_high(s, down_hi_last).then_inc(hi_ready, 1)
                if not last:
                    block_columns(l, n + 1, 1 - s)
                if not first:
                    act.wait_ge(y_done, n)
                if not last:
                    act.wait_ge(down_loaded[s], loaded)
                    weights_high(s).then_inc(hi_ready, 1)
                act.wait_ge(act_T, n + 1)
                act_high().then_inc(aT_hi_ready, 1)

            def moe(l):
                act.wait_ge(exp_in_ready, 2 * l + 1)
                a.activation(g_exp[:, :, :], g_diff[:, :, :], ACT.Exp).then_inc(exp_ready, 1)
                act.wait_ge(exp_in_ready, 2 * l + 2)
                a.activation(r_e[:, :], r_m[3][:, :], ACT.Exp).then_inc(exp_ready, 1)
                n0 = l * NE
                block_columns(l, n0, 0)
                c0 = 16 * (NE // 2) * l
                act.wait_ge(extra_ready, l + 1)
                for e in range(HEAD):
                    act_block(l, n0 + e, e % 2, c0 + 16 * (e // 2 + 1), first=n0 + e == 0)
                with act.Fori(0, PAIRS) as i:
                    for e in PAIR:
                        act_block(l, 2 * i + (n0 + e), e % 2, 16 * i + (c0 + 16 * (e // 2 + 1)))
                for e in range(NE - TAIL, NE):
                    act_block(l, n0 + e, e % 2, c0 + 16 * (e // 2 + 1), last=e == NE - 1)
                m = more[l]
                act.wait_ge(extra_ready, l + 1)
                count = act.value_load(extra[l][0:1, XB + 1:XB + 2], min_val=0, max_val=XB)
                with act.If(count > 0):
                    with act.Fori(0, XB) as j:
                        with act.If(j < count):
                            act.wait_ge(m["T"], j + 1)
                            columns(xT[1], PT, l).then_inc(m["xT"], 1)
                            act.wait_ge(m["gu"], j + 1)
                            a.activation(sig[:, :], BANK[0], ACT.Exp, scale=-1.0).then_inc(m["act"], 1)
                            act.wait_ge(m["w"], 48 * j + 48)
                            weights_high(1).then_inc(m["act"], 1)
                            act.wait_ge(m["aT_ps"], j + 1)
                            act_high().then_inc(m["act"], 1)

            moe(0)
            for k in range(NT + 4):
                if k < NT:
                    act.wait_ge(combined, k + 1)
                    ch.link(a.activation(y_in[k % YB][:, 1, :], xr[:, k, :], ACT.Square,
                                         accum_out=ss[:, N_MIX1, k:k + 1]))
                    root(N_MIX1, k, k + 1).then_inc(c_ss, 1)
                if 0 <= k - 1 < NT:
                    act.wait_ge(pool_T, k)
                    if k >= 2:
                        act.wait_ge(mixed1_done, k - 1)
                    a.activation(pooledT[:, :, :], PA[0].rearrange("p (k q) -> p k q", q=P), ACT.Copy)\
                     .then_inc(pool_kept, 1)
                if 0 <= k - 4:
                    entry_columns(1, k - 4)
                if 0 <= k - 3 < NT:
                    entry_rows(1, k - 3)
                    act.wait_ge(xn_ready, NT + k - 2)
                    act.dma_start(xn_dram[1][(k - 3) * P:(k - 2) * P, :], xn[(k - 3) % 2][:, :])\
                       .then_inc(xn_stored[(k - 3) % 2], 16)
                if 0 <= k - 2 < NT:
                    entry_squares(1, k - 2)
            moe(1)
            for k in range(NT + 2):
                if k < NT:
                    act.wait_ge(combined, NT + k + 1)
                    ch.link(a.activation(y_in[k % YB][:, 1, :], xr[:, k, :], ACT.Square,
                                         accum_out=ss[:, N_FINAL, k:k + 1]))
                    root(N_FINAL, k, k + 1).then_inc(c_ss, 1)
                if k >= 2:
                    act.wait_ge(out_ready, k - 1)
                    act.dma_start(outv[:, k - 2, :], xr[:, k - 2, :]).then_inc(out_stored, 16)

        @block.vector
        def _(dve):
            v = nc.vector
            ch = Chain(dve, dve_chain)

            dve.wait_ge(consts, 1)
            ch.link(v.reciprocal(inv_count[:, :], inv_count[:, :]))
            dve.wait_ge(vec_T, 1)
            v.tensor_copy(vec[:, 0:NVEC], PM[:, 0:NVEC]).then_inc(vec_ready, 1)
            dve.wait_ge(c_exp_ready, 1)
            ch.link(v.tensor_scalar(c_e[:, :], c_e[:, :], 1.0, None, ALU.add))
            ch.link(v.reciprocal(c_e[:, :], c_e[:, :]))
            ch.link(v.tensor_tensor(c_act[:, :], c_e[:, :], vc, ALU.mult))
            for j in range(2):
                part = acc0[:, j * D:(j + 1) * D]
                for q in range(4):
                    if j == 0 and q == 1:
                        dve.wait_ge(x_ss, 1)
                        v.reciprocal(rstd[:, X_IN, :], sd[:, X_IN, :]).then_inc(x_rstd, 1)
                    dve.wait_ge(cond0_loaded[q], 16 * j + (16 if q else 32))
                    for i in range(2):
                        ch.link(v.scalar_tensor_tensor(out=part, in0=cond0[q][:, i, :],
                                                       scalar=c_act[:, 2 * q + i:2 * q + i + 1],
                                                       in1=part, op0=ALU.mult, op1=ALU.add))
                    v.sem_inc(cond0_used, 1)
                v.sem_inc(acc0_ready, 1)
            dve.wait_ge(mod_cols0, 1)
            ch.link(v.tensor_copy(mod[0][:, 0:2, :], PM[:, 0:2 * KD].rearrange("p (m k) -> p m k", k=KD)))
            ch.link(v.scalar_tensor_tensor(out=a_m[:, :], in0=mod[0][:, SC_M, :], scalar=1.0, in1=vg_mix[0],
                                           op0=ALU.add, op1=ALU.mult))
            v.sem_inc(mod_ready0, 1)
            dve.wait_ge(x_T_kept, NT)
            for k in range(KD):
                dve.wait_ge(h_act, k + 1)
                v.tensor_scalar(hT[:, k, :], hT[:, k, :], a_m[:, k:k + 1], mod[0][:, SH_M, k:k + 1],
                                ALU.mult, ALU.add).then_inc(h_dve, 1)
                if k % 2 == 0:
                    dve.wait_ge(h_dve, h_made(k))
                    v.tensor_tensor(h_lo[:, k, :], hT[:, k, :], h_hi[:, k, :].bitcast(F32), ALU.subtract)\
                     .then_inc(h_dve, 1)

            def part_sum(n, parity):
                static = isinstance(n, int)
                if not static or n >= 2:
                    dve.wait_ge(part_summed, n - 1)
                past = 16 * (n // 2 + 1) if static else n * 8 + (16 - 8 * parity)
                dve.wait_ge(bias_loaded[parity], past)
                for k in range(KD):
                    dve.wait_ge(cond_loaded[k % UNITS], n * 32 + 16 * (k // UNITS + 1))
                    ch.link(v.scalar_tensor_tensor(out=acc[parity][:, :], in0=cond[k % UNITS][:, :],
                                                   scalar=c_act[:, k:k + 1],
                                                   in1=acc[parity][:, :] if k else bias[parity][:, :],
                                                   op0=ALU.mult, op1=ALU.add))
                    v.sem_inc(cond_used, 1)
                v.sem_inc(acc_ready, 1)

            for n in range(N0):
                part_sum(n, n % 2)
            with dve.Fori(0, NMOD // 2) as j:
                ch.enter(j, 2 * KD)
                for q in range(2):
                    part_sum(2 * j + (N0 + q), q)
            ch.leave(NMOD // 2)
            dve.wait_ge(part_summed, len(PARTS))
            for l in range(LAYERS):
                lo = (l * NMOD + SH_F) * KD
                ch.link(v.tensor_copy(mod[l][:, SH_F:SC_F + 1, :],
                                      PM[:, lo:lo + 2 * KD].rearrange("p (m k) -> p m k", k=KD)))
                ch.link(v.scalar_tensor_tensor(out=a_f[l][:, :], in0=mod[l][:, SC_F, :], scalar=1.0, in1=vg_ffn[l],
                                               op0=ALU.add, op1=ALU.mult))
            v.sem_inc(mod_ready, 1)

            def conv(m):
                ch.link(v.tensor_scalar(conv_t[:, :], zT[:, m, :], conv_col(2, m), None, ALU.mult))
                for back in (1, 2):
                    ch.link(v.scalar_tensor_tensor(out=conv_t[:, back:], in0=zT[:, m, 0:S - back],
                                                   scalar=conv_col(2 - back, m), in1=conv_t[:, back:],
                                                   op0=ALU.mult, op1=ALU.add))
                ch.link(v.tensor_tensor(ybT[:, m, :], ybT[:, m, :], conv_t[:, :], ALU.mult))

            dve.wait_ge(proj_kept, 6 * KA)
            dve.wait_ge(row_stored, 16 * 4)
            for m in range(KA):
                for half in range(2):
                    u = 6 * KA + 2 * m + half
                    dve.wait_ge(proj_done, u + 1)
                    part = zT[:, m, half * CH:(half + 1) * CH]
                    v.tensor_tensor(part, BANK[u % 4], part, ALU.mult).then_inc(z_kept, 1)
                dve.wait_ge(z_kept, 2 * m + 2)
                conv(m)
            v.sem_inc(conv_done, 1)

            def v_norm(t):
                dve.wait_ge(v_sq_done, t + 1)
                v.tensor_reduce(out=vss[:, :], in_=v_sq[:, :].rearrange("p (h d) -> p h d", d=HD),
                                axis=AX.X, op=ALU.add).then_inc(v_ms_ready, 1)
                dve.wait_ge(v_rs_half, t + 1)
                ch.link(v.reciprocal(vrs[:, :], vsd[:, :]))
                if t >= 2:
                    dve.wait_ge(sgu_done, t - 1)
                dst = v_n[t % 2][:, :].rearrange("p (h d) -> p h d", d=HD)
                ch.link(v.tensor_tensor(dst, BANK[t % 2].rearrange("p (h d) -> p h d", d=HD),
                                        bc(vrs[:, :].unsqueeze(2), [P, HEADS, HD]), ALU.mult))
                v.tensor_tensor(v_n[t % 2][:, :], v_n[t % 2][:, :], gv[:, :], ALU.mult).then_inc(v_ready, 1)

            def spatial_gate(t):
                dve.wait_ge(sgu_done, t + 1)
                ch.link(v.tensor_tensor(gated[:, :], PM, bsp[:, :, :].rearrange("p m q -> p (m q)"), ALU.add))
                u = yaT[:, :, t * P:(t + 1) * P]
                v.tensor_tensor(u, u, gated[:, :].rearrange("p (m q) -> p m q", q=P), ALU.mult).then_inc(ya_ready, 1)

            def residual(t):
                dve.wait_ge(mixed_done, t + 1)
                if t == 0:
                    dve.wait_ge(row_out, 1)
                else:
                    dve.wait_ge(x_mixed, t)
                dve.wait_ge(x_loaded[t // 2], 32)
                ch.link(v.tensor_tensor(res_t[:, :], PA[1 - t % 2], grow[0][:, :], ALU.mult))
                v.tensor_tensor(xr[:, t, :], xr[:, t, :], res_t[:, :], ALU.add).then_inc(x_mixed, 1)

            def entry_rstd(l, t):
                which = N_FFN0 if l == 0 else N_FFN1
                dve.wait_ge(n_ss, l * NT + t + 1)
                v.reciprocal(rstd[:, which, t:t + 1], sd[:, which, t:t + 1]).then_inc(n_rstd, 1)

            dve.wait_ge(sgu_loaded, 16 * (1 + HEADS))
            for k in range(NT + 1):
                if k < NT:
                    v_norm(k)
                if k == NT:
                    for q in LOW_BY_DVE:
                        dve.wait_ge(w_high, out_high(q))
                        v.tensor_tensor(out_lo[q], out_w[q], out_hi[:, q, :].bitcast(F32), ALU.subtract)\
                         .then_inc(out_low, 1)
                if k:
                    spatial_gate(k - 1)
            for k in range(NT + 2):
                if 0 <= k - 2:
                    entry_rstd(0, k - 2)
                if k < NT:
                    residual(k)

            def routing_of(l):
                dve.wait_ge(logit_done, (l + 1) * NT)
                for s in range(2):
                    dve.wait_ge(xn_stored[s], 16 * (NT // 2) * (l + 1))
                if l == 0:
                    dve.wait_ge(const_loaded, 16 * 4 * LAYERS)
                ch.link(v.tensor_tensor(logits[:, :, :], PL[:, 0:NT * NR].rearrange("p (t r) -> p t r", r=NR),
                                        bc(r_b[l][:, :].unsqueeze(1), [P, NT, NR]), ALU.add))
                gl = logits[:, :, 0:NG]
                el = logits[:, :, NG:NR].rearrange("p t (g e) -> p t g e", e=EG)
                gshape, eshape = [P, NT, NG], [P, NT, EG]

                def first_max(val, mx, diff, key, rank, top, hot_, shape):
                    ch.link(v.tensor_reduce(out=mx, in_=val, axis=AX.X, op=ALU.max))
                    ch.link(v.tensor_tensor(diff, val, bc(mx.unsqueeze(2), shape), ALU.subtract))
                    ch.link(v.tensor_scalar(key, diff, 0.0, None, ALU.is_ge))
                    rb = bc(rank.unsqueeze(1), shape)
                    ch.link(v.tensor_tensor(key, key, rb, ALU.mult))
                    ch.link(v.tensor_reduce(out=top, in_=key, axis=AX.X, op=ALU.max))
                    ch.link(v.tensor_tensor(hot_, rb, bc(top.unsqueeze(2), shape), ALU.is_equal))

                first_max(gl, r_m[0][:, :], g_diff[:, :, :], g_key[:, :, :], rank_g[:, :],
                          kg_hot[:, :], g_hot[:, :, :], gshape)
                v.sem_inc(exp_in_ready, 1)
                dve.wait_ge(exp_ready, 2 * l + 1)
                ch.link(v.tensor_reduce(out=g_w[:, :], in_=g_exp[:, :, :], axis=AX.X, op=ALU.add))
                ch.link(v.reciprocal(g_w[:, :], g_w[:, :]))
                ch.link(v.tensor_tensor(e_prod[:, :, :, :], el, bc(g_hot[:, :, :].unsqueeze(3), [P, NT, NG, EG]), ALU.mult))
                ch.link(v.tensor_reduce(out=e_sel[:, :, :], in_=e_prod[:, :, :, :].rearrange("p t g e -> p t e g"),
                                        axis=AX.X, op=ALU.add))
                first_max(e_sel[:, :, :], r_m[1][:, :], e_diff[:, :, :], e_key[:, :, :], rank_e[:, :],
                          ke_hot[0][:, :], e_hot[0][:, :, :], eshape)
                ch.link(v.scalar_tensor_tensor(out=e_sel[:, :, :], in0=e_hot[0][:, :, :], scalar=-3e38,
                                               in1=e_sel[:, :, :], op0=ALU.mult, op1=ALU.add))
                first_max(e_sel[:, :, :], r_m[2][:, :], e_diff[:, :, :], e_key[:, :, :], rank_e[:, :],
                          ke_hot[1][:, :], e_hot[1][:, :, :], eshape)
                ch.link(v.tensor_tensor(r_m[3][:, :], r_m[2][:, :], r_m[1][:, :], ALU.subtract))
                v.sem_inc(exp_in_ready, 1)
                for i in range(2):
                    ch.link(v.tensor_tensor(hot[i][:, :, :].rearrange("p t (g e) -> p t g e", e=EG),
                                            bc(g_hot[:, :, :].unsqueeze(3), [P, NT, NG, EG]),
                                            bc(e_hot[i][:, :, :].unsqueeze(2), [P, NT, NG, EG]), ALU.mult))
                ch.link(v.tensor_tensor(hots[:, :, :], hot[0][:, :, :], hot[1][:, :, :], ALU.add))
                ch.link(v.memset(before[:, 0, :], 0.0))
                for t in range(NT):
                    ch.link(v.tensor_tensor(before[:, t + 1, :], before[:, t, :], hots[:, t, :], ALU.add))
                v.sem_inc(hots_ready, 1)
                dve.wait_ge(exp_ready, 2 * l + 2)
                ch.link(v.tensor_scalar(r_r[:, :], r_e[:, :], 1.0, None, ALU.add))
                ch.link(v.reciprocal(r_r[:, :], r_r[:, :]))
                ch.link(v.tensor_tensor(r_r[:, :], r_r[:, :], g_w[:, :], ALU.mult))
                ch.link(v.tensor_copy(gates[:, :, 0], r_r[:, :]))
                ch.link(v.tensor_tensor(gates[:, :, 1], r_r[:, :], r_e[:, :], ALU.mult))
                ch.link(v.tensor_scalar(kg_hot[:, :], kg_hot[:, :], -float(EG), float(NE + EG), ALU.mult, ALU.add))
                for i in range(2):
                    ch.link(v.tensor_tensor(a_exp[:, :, i], kg_hot[:, :], ke_hot[i][:, :], ALU.subtract))
                dve.wait_ge(rank_done, l + 1)
                cnt = PM[:, NT * NE:(NT + 1) * NE]
                ch.link(v.tensor_scalar(nblk[:, :], cnt, float(P - 1), None, ALU.add))
                ch.link(v.tensor_copy(cnt_i[:, :], nblk[:, :]))
                ch.link(v.tensor_scalar(cnt_i[:, :], cnt_i[:, :], 7, None, ALU.arith_shift_right))
                ch.link(v.tensor_copy(nblk[:, :], cnt_i[:, :]))
                ch.link(v.tensor_scalar(nblk[:, :], nblk[:, :], -1.0, 0.0, ALU.add, ALU.max))
                ch.link(v.tensor_tensor_scan(bend[:, :], ones[:, 0:NE], nblk[:, :], 0.0, ALU.mult, ALU.add))
                ranks = PM[:, 0:NT * NE].rearrange("p (t e) -> p t e", e=NE)
                for i in range(2):
                    ch.link(v.tensor_tensor(s_tmp[:, :, :], ranks, hot[i][:, :, :], ALU.mult))
                    ch.link(v.tensor_reduce(out=a_pos[:, :, i], in_=s_tmp[:, :, :], axis=AX.X, op=ALU.add))
                ch.link(v.tensor_copy(a_posi[:, :, :], a_pos[:, :, :]))
                ch.link(v.tensor_scalar(a_posi[:, :, :], a_posi[:, :, :], 7, None, ALU.arith_shift_right))
                ch.link(v.tensor_copy(a_quo[:, :, :], a_posi[:, :, :]))
                ch.link(v.scalar_tensor_tensor(out=a_row[:, :, :], in0=a_quo[:, :, :], scalar=-float(P),
                                               in1=a_pos[:, :, :], op0=ALU.mult, op1=ALU.add))
                ch.link(v.tensor_tensor(b_off[:, :], bend[:, :], nblk[:, :], ALU.subtract))
                for i in range(2):
                    ch.link(v.tensor_tensor(s_tmp[:, :, :], hot[i][:, :, :], bc(b_off[:, :].unsqueeze(1), [P, NT, NE]),
                                            ALU.mult))
                    ch.link(v.tensor_reduce(out=a_blk[:, :, i], in_=s_tmp[:, :, :], axis=AX.X, op=ALU.add))
                ch.link(v.scalar_tensor_tensor(out=a_blk[:, :, :], in0=a_blk[:, :, :], scalar=float(NE - 1),
                                               in1=a_exp[:, :, :], op0=ALU.add, op1=ALU.subtract))
                ch.link(v.scalar_tensor_tensor(out=a_blk[:, :, :], in0=a_quo[:, :, :], scalar=0.0,
                                               in1=a_blk[:, :, :], op0=ALU.is_gt, op1=ALU.mult))
                ch.link(v.tensor_tensor(a_blk[:, :, :], a_blk[:, :, :], a_exp[:, :, :], ALU.add))
                ch.link(v.tensor_tensor(a_blk[:, :, :], a_blk[:, :, :], a_quo[:, :, :], ALU.add))
                two = lambda ap: ap.rearrange("p t i -> p (t i)").unsqueeze(2)
                bsh = [P, 2 * NT, NBLK]
                ch.link(v.tensor_tensor(blk_hot[:, :, :], bc(two(a_blk[:, :, :]), bsh),
                                        bc(row_id[:, 0:NBLK].unsqueeze(1), bsh), ALU.is_equal))
                for i, val in enumerate((number, gates)):
                    ch.link(v.tensor_tensor(blk_val[:, :, i, :], blk_hot[:, :, :], bc(two(val[:, :, :]), bsh), ALU.mult))
                rsh = [P, 2 * NT, P]
                ch.link(v.tensor_tensor(row_hot[:, :, :], bc(two(a_row[:, :, :]), rsh),
                                        bc(row_id[:, :].unsqueeze(1), rsh), ALU.is_equal))
                v.sem_inc(entries_ready, 1)

            def further_blocks(l):
                esh = [1, XB + 1, NE]
                ch.link(v.tensor_tensor(cmp_t[0:1, :, :], bc(bend[0:1, :].unsqueeze(1), esh),
                                        bc(j_id[0:1, :].unsqueeze(2), esh), ALU.is_le))
                ch.link(v.tensor_reduce(out=eid_f[0:1, 0:XB + 1], in_=cmp_t[0:1, :, :], axis=AX.X, op=ALU.add))
                ch.link(v.tensor_scalar(eid_f[0:1, 0:XB + 1], eid_f[0:1, 0:XB + 1], float(NE - 1), None, ALU.min))
                ch.link(v.tensor_copy(eid_f[0:1, XB + 1:XB + 2], bend[0:1, NE - 1:NE]))
                ch.link(v.tensor_copy(extra[l][0:1, :], eid_f[0:1, :]))
                v.sem_inc(extra_ready, 1)

            def gather_index(e, loaded, s):
                if loaded is not None:
                    dve.wait_ge(xg_loaded[s], loaded)
                v.tensor_copy(idx_g[s][:, :], tok[:, ds(e, 1)]).then_inc(idx_g_ready, 1)

            def silu_mul(done, chain):
                chain.link(v.tensor_scalar(sig[:, :], sig[:, :], 1.0, None, ALU.add))
                chain.link(v.reciprocal(sig[:, :], sig[:, :]))
                chain.link(v.tensor_tensor(act_r[:, :], BANK[0], sig[:, :], ALU.mult))
                done()

            def silu(n):
                dve.wait_ge(sig_ready, n + 1)
                silu_mul(lambda: dve.wait_ge(u_done, n + 1), ch)
                v.tensor_tensor(act_r[:, :], act_r[:, :], BANK[1], ALU.mult).then_inc(act_ready, 1)

            def weights_low(s, high=down_hi):
                return v.tensor_tensor(down_lo[s][:, :, :], down_w[s][:, :, :], high[:, :, :].bitcast(F32),
                                       ALU.subtract)

            def act_low():
                return v.tensor_tensor(aT_lo[:, :, :], PM.rearrange("p (k q) -> p k q", q=P),
                                       aT_hi[:, :, :].bitcast(F32), ALU.subtract)

            def low_part_of_weights(n, s, high=down_hi):
                dve.wait_ge(hi_ready, n + 1)
                weights_low(s, high).then_inc(lo_ready, 1)

            def low_part_of_act(n):
                dve.wait_ge(aT_hi_ready, n + 1)
                act_low().then_inc(aT_ready, 1)

            def results(e, n, s, stored):
                dve.wait_ge(y_done, n + 1)
                if stored is not None:
                    dve.wait_ge(y_stored[s], stored)
                ch.link(v.tensor_copy(idx_s[s][:, :], asg[:, ds(e, 1)]))
                ch.link(v.tensor_copy(gate_c[s][:, :], slot_gate[:, ds(e, 1)]))
                v.scalar_tensor_tensor(out=y_o[s][:, :], in0=PA[1], scalar=gate_c[s][:, :], in1=grow[1][:, :],
                                       op0=ALU.mult, op1=ALU.mult).then_inc(y_ready, 1)

            def moe(l):
                routing_of(l)
                n0, c0 = l * NE, 16 * (NE // 2) * l
                dve.wait_ge(table_summed, l + 1)
                ch.link(v.tensor_scalar(empty[:, :], PL[:, 0:NBLK], 0.0, float(PAD + 1), ALU.is_equal, ALU.mult))
                ch.link(v.tensor_tensor(asg_f[:, :], PL[:, 0:NBLK], empty[:, :], ALU.add))
                ch.link(v.tensor_scalar(asg[:, :], asg_f[:, :], -1.0, None, ALU.add))
                ch.link(v.tensor_scalar(tok[:, :], asg[:, :], TOKEN_MASK, None, ALU.bitwise_and))
                ch.link(v.tensor_copy(slot_gate[:, :], PL[:, NBLK:2 * NBLK]))
                for e in range(2):
                    gather_index(e, None, e)
                further_blocks(l)
                if l == 0:
                    dve.wait_ge(rows1_loaded, 16 * 2)
                    ch.link(v.tensor_tensor(grow[0][:, :], grow[0][:, :], factor[:, :], ALU.mult))
                else:
                    dve.wait_ge(gain1_loaded, 16)
                def dve_block(e, i=None):
                    past, n = (0, n0 + e) if i is None else (16 * i, 2 * i + (n0 + e))
                    if e + 2 < NE:
                        nxt = e + 2 if i is None else 2 * i + (e + 2)
                        gather_index(nxt, past + (c0 + 16 * (e // 2 + 1)), e % 2)
                    silu(n)
                    if e == NE - 1:
                        low_part_of_weights(n, e % 2, down_hi_last)
                    if e:
                        m, before_m = e - 1, (e - 1) // 2
                        results(m if i is None else 2 * i + m, n - 1, m % 2,
                                past + (c0 + 16 * before_m) if c0 + before_m else None)
                    if e < NE - 1:
                        low_part_of_weights(n, e % 2)
                    low_part_of_act(n)

                for e in range(HEAD):
                    dve_block(e)
                with dve.Fori(0, PAIRS) as i:
                    ch.enter(i, 10)
                    for e in PAIR:
                        dve_block(e, i)
                ch.leave(PAIRS)
                for e in range(NE - TAIL, NE):
                    dve_block(e)
                results(NE - 1, n0 + NE - 1, (NE - 1) % 2, c0 + 16 * ((NE - 1) // 2))
                m = more[l]
                count = dve.value_load(extra[l][0:1, XB + 1:XB + 2], min_val=0, max_val=XB)
                with dve.If(count > 0):
                    xch = Chain(dve, m["chain"])
                    with dve.Fori(0, XB) as j:
                        with dve.If(j < count):
                            xch.enter(j, 6)
                            dve.wait_ge(m["free"], j + 1)
                            xch.link(v.tensor_copy(idx_g[1][:, :], tok[:, ds(j + NE, 1)]))
                            xch.link(v.tensor_copy(idx_s[1][:, :], asg[:, ds(j + NE, 1)]))
                            xch.link(v.tensor_copy(gate_c[1][:, :], slot_gate[:, ds(j + NE, 1)]))
                            v.sem_inc(m["idx"], 1)
                            dve.wait_ge(m["act"], 3 * j + 1)
                            silu_mul(lambda: None, xch)
                            v.tensor_tensor(act_r[:, :], act_r[:, :], BANK[1], ALU.mult).then_inc(m["dve"], 1)
                            dve.wait_ge(m["act"], 3 * j + 2)
                            weights_low(1).then_inc(m["dve"], 1)
                            dve.wait_ge(m["act"], 3 * j + 3)
                            act_low().then_inc(m["dve"], 1)
                            dve.wait_ge(m["y"], j + 1)
                            v.scalar_tensor_tensor(out=y_o[1][:, :], in0=PA[1], scalar=gate_c[1][:, :],
                                                   in1=grow[1][:, :], op0=ALU.mult, op1=ALU.mult).then_inc(m["yr"], 1)

            def combine(l, t):
                dve.wait_ge(y_in_loaded[t % YB], 16 * ((l * NT + t) // YB + 1))
                ch.link(v.tensor_tensor(xr[:, t, :], xr[:, t, :], y_in[t % YB][:, 0, :], ALU.add))
                v.tensor_tensor(xr[:, t, :], xr[:, t, :], y_in[t % YB][:, 1, :], ALU.add).then_inc(combined, 1)

            moe(0)
            dve.wait_ge(rows1_loaded, 16 * 5)
            ch.link(v.scalar_tensor_tensor(out=a1b[:, :], in0=a1b[:, :], scalar=1.0, in1=factor[:, :],
                                           op0=ALU.add, op1=ALU.mult))
            for k in range(NT + 3):
                if k < NT:
                    combine(0, k)
                if 0 <= k - 1 < NT:
                    t = k - 1
                    dve.wait_ge(c_ss, t + 1)
                    ch.link(v.reciprocal(rstd[:, N_MIX1, t:t + 1], sd[:, N_MIX1, t:t + 1]))
                    if t >= 2:
                        dve.wait_ge(pool_T, t)
                    ch.link(v.scalar_tensor_tensor(out=h_r[t % 2][:, :], in0=xr[:, t, :],
                                                   scalar=rstd[:, N_MIX1, t:t + 1], in1=a1b[:, :],
                                                   op0=ALU.mult, op1=ALU.mult))
                    v.tensor_tensor(h_r[t % 2][:, :], h_r[t % 2][:, :], b1b[:, :], ALU.add).then_inc(h_ready, 1)
                if 0 <= k - 3:
                    entry_rstd(1, k - 3)
                if 0 <= k - 2 < NT:
                    t = k - 2
                    dve.wait_ge(mixed1_done, t + 1)
                    tmp = y_in[t % YB][:, 0, :]
                    ch.link(v.tensor_tensor(tmp, PA[1], grow[0][:, :], ALU.mult))
                    v.tensor_tensor(xr[:, t, :], xr[:, t, :], tmp, ALU.add).then_inc(x_mixed1, 1)
            moe(1)
            dve.wait_ge(final_loaded, 16)
            for k in range(NT + 1):
                if k < NT:
                    combine(1, k)
                if k >= 1:
                    t = k - 1
                    dve.wait_ge(c_ss, NT + t + 1)
                    ch.link(v.reciprocal(rstd[:, N_FINAL, t:t + 1], sd[:, N_FINAL, t:t + 1]))
                    v.scalar_tensor_tensor(out=xr[:, t, :], in0=xr[:, t, :], scalar=rstd[:, N_FINAL, t:t + 1],
                                           in1=grow[0][:, :], op0=ALU.mult, op1=ALU.mult).then_inc(out_ready, 1)

        @block.tensor
        def _(pe):
            mm = nc.tensor.matmul

            def rows_to_columns(dst, src):
                for k in range(KD):
                    last = nc.tensor.transpose(dst[:, k * P:(k + 1) * P], src[:, k * P:(k + 1) * P], ident[:, :])
                return last

            pe.wait_ge(consts, 1)
            pe.wait_ge(vec_loaded, 16 * 6)
            nc.tensor.transpose(PM[:, 0:NVEC], vec_rows[0:NVEC, :], ident[0:NVEC, 0:NVEC]).then_inc(vec_T, 1)
            for t in range(NT):
                pe.wait_ge(x_normed, t + 1)
                if t >= 2:
                    pe.wait_ge(x_T_kept, t - 1)
                rows_to_columns(PT if t % 2 == 0 else PA[1], xr[:, t, :]).then_inc(x_T, 1)

            def to_columns(col, rows_):
                for k in range(KD):
                    last = mm(PM[:, col * KD + k:col * KD + k + 1], rows_[:, k * P:(k + 1) * P], ones[:, 0:1],
                              start=True, stop=True)
                return last

            pe.wait_ge(vec_ready, 1)
            for m in range(2):
                pe.wait_ge(acc0_ready, m + 1)
                last = to_columns(m, acc0[:, m * D:(m + 1) * D])
            last.then_inc(mod_cols0, 1)

            def sum_part(n):
                l, m = PARTS[n]
                pe.wait_ge(acc_ready, n + 1)
                if as_columns(l, m):
                    to_columns(l * NMOD + m, acc[n % 2][:, :]).then_inc(part_summed, 1)
                else:
                    if ROWS_BEFORE[n]:
                        pe.wait_ge(row_out, ROWS_BEFORE[n])
                    for half in range(2):
                        last = mm(PT[:, half * CH:(half + 1) * CH], ones[:, :],
                                  acc[n % 2][:, half * CH:(half + 1) * CH], start=True, stop=True)
                    last.then_inc(part_summed, 1)

            def project(w):
                pe.wait_ge(w_low, w + 1)
                for half in range(2):
                    u = 2 * w + half
                    if u >= 4:
                        done = u - 3
                        pe.wait_ge(*((proj_kept, done) if done <= 6 * KA else (z_kept, done - 6 * KA)))
                    tokens = slice(half * CH, (half + 1) * CH)
                    for k in range(KD):
                        if u == 0:
                            if k % 2:
                                pe.wait_ge(h_pool, k // 2 + 1)
                            else:
                                pe.wait_ge(h_dve, h_made(k) + 1)
                        w_hi, w_lo = piece_hi[w % HRING][:, k, :], piece_lo[w % RING][:, k, :]
                        mm(BANK[u % 4], w_hi, h_hi[:, k, tokens], start=k == 0, stop=False)
                        mm(BANK[u % 4], w_hi, h_lo[:, k, tokens], start=False, stop=False)
                        last = mm(BANK[u % 4], w_lo, h_hi[:, k, tokens], start=False, stop=k == KD - 1)
                    last.then_inc(proj_done, 1)
                    if u in PART_BEHIND:
                        sum_part(PART_BEHIND[u])

            pe.wait_ge(x_T_kept, NT)
            pe.wait_ge(mod_ready0, 1)
            for w in range(PIECES):
                project(w)
            pe.wait_ge(ws_loaded, 16)
            pe.wait_ge(row_out, ROWS_BEFORE[-1])
            for h in range(HEADS):
                last = nc.tensor.transpose(PT[:, h * P:(h + 1) * P], ws_raw[:, h, :], ident[:, :])
            last.then_inc(ws_T, 1)

            def entry_T(l, t):
                n = l * NT + t
                pe.wait_ge(xn_ready, n + 1)
                if t:
                    pe.wait_ge(n_T_kept, n)
                rows_to_columns(PT, xn[t % 2]).then_inc(n_T, 1)

            def entry_logits(l, t):
                pe.wait_ge(n_T_kept, l * NT + t + 1)
                for k in range(KD):
                    last = mm(PL[:, t * NR:(t + 1) * NR], hTt[t % 2][:, k, :], r_w[l][:, k, :],
                              start=k == 0, stop=k == KD - 1)
                last.then_inc(logit_done, 1)

            pe.wait_ge(w_low, PIECES + 1)
            pe.wait_ge(z_kept, 2 * KA)
            for k in range(NT + 1):
                if k < NT:
                    if k >= 2:
                        pe.wait_ge(v_ready, k - 1)
                    for q in range(KD):
                        hi, lo = h_hi[:, q, k * P:(k + 1) * P], h_lo[:, q, k * P:(k + 1) * P]
                        mm(BANK[k % 2], hi, v_hi[:, q, :], start=q == 0, stop=False)
                        mm(BANK[k % 2], hi, v_lo[:, q, :], start=False, stop=False)
                        last = mm(BANK[k % 2], lo, v_hi[:, q, :], start=False, stop=q == KD - 1)
                    last.then_inc(v_done, 1)
                if k:
                    t = k - 1
                    pe.wait_ge(v_ready, t + 1)
                    if t == 0:
                        pe.wait_ge(ws_masked, 1)
                        pe.wait_ge(mod_ready, 1)
                    else:
                        pe.wait_ge(ya_ready, t)
                    for h in range(HEADS):
                        q = (h % 2) * HD
                        last = mm(PM[q:q + HD, (h // 2) * P:(h // 2 + 1) * P], v_n[t % 2][:, h * HD:(h + 1) * HD],
                                  wsT[:, h, :], start=True, stop=True)
                    last.then_inc(sgu_done, 1)
            pe.wait_ge(conv_done, 1)
            for k in range(NT + 3):
                if k < NT:
                    pe.wait_ge(w_low, mix_low(k))
                    if k >= 2:
                        pe.wait_ge(x_mixed, k - 1)
                    for half in range(2):
                        dst, cols = PA[1 - k % 2][:, half * CH:(half + 1) * CH], slice(half * CH, (half + 1) * CH)
                        for q in range(KD):
                            if k == 0 and half == 0:
                                if q in LOW_BY_POOL:
                                    pe.wait_ge(w_low, mix_low(0) + LOW_BY_POOL.index(q) + 1)
                                else:
                                    pe.wait_ge(out_low, LOW_BY_DVE.index(q) + 1)
                            hi, lo = y_hi[k % 2][:, q, :], y_lo[k % 2][:, q, :]
                            mm(dst, hi, out_hi[:, q, cols], start=q == 0, stop=False)
                            mm(dst, hi, out_lo[q][:, cols], start=False, stop=False)
                            last = mm(dst, lo, out_hi[:, q, cols], start=False, stop=q == KD - 1)
                    last.then_inc(mixed_done, 1)
                if k == 2:
                    pe.wait_ge(const_loaded, 16 * 4 * LAYERS)
                    pe.wait_ge(ws_kept, 1)
                if 0 <= k - 2 < NT:
                    entry_T(0, k - 2)
                if 0 <= k - 3:
                    entry_logits(0, k - 3)

            def block_T(n, s, loaded):
                pe.wait_ge(xg_loaded[s], loaded)
                pe.wait_ge(xT_ready, n) if not isinstance(n, int) or n > 0 else None
                rows_to_columns(PT, xg[s]).then_inc(b_T, 1)

            def gate_up(s):
                for q in range(KD):
                    lg = mm(BANK[0], xT[s][:, q, :], gate_w[s][:, q, :], start=q == 0, stop=q == KD - 1)
                yield lg
                for q in range(KD):
                    lu = mm(BANK[1], xT[s][:, q, :], up_w[s][:, q, :], start=q == 0, stop=q == KD - 1)
                yield lu

            def act_transpose():
                for q in range(KF):
                    last = nc.tensor.transpose(PM[:, q * P:(q + 1) * P], act_r[:, q * P:(q + 1) * P], ident[:, :])
                return last

            def down(s, high=down_hi):
                for half in range(2):
                    part = slice(half * CH, (half + 1) * CH)
                    for q in range(KF):
                        mm(BANK[2 + half], aT_hi[:, q, :], high[:, q, part], start=q == 0, stop=False)
                        mm(BANK[2 + half], aT_hi[:, q, :], down_lo[s][:, q, part], start=False, stop=False)
                        last = mm(BANK[2 + half], aT_lo[:, q, :], high[:, q, part], start=False, stop=q == KF - 1)
                return last

            def down_block(n, s, high=down_hi):
                pe.wait_ge(lo_ready, n + 1)
                pe.wait_ge(aT_ready, n + 1)
                if not (isinstance(n, int) and n == 0):
                    pe.wait_ge(y_ready, n)
                down(s, high).then_inc(y_done, 1)

            def pe_block(n, s, loaded, next_loaded, first=False, last=False):
                pe.wait_ge(xT_ready, n + 1)
                pe.wait_ge(gate_loaded[s], loaded)
                if not (isinstance(n, int) and n == 0):
                    pe.wait_ge(act_ready, n)
                parts = gate_up(s)
                next(parts).then_inc(g_done, 1)
                pe.wait_ge(up_loaded[s], loaded)
                next(parts).then_inc(u_done, 1)
                if not last:
                    block_T(n + 1, 1 - s, next_loaded)
                if not first:
                    down_block(n - 1, 1 - s)
                pe.wait_ge(act_ready, n + 1)
                act_transpose().then_inc(act_T, 1)

            def moe(l):
                pe.wait_ge(hots_ready, l + 1)
                if l == 0:
                    pe.wait_ge(ya_ready, NT)
                flat = hots[:, :, :].rearrange("p t e -> p (t e)")
                bflat = before[:, :, :].rearrange("p t e -> p (t e)")
                mm(PM[:, 0:NT * NE], lower[:, :], flat, start=True, stop=False)
                mm(PM[:, 0:NT * NE], ones[:, :], bflat[:, 0:NT * NE], start=False, stop=True)
                mm(PM[:, NT * NE:(NT + 1) * NE], ones[:, :], bflat[:, NT * NE:(NT + 1) * NE],
                   start=True, stop=True).then_inc(rank_done, 1)
                n0, c0 = l * NE, 16 * (NE // 2) * l
                pe.wait_ge(n_T_kept, (l + 1) * NT)
                pe.wait_ge(entries_ready, l + 1)
                for q in range(2 * NT):
                    last = mm(PL[:, 0:2 * NBLK], row_hot[:, q, :],
                              blk_val[:, q, :, :].rearrange("p i b -> p (i b)"), start=q == 0, stop=q == 2 * NT - 1)
                last.then_inc(table_summed, 1)
                block_T(n0, 0, c0 + 16)
                def one(e, i=None):
                    n, past = (n0 + e, c0) if i is None else (2 * i + (n0 + e), 16 * i + c0)
                    pe_block(n, e % 2, past + 16 * (e // 2 + 1), past + 16 * ((e + 1) // 2 + 1),
                             first=e == 0, last=e == NE - 1)

                for e in range(HEAD):
                    one(e)
                with pe.Fori(0, PAIRS) as i:
                    for e in PAIR:
                        one(e, i)
                for e in range(NE - TAIL, NE):
                    one(e)
                down_block(n0 + NE - 1, (NE - 1) % 2, down_hi_last)
                m = more[l]
                pe.wait_ge(extra_ready, l + 1)
                count = pe.value_load(extra[l][0:1, XB + 1:XB + 2], min_val=0, max_val=XB)
                with pe.If(count > 0):
                    with pe.Fori(0, XB) as j:
                        with pe.If(j < count):
                            pe.wait_ge(m["xg"], 16 * j + 16)
                            rows_to_columns(PT, xg[1]).then_inc(m["T"], 1)
                            pe.wait_ge(m["xT"], j + 1)
                            pe.wait_ge(m["w"], 48 * j + 48)
                            parts = gate_up(1)
                            next(parts)
                            next(parts).then_inc(m["gu"], 1)
                            pe.wait_ge(m["dve"], 3 * j + 1)
                            act_transpose().then_inc(m["aT_ps"], 1)
                            pe.wait_ge(m["dve"], 3 * j + 3)
                            down(1).then_inc(m["y"], 1)
                            pe.wait_ge(m["y"], j + 1)
                nc.tensor.sem_inc(more_done, 1)

            moe(0)
            pe.wait_ge(bands_ready, 1)
            pe.wait_ge(pool_loaded, 16)
            for k in range(NT + 5):
                if 0 <= k - 1 < NT:
                    t = k - 1
                    pe.wait_ge(h_ready, t + 1)
                    if t:
                        pe.wait_ge(pool_kept, t)
                    for q in range(KD):
                        g = q // 2
                        part = PA[0][:, q * P:(q + 1) * P]
                        last = mm(part, h_r[t % 2][:, q * P:(q + 1) * P], (band if t else band0)[:, g, :],
                                  start=True, stop=t == 0)
                        if t:
                            last = mm(part[:, 0:REACH], h_r[1 - t % 2][:, q * P:(q + 1) * P], band_prev[:, g, :],
                                      start=False, stop=True)
                    last.then_inc(pool_T, 1)
                if 0 <= k - 4 < NT:
                    entry_T(1, k - 4)
                if 0 <= k - 5:
                    entry_logits(1, k - 5)
                if 0 <= k - 1 < NT:
                    pe.wait_ge(pool_kept, t + 1)
                    if t:
                        pe.wait_ge(x_mixed1, t)
                    for g in range(PG):
                        for q in range(2):
                            last = mm(PA[1][:, g * PD:(g + 1) * PD], pooledT[:, 2 * g + q, :], pool_w[:, g, q, :],
                                      start=q == 0, stop=q == 1)
                    last.then_inc(mixed1_done, 1)
            moe(1)


_INS = ["x", "c", "w_ada", "b_ada", "norm_mix_g", "norm_ffn_g", "w_in_even", "sgu_norm_g", "w_spatial",
        "b_spatial", "conv_w", "w_out_even", "w_pool", "pool_scale", "w_group_router", "b_group_router",
        "w_expert_router", "b_expert_router", "moe_w_gate", "moe_w_up", "moe_w_down", "final_norm_g"]


def kernel(**inputs):
    import numpy as _np
    import concourse.bacc as _bacc
    from concourse import mybir as _mybir
    from concourse.bass_utils import run_bass_kernel_spmd as _run

    nc = _bacc.Bacc("TRN2", target_bir_lowering=False, num_devices=1)
    arrays, args = {}, []
    for name in _INS:
        a = _np.ascontiguousarray(inputs[name])
        arrays[f"in_{name}_dram"] = a
        args.append(nc.dram_tensor(f"in_{name}_dram", a.shape, _mybir.dt.from_np(a.dtype), kind="ExternalInput").ap())
    shape = tuple(inputs["x"].shape)
    args.append(nc.dram_tensor("out_0_dram", shape, _mybir.dt.from_np(_np.dtype("float32")), kind="ExternalOutput").ap())
    hybrid_trunk(nc, *args)
    r = _run(nc, [arrays], core_ids=[0])
    return r.results[0]["out_0_dram"]
```
